# Optimizing a Trainium2 kernel written in Bass

```python
import math
import jax, jax.numpy as jnp
from jax import lax
import numpy as np
import jax
import jax.numpy as jnp

D_MODEL = 1024
BATCH = 1
SEQ = 512
DEPTH = 2

GRID_W = 64
CTX_LEN = 256
N_MIXERS = 3
CHUNK = 64
CONV_K = 3
Q_BLOCK = 128
ROPE_BASE = 10000.0
EPS = 1e-6
ADA_CHUNKS = 6

GDN_HEADS = 8
GDN_HEAD_K = 128
GDN_HEAD_V = 128
GDN_KW = GDN_HEADS * GDN_HEAD_K
GDN_VW = GDN_HEADS * GDN_HEAD_V
GDN_IN = 2 * GDN_KW + 2 * GDN_VW + 4 * GDN_HEADS

SSD_INNER = 2 * D_MODEL
SSD_HEAD_DIM = 64
SSD_HEADS = SSD_INNER // SSD_HEAD_DIM
SSD_GROUPS = 8
SSD_STATE = 128
SSD_GN = SSD_GROUPS * SSD_STATE
SSD_CONV_CH = SSD_INNER + 2 * SSD_GN
SSD_IN = SSD_INNER + SSD_CONV_CH + 2 * SSD_HEADS

MLA_HEADS = 16
MLA_NOPE = 64
MLA_ROPE = 32
MLA_V = 64
MLA_Q_RANK = 768
MLA_KV_RANK = 256
MLA_IN = MLA_Q_RANK + MLA_KV_RANK + MLA_ROPE

N_EXPERTS = 16
EXPERT_FF = 1024
EC_CAPACITY = 2


F32 = jnp.float32

def rms_norm(x, g):
    xf = x.astype(F32)
    y = xf * lax.rsqrt(jnp.mean(xf * xf, axis=-1, keepdims=True) + EPS)
    return (y * g.astype(F32)).astype(x.dtype)

def _l2norm(x):
    xf = x.astype(F32)
    return (xf * lax.rsqrt(jnp.sum(xf * xf, axis=-1, keepdims=True) + EPS)).astype(x.dtype)

def _rev(a):
    return jnp.flip(a, axis=1)

def depthwise_conv(x, w):
    k = w.shape[0]
    return lax.conv_general_dilated(
        x, w[:, None, :].astype(x.dtype), window_strides=(1,), padding=[((k - 1) // 2, k // 2)],
        dimension_numbers=('NWC', 'WIO', 'NWC'), feature_group_count=x.shape[-1])

def ada_chunks(cvec, w, b):
    m = jax.nn.silu(cvec) @ w + b
    return jnp.split(m, ADA_CHUNKS, axis=-1)

def modulate(h, shift, scale):
    return h * (1 + scale) + shift

def axial_rope(x, rows, cols):
    def rot(xp, pos):
        d = xp.shape[-1]
        half = d // 2
        inv = ROPE_BASE ** (-jnp.arange(half, dtype=F32) * 2.0 / d)
        ang = pos.astype(F32)[:, None] * inv[None, :]
        cos = jnp.cos(ang)[None, :, None, :]
        sin = jnp.sin(ang)[None, :, None, :]
        x1 = xp[..., :half].astype(F32)
        x2 = xp[..., half:].astype(F32)
        return jnp.concatenate([x1 * cos - x2 * sin, x1 * sin + x2 * cos], -1).astype(xp.dtype)
    r = x.shape[-1] // 2
    return jnp.concatenate([rot(x[..., :r], rows), rot(x[..., r:], cols)], -1)

def gated_delta_scan(q, k, v, g, beta, s0):
    b, t, h, dk = q.shape
    dv = v.shape[-1]
    n = t // CHUNK

    def chunk(a):
        a = a.astype(F32).reshape((b, n, CHUNK) + a.shape[2:])
        return jnp.swapaxes(jnp.swapaxes(a, 0, 1), 2, 3)

    qc = chunk(q) * (dk ** -0.5)
    kc, vc, gc, bc = chunk(k), chunk(v), chunk(g), chunk(beta)
    gcum = jnp.cumsum(gc, axis=-1)
    tril = jnp.tril(jnp.ones((CHUNK, CHUNK), bool))
    strict = jnp.tril(jnp.ones((CHUNK, CHUNK), bool), -1)
    decay = jnp.exp(jnp.where(tril, gcum[..., :, None] - gcum[..., None, :], -jnp.inf))
    kb = kc * bc[..., None]
    lower = jnp.where(strict, jnp.einsum('nbhid,nbhjd->nbhij', kb, kc) * decay, 0.0)
    eye = jnp.broadcast_to(jnp.eye(CHUNK, dtype=F32), lower.shape)
    rhs = jnp.concatenate([vc * bc[..., None], kb * jnp.exp(gcum)[..., None]], axis=-1)
    sol = lax.linalg.triangular_solve(eye + lower, rhs, left_side=True, lower=True, unit_diagonal=True)
    u, w = sol[..., :dv], sol[..., dv:]
    attn = jnp.where(tril, jnp.einsum('nbhid,nbhjd->nbhij', qc, kc) * decay, 0.0)

    def step(S, inp):
        q_i, k_i, u_i, w_i, a_i, g_i = inp
        v_new = u_i - jnp.einsum('bhck,bhkv->bhcv', w_i, S)
        o = (jnp.einsum('bhck,bhkv->bhcv', q_i * jnp.exp(g_i)[..., None], S)
             + jnp.einsum('bhij,bhjv->bhiv', a_i, v_new))
        g_last = g_i[..., -1]
        S = (S * jnp.exp(g_last)[..., None, None]
             + jnp.einsum('bhck,bhcv->bhkv', k_i * jnp.exp(g_last[..., None] - g_i)[..., None], v_new))
        return S, o

    S, o = lax.scan(step, s0, (qc, kc, u, w, attn, gcum))
    o = jnp.swapaxes(jnp.swapaxes(o, 2, 3), 0, 1).reshape(b, t, h, dv)
    return o, S

def gdn_mixer(hx, hc, w_in, conv_w, a_log, dt_bias, norm_g, w_out):
    neg_a = -jnp.exp(a_log.astype(F32))

    def project(h):
        b, t, _ = h.shape
        p = h @ w_in
        qkv = jax.nn.silu(depthwise_conv(p[..., :2 * GDN_KW + GDN_VW], conv_w))
        q = _l2norm(qkv[..., :GDN_KW].reshape(b, t, GDN_HEADS, GDN_HEAD_K))
        k = _l2norm(qkv[..., GDN_KW:2 * GDN_KW].reshape(b, t, GDN_HEADS, GDN_HEAD_K))
        v = qkv[..., 2 * GDN_KW:].reshape(b, t, GDN_HEADS, GDN_HEAD_V)
        off = 2 * GDN_KW + GDN_VW
        z = p[..., off:off + GDN_VW].reshape(b, t, GDN_HEADS, GDN_HEAD_V)
        off += GDN_VW
        beta = jax.nn.sigmoid(p[..., off:off + 2 * GDN_HEADS].astype(F32)).reshape(b, t, 2, GDN_HEADS)
        off += 2 * GDN_HEADS
        g = neg_a * jax.nn.softplus(p[..., off:].astype(F32).reshape(b, t, 2, GDN_HEADS) + dt_bias.astype(F32))
        return q, k, v, z, g, beta

    def mix(h, s0f, s0b):
        b, t, _ = h.shape
        q, k, v, z, g, beta = project(h)
        of, sf = gated_delta_scan(q, k, v, g[:, :, 0], beta[:, :, 0], s0f)
        ob, sb = gated_delta_scan(_rev(q), _rev(k), _rev(v), _rev(g[:, :, 1]), _rev(beta[:, :, 1]), s0b)
        o = (of + _rev(ob)).astype(h.dtype)
        o = rms_norm(o, norm_g) * jax.nn.silu(z)
        return o.reshape(b, t, GDN_VW) @ w_out, sf, sb

    s0 = jnp.zeros((hc.shape[0], GDN_HEADS, GDN_HEAD_K, GDN_HEAD_V), F32)
    oc, sf, sb = mix(hc, s0, s0)
    ox, _, _ = mix(hx, sf, sb)
    return ox, oc

def ssd_scan(xs, dt, A, bm, cm, h0):
    b, t = xs.shape[:2]
    n = t // CHUNK

    def chunk(a):
        return jnp.swapaxes(a.astype(F32).reshape((b, n, CHUNK) + a.shape[2:]), 0, 1)

    tril = jnp.tril(jnp.ones((CHUNK, CHUNK), bool))[None, :, :, None, None]

    def step(h, inp):
        x_i, dt_i, b_i, c_i = inp
        acs = jnp.cumsum(dt_i * A, axis=1)
        seg = jnp.where(tril, acs[:, :, None] - acs[:, None, :], -jnp.inf)
        wts = jnp.einsum('btgn,bsgn->btsg', c_i, b_i)[..., None] * jnp.exp(seg) * dt_i[:, None]
        y = (jnp.einsum('btsgr,bsgrp->btgrp', wts, x_i)
             + jnp.einsum('btgn,bgrpn->btgrp', c_i, h) * jnp.exp(acs)[..., None])
        to_end = jnp.exp(acs[:, -1:] - acs) * dt_i
        h = (h * jnp.exp(acs[:, -1])[..., None, None]
             + jnp.einsum('bsgn,bsgr,bsgrp->bgrpn', b_i, to_end, x_i))
        return h, y

    h, y = lax.scan(step, h0, (chunk(xs), chunk(dt), chunk(bm), chunk(cm)))
    return jnp.swapaxes(y, 0, 1).reshape(xs.shape), h

def ssd_mixer(hx, hc, w_in, conv_w, conv_b, a_log, dt_bias, d_skip, norm_g, w_out):
    r = SSD_HEADS // SSD_GROUPS
    A = -jnp.exp(a_log.astype(F32)).reshape(2, SSD_GROUPS, r)

    def project(h):
        b, t, _ = h.shape
        p = h @ w_in
        z = p[..., :SSD_INNER]
        xbc = jax.nn.silu(depthwise_conv(p[..., SSD_INNER:SSD_INNER + SSD_CONV_CH], conv_w) + conv_b)
        dt = jax.nn.softplus((p[..., SSD_INNER + SSD_CONV_CH:] + dt_bias.reshape(-1)).astype(F32))
        dt = dt.reshape(b, t, 2, SSD_GROUPS, r)
        xs = xbc[..., :SSD_INNER].reshape(b, t, SSD_GROUPS, r, SSD_HEAD_DIM)
        bm = xbc[..., SSD_INNER:SSD_INNER + SSD_GN].reshape(b, t, SSD_GROUPS, SSD_STATE)
        cm = xbc[..., SSD_INNER + SSD_GN:].reshape(b, t, SSD_GROUPS, SSD_STATE)
        return z, xs, bm, cm, dt

    def mix(h, h0f, h0b):
        b, t, _ = h.shape
        z, xs, bm, cm, dt = project(h)
        yf, hf = ssd_scan(xs, dt[:, :, 0], A[0], bm, cm, h0f)
        yb, hb = ssd_scan(_rev(xs), _rev(dt[:, :, 1]), A[1], _rev(bm), _rev(cm), h0b)
        y = yf + _rev(yb) + d_skip.astype(F32).reshape(SSD_GROUPS, r)[..., None] * xs.astype(F32)
        y = y.reshape(b, t, SSD_INNER).astype(h.dtype) * jax.nn.silu(z)
        return rms_norm(y, norm_g) @ w_out, hf, hb

    h0 = jnp.zeros((hc.shape[0], SSD_GROUPS, r, SSD_HEAD_DIM, SSD_STATE), F32)
    oc, hf, hb = mix(hc, h0, h0)
    ox, _, _ = mix(hx, hf, hb)
    return ox, oc

def block_attention(q_nope, q_rope, k_nope, k_rope, v):
    b, t, h, _ = q_nope.shape
    nb = t // Q_BLOCK
    scale = (MLA_NOPE + MLA_ROPE) ** -0.5

    def blocks(a):
        return jnp.swapaxes(a.reshape((b, nb, Q_BLOCK) + a.shape[2:]), 0, 1)

    def one(args):
        qn, qr = args
        s = (jnp.einsum('bqhd,bkhd->bhqk', qn, k_nope).astype(F32)
             + jnp.einsum('bqhr,bkr->bhqk', qr, k_rope).astype(F32)) * scale
        p = jax.nn.softmax(s, axis=-1).astype(v.dtype)
        return jnp.einsum('bhqk,bkhd->bqhd', p, v)

    o = lax.map(one, (blocks(q_nope), blocks(q_rope)))
    return jnp.swapaxes(o, 0, 1).reshape(b, t, h, v.shape[-1])

def mla_mixer(hx, hc, w_in, q_norm_g, w_uq, kv_norm_g, w_ukv, w_out, rows, cols):
    def project(h, positioned):
        b, t, _ = h.shape
        p = h @ w_in
        cq = p[..., :MLA_Q_RANK]
        ckv = p[..., MLA_Q_RANK:MLA_Q_RANK + MLA_KV_RANK]
        kr = p[..., MLA_Q_RANK + MLA_KV_RANK:][:, :, None, :]
        q = (rms_norm(cq, q_norm_g) @ w_uq).reshape(b, t, MLA_HEADS, MLA_NOPE + MLA_ROPE)
        kv = (rms_norm(ckv, kv_norm_g) @ w_ukv).reshape(b, t, MLA_HEADS, MLA_NOPE + MLA_V)
        q_nope, q_rope = q[..., :MLA_NOPE], q[..., MLA_NOPE:]
        k_nope, v = kv[..., :MLA_NOPE], kv[..., MLA_NOPE:]
        if positioned:
            q_rope = axial_rope(q_rope, rows, cols)
            kr = axial_rope(kr, rows, cols)
        return q_nope, q_rope, k_nope, kr[:, :, 0], v

    qn_c, qr_c, kn_c, kr_c, v_c = project(hc, False)
    qn_x, qr_x, kn_x, kr_x, v_x = project(hx, True)
    oc = block_attention(qn_c, qr_c, kn_c, kr_c, v_c)
    ox = block_attention(qn_x, qr_x,
                         jnp.concatenate([kn_c, kn_x], axis=1),
                         jnp.concatenate([kr_c, kr_x], axis=1),
                         jnp.concatenate([v_c, v_x], axis=1))
    bx, tx = hx.shape[:2]
    bc, tc = hc.shape[:2]
    return (ox.reshape(bx, tx, MLA_HEADS * MLA_V) @ w_out,
            oc.reshape(bc, tc, MLA_HEADS * MLA_V) @ w_out)

def ec_moe(h, w_router, w_gate, w_up, w_down):
    b, n, _ = h.shape
    cap = EC_CAPACITY * n // N_EXPERTS
    aff = jax.nn.softmax((h @ w_router).astype(F32), axis=-1)
    gate, idx = lax.top_k(jnp.swapaxes(aff, 1, 2), cap)
    bidx = jnp.arange(b)[:, None, None]
    xs = h[bidx, idx]
    hid = jax.nn.silu(jnp.einsum('becd,edf->becf', xs, w_gate)) * jnp.einsum('becd,edf->becf', xs, w_up)
    y = jnp.einsum('becf,efd->becd', hid, w_down) * gate.astype(h.dtype)[..., None]
    return jnp.zeros_like(h).at[bidx, idx].add(y)

def first_inputs(seed: int = 0) -> dict:
    key = jax.random.key(seed)
    ks = iter(jax.random.split(key, 40))
    n_a = len(range(0, DEPTH, N_MIXERS))
    n_b = len(range(1, DEPTH, N_MIXERS))
    n_c = len(range(2, DEPTH, N_MIXERS))

    def nrm(shape, scale):
        return jax.random.normal(next(ks), shape, F32) * scale

    def gain(shape):
        return 1.0 + nrm(shape, 0.05)

    def a_log(shape):
        return jnp.log(jax.random.uniform(next(ks), shape, F32, 1.0, 16.0))

    def dt_bias(shape):
        dt = jnp.exp(jax.random.uniform(next(ks), shape, F32, math.log(1e-3), math.log(1e-1)))
        return dt + jnp.log(-jnp.expm1(-dt))

    d = D_MODEL
    return {
        "x": nrm((BATCH, SEQ, d), 1.0),
        "c": nrm((BATCH, d), 1.0),
        "ctx": nrm((BATCH, CTX_LEN, d), 1.0),
        "c_ctx": nrm((d,), 1.0),
        "ada_w": nrm((DEPTH, d, ADA_CHUNKS * d), 0.5 * d ** -0.5),
        "ada_b": nrm((DEPTH, ADA_CHUNKS * d), 0.02),
        "norm1_g": gain((DEPTH, d)),
        "norm2_g": gain((DEPTH, d)),
        "router_w": nrm((DEPTH, d, N_EXPERTS), d ** -0.5),
        "moe_w_gate": nrm((DEPTH, N_EXPERTS, d, EXPERT_FF), d ** -0.5),
        "moe_w_up": nrm((DEPTH, N_EXPERTS, d, EXPERT_FF), d ** -0.5),
        "moe_w_down": nrm((DEPTH, N_EXPERTS, EXPERT_FF, d), EXPERT_FF ** -0.5),
        "gdn_w_in": nrm((n_a, d, GDN_IN), d ** -0.5),
        "gdn_conv_w": nrm((n_a, CONV_K, 2 * GDN_KW + GDN_VW), CONV_K ** -0.5),
        "gdn_a_log": a_log((n_a, 2, GDN_HEADS)),
        "gdn_dt_bias": dt_bias((n_a, 2, GDN_HEADS)),
        "gdn_norm_g": gain((n_a, GDN_HEAD_V)),
        "gdn_w_out": nrm((n_a, GDN_VW, d), GDN_VW ** -0.5),
        "ssd_w_in": nrm((n_b, d, SSD_IN), d ** -0.5),
        "ssd_conv_w": nrm((n_b, CONV_K, SSD_CONV_CH), CONV_K ** -0.5),
        "ssd_conv_b": nrm((n_b, SSD_CONV_CH), 0.02),
        "ssd_a_log": a_log((n_b, 2, SSD_HEADS)),
        "ssd_dt_bias": dt_bias((n_b, 2, SSD_HEADS)),
        "ssd_d": 1.0 + nrm((n_b, SSD_HEADS), 0.1),
        "ssd_norm_g": gain((n_b, SSD_INNER)),
        "ssd_w_out": nrm((n_b, SSD_INNER, d), SSD_INNER ** -0.5),
        "mla_w_in": nrm((n_c, d, MLA_IN), d ** -0.5),
        "mla_q_norm_g": gain((n_c, MLA_Q_RANK)),
        "mla_w_uq": nrm((n_c, MLA_Q_RANK, MLA_HEADS * (MLA_NOPE + MLA_ROPE)), MLA_Q_RANK ** -0.5),
        "mla_kv_norm_g": gain((n_c, MLA_KV_RANK)),
        "mla_w_ukv": nrm((n_c, MLA_KV_RANK, MLA_HEADS * (MLA_NOPE + MLA_V)), MLA_KV_RANK ** -0.5),
        "mla_w_out": nrm((n_c, MLA_HEADS * MLA_V, d), (MLA_HEADS * MLA_V) ** -0.5),
        "final_norm_g": gain((d,)),
    }

def first_block(x, c, ctx, c_ctx, ada_w, ada_b, norm1_g, norm2_g, router_w, moe_w_gate, moe_w_up, moe_w_down,
              gdn_w_in, gdn_conv_w, gdn_a_log, gdn_dt_bias, gdn_norm_g, gdn_w_out,
              ssd_w_in, ssd_conv_w, ssd_conv_b, ssd_a_log, ssd_dt_bias, ssd_d, ssd_norm_g, ssd_w_out,
              mla_w_in, mla_q_norm_g, mla_w_uq, mla_kv_norm_g, mla_w_ukv, mla_w_out, final_norm_g):
    t = x.shape[1]
    ROWS = t // GRID_W
    rows = jnp.repeat(jnp.arange(ROWS, dtype=jnp.int32), GRID_W)
    cols = jnp.tile(jnp.arange(GRID_W, dtype=jnp.int32), ROWS)

    for i in range(DEPTH):
        last = i == DEPTH - 1
        mx = [m[:, None, :] for m in ada_chunks(c, ada_w[i], ada_b[i])]
        mc = ada_chunks(c_ctx, ada_w[i], ada_b[i])
        hx = modulate(rms_norm(x, norm1_g[i]), mx[0], mx[1])
        hc = modulate(rms_norm(ctx, norm1_g[i]), mc[0], mc[1])
        kind = i % N_MIXERS
        j = i // N_MIXERS
        if kind == 0:
            ox, oc = gdn_mixer(hx, hc, gdn_w_in[j], gdn_conv_w[j], gdn_a_log[j], gdn_dt_bias[j],
                               gdn_norm_g[j], gdn_w_out[j])
        elif kind == 1:
            ox, oc = ssd_mixer(hx, hc, ssd_w_in[j], ssd_conv_w[j], ssd_conv_b[j], ssd_a_log[j],
                               ssd_dt_bias[j], ssd_d[j], ssd_norm_g[j], ssd_w_out[j])
        else:
            ox, oc = mla_mixer(hx, hc, mla_w_in[j], mla_q_norm_g[j], mla_w_uq[j], mla_kv_norm_g[j],
                               mla_w_ukv[j], mla_w_out[j], rows, cols)
        x = x + mx[2] * ox
        hx = modulate(rms_norm(x, norm2_g[i]), mx[3], mx[4])
        x = x + mx[5] * ec_moe(hx, router_w[i], moe_w_gate[i], moe_w_up[i], moe_w_down[i])
        if not last:
            ctx = ctx + mc[2] * oc
            hc = modulate(rms_norm(ctx, norm2_g[i]), mc[3], mc[4])
            ctx = ctx + mc[5] * ec_moe(hc, router_w[i], moe_w_gate[i], moe_w_up[i], moe_w_down[i])

    return rms_norm(x, final_norm_g)


DEPTH_2 = 1

SSM_WIDTH = D_MODEL // 2
SSM_GROUP = 16
SSM_GROUPS = SSM_WIDTH // SSM_GROUP
SSM_STATE = 64
DT_MIN = 1e-3
DT_MAX = 1e-1
CONV_CH = D_MODEL // 2
HEAD_DIM = 64
N_HEADS = (D_MODEL // 2) // HEAD_DIM
N_KV_HEADS = 2
GQA = N_HEADS // N_KV_HEADS
ATTN_WIDTH = N_HEADS * HEAD_DIM
KV_WIDTH = N_KV_HEADS * HEAD_DIM
CMP_BLOCK = 32
SEL_BLOCK = 64
N_SELECT = 16
WINDOW = 512
CMP_HIDDEN = 256
Q_CHUNK = 64
FORCE_SCORE = 1e4
NSA_BRANCHES = 3
MIX_BRANCHES = 3
D_FF = -(-8 * D_MODEL // (3 * 256)) * 256
RMS_EPS = 1e-6
IN_WIDTH = SSM_WIDTH + 3 * CONV_CH + ATTN_WIDTH + 6 * KV_WIDTH + N_HEADS * NSA_BRANCHES + MIX_BRANCHES * D_MODEL


def rms_norm_2(x, g):
    xf = x.astype(jnp.float32)
    y = xf * lax.rsqrt(jnp.mean(xf * xf, axis=-1, keepdims=True) + RMS_EPS)
    return (y * g.astype(jnp.float32)).astype(x.dtype)

def masked_softmax(s, mask):
    s = jnp.where(mask, s, -jnp.inf)
    m = jnp.max(s, axis=-1, keepdims=True)
    m = jnp.where(jnp.isfinite(m), m, 0.0)
    e = jnp.exp(s - m)
    return e / jnp.maximum(jnp.sum(e, axis=-1, keepdims=True), 1e-30)

def split_projection(z):
    sizes = ([SSM_WIDTH, CONV_CH, CONV_CH, CONV_CH, ATTN_WIDTH] + [KV_WIDTH] * 6
             + [N_HEADS * NSA_BRANCHES, MIX_BRANCHES * D_MODEL])
    return jnp.split(z, np.cumsum(sizes)[:-1].tolist(), axis=-1)

def s5_mixer(u, lam_re, lam_im, b_re, b_im, c_re, c_im, d_skip, log_dt, w_glu):
    bsz, seq, _ = u.shape
    f32 = jnp.float32
    uf = u.astype(f32).reshape(bsz, seq, SSM_GROUPS, SSM_GROUP)
    lam = lax.complex(lam_re.astype(f32), lam_im.astype(f32))
    dt = jnp.exp(log_dt.astype(f32))[:, None]
    lam_bar = jnp.exp(lam * dt)
    b = lax.complex(b_re.astype(f32), b_im.astype(f32))
    b_bar = ((lam_bar - 1.0) / lam)[..., None] * b
    c = lax.complex(c_re.astype(f32), c_im.astype(f32))
    bu = jnp.einsum('bsgh,gph->bsgp', uf.astype(jnp.complex64), b_bar)
    a = jnp.broadcast_to(lam_bar, bu.shape)

    def combine(left, right):
        a_l, b_l = left
        a_r, b_r = right
        return a_r * a_l, a_r * b_l + b_r

    _, states = lax.associative_scan(combine, (a, bu), axis=1)
    y = jnp.einsum('bsgp,ghp->bsgh', states, c).real + d_skip.astype(f32).reshape(SSM_GROUPS, SSM_GROUP) * uf
    y = jax.nn.gelu(y.reshape(bsz, seq, SSM_WIDTH)).astype(u.dtype)
    y_lin, y_gate = jnp.split(y @ w_glu, 2, axis=-1)
    return y_lin * jax.nn.sigmoid(y_gate)

def short_conv_mixer(xin, gate_b, gate_c, conv_w, w_out):
    z = gate_c * xin
    z = lax.conv_general_dilated(z, conv_w[:, None, :], window_strides=(1,), padding=[(CONV_K - 1, 0)],
                                 dimension_numbers=('NWC', 'WIO', 'NWC'), feature_group_count=CONV_CH)
    return (gate_b * z) @ w_out

def nsa_mixer(q, k_cmp, v_cmp, k_sel, v_sel, k_win, v_win, gate_logits,
              q_norm_g, k_norm_g, cmp_pe, cmp_w1, cmp_w2, w_o):
    bsz, seq, _ = q.shape
    f32 = jnp.float32
    scale = HEAD_DIM ** -0.5
    pos = jnp.arange(seq)

    def heads(t, n):
        return t.reshape(bsz, seq, n, HEAD_DIM)

    q = rms_norm_2(heads(q, N_HEADS), q_norm_g).reshape(bsz, seq, N_KV_HEADS, GQA, HEAD_DIM)

    n_cmp = seq // CMP_BLOCK

    def compress(t, which):
        blocks = heads(t, N_KV_HEADS).reshape(bsz, n_cmp, CMP_BLOCK, N_KV_HEADS, HEAD_DIM) + cmp_pe[which][:, None, :]
        blocks = blocks.transpose(0, 1, 3, 2, 4).reshape(bsz, n_cmp, N_KV_HEADS, CMP_BLOCK * HEAD_DIM)
        return jax.nn.gelu(blocks @ cmp_w1[which]) @ cmp_w2[which]

    kc = rms_norm_2(compress(k_cmp, 0), k_norm_g[0])
    vc = compress(v_cmp, 1)
    s = jnp.einsum('bqhgd,bchd->bhgqc', q, kc).astype(f32) * scale
    cmp_end = (jnp.arange(n_cmp) + 1) * CMP_BLOCK - 1
    p_cmp = masked_softmax(s, cmp_end[None, :] <= pos[:, None])
    o_cmp = jnp.einsum('bhgqc,bchd->bqhgd', p_cmp.astype(vc.dtype), vc)

    n_blocks = seq // SEL_BLOCK
    n_top = min(N_SELECT, n_blocks)
    imp = jnp.sum(p_cmp, axis=2).reshape(bsz, N_KV_HEADS, seq, n_blocks, SEL_BLOCK // CMP_BLOCK).sum(-1)
    blk = jnp.arange(n_blocks)[None, :]
    cur = (pos // SEL_BLOCK)[:, None]
    forced = (blk == 0) | (blk == cur) | (blk == cur - 1)
    visible = blk * SEL_BLOCK <= pos[:, None]
    imp = jnp.where(forced, FORCE_SCORE, jnp.where(visible, imp, -jnp.inf))
    _, sel_idx = lax.top_k(imp, n_top)

    ks_blocks = rms_norm_2(heads(k_sel, N_KV_HEADS), k_norm_g[1]).reshape(
        bsz, n_blocks, SEL_BLOCK, N_KV_HEADS, HEAD_DIM).transpose(0, 3, 1, 2, 4)
    vs_blocks = heads(v_sel, N_KV_HEADS).reshape(
        bsz, n_blocks, SEL_BLOCK, N_KV_HEADS, HEAD_DIM).transpose(0, 3, 1, 2, 4)
    pad = ((0, 0), (WINDOW, 0), (0, 0), (0, 0))
    kw_pad = jnp.pad(rms_norm_2(heads(k_win, N_KV_HEADS), k_norm_g[2]), pad)
    vw_pad = jnp.pad(heads(v_win, N_KV_HEADS), pad)
    b_ix = jnp.arange(bsz)[:, None, None, None]
    h_ix = jnp.arange(N_KV_HEADS)[None, :, None, None]
    n_sel_keys = n_top * SEL_BLOCK

    def query_chunk(c):
        start = c * Q_CHUNK
        t = start + jnp.arange(Q_CHUNK)
        qc = lax.dynamic_slice_in_dim(q, start, Q_CHUNK, axis=1)
        idx = lax.dynamic_slice_in_dim(sel_idx, start, Q_CHUNK, axis=2)
        kg = ks_blocks[b_ix, h_ix, idx].reshape(bsz, N_KV_HEADS, Q_CHUNK, n_sel_keys, HEAD_DIM)
        vg = vs_blocks[b_ix, h_ix, idx].reshape(bsz, N_KV_HEADS, Q_CHUNK, n_sel_keys, HEAD_DIM)
        key_pos = (idx[..., None] * SEL_BLOCK + jnp.arange(SEL_BLOCK)).reshape(bsz, N_KV_HEADS, Q_CHUNK, n_sel_keys)
        s_sel = jnp.einsum('bqhgd,bhqkd->bhgqk', qc, kg).astype(f32) * scale
        p_sel = masked_softmax(s_sel, (key_pos <= t[:, None])[:, :, None])
        o_sel = jnp.einsum('bhgqk,bhqkd->bqhgd', p_sel.astype(vg.dtype), vg)
        kwc = lax.dynamic_slice_in_dim(kw_pad, start, Q_CHUNK + WINDOW, axis=1)
        vwc = lax.dynamic_slice_in_dim(vw_pad, start, Q_CHUNK + WINDOW, axis=1)
        wpos = (start - WINDOW + jnp.arange(Q_CHUNK + WINDOW))[None, :]
        wmask = (wpos <= t[:, None]) & (wpos > t[:, None] - WINDOW) & (wpos >= 0)
        s_win = jnp.einsum('bqhgd,bkhd->bhgqk', qc, kwc).astype(f32) * scale
        p_win = masked_softmax(s_win, wmask)
        o_win = jnp.einsum('bhgqk,bkhd->bqhgd', p_win.astype(vwc.dtype), vwc)
        return o_sel, o_win

    o_sel, o_win = lax.map(query_chunk, jnp.arange(seq // Q_CHUNK))

    def unchunk(o):
        return jnp.moveaxis(o, 0, 1).reshape(bsz, seq, N_KV_HEADS, GQA, HEAD_DIM)

    g = jax.nn.sigmoid(gate_logits.astype(f32)).reshape(bsz, seq, N_KV_HEADS, GQA, NSA_BRANCHES).astype(q.dtype)
    o = g[..., 0:1] * o_cmp + g[..., 1:2] * unchunk(o_sel) + g[..., 2:3] * unchunk(o_win)
    return o.reshape(bsz, seq, ATTN_WIDTH) @ w_o

def second_inputs(seed: int = 0) -> dict:
    key = jax.random.key(seed)
    ks = jax.random.split(key, 24)
    f32 = jnp.float32
    nl, G, P, H = DEPTH_2, SSM_GROUPS, SSM_STATE, SSM_GROUP

    def nrm(k, shape, scale):
        return scale * jax.random.normal(k, shape, f32)

    return {
        'x': nrm(ks[0], (BATCH, SEQ, D_MODEL), 1.0),
        'mix_norm_g': 1.0 + nrm(ks[1], (nl, D_MODEL), 0.02),
        'w_in': nrm(ks[2], (nl, D_MODEL, IN_WIDTH), D_MODEL ** -0.5),
        'ssm_lam_re': -0.5 + nrm(ks[3], (nl, G, P), 0.01),
        'ssm_lam_im': jnp.pi * jnp.arange(P, dtype=f32) + nrm(ks[4], (nl, G, P), 0.01),
        'ssm_b_re': nrm(ks[5], (nl, G, P, H), (2 * H) ** -0.5),
        'ssm_b_im': nrm(ks[6], (nl, G, P, H), (2 * H) ** -0.5),
        'ssm_c_re': nrm(ks[7], (nl, G, H, P), 0.5 ** 0.5),
        'ssm_c_im': nrm(ks[8], (nl, G, H, P), 0.5 ** 0.5),
        'ssm_d': nrm(ks[9], (nl, SSM_WIDTH), 1.0),
        'ssm_log_dt': jax.random.uniform(ks[10], (nl, G), f32, float(np.log(DT_MIN)), float(np.log(DT_MAX))),
        'ssm_w_glu': nrm(ks[11], (nl, SSM_WIDTH, 2 * D_MODEL), SSM_WIDTH ** -0.5),
        'conv_w': nrm(ks[12], (nl, CONV_K, CONV_CH), CONV_K ** -0.5),
        'conv_w_out': nrm(ks[13], (nl, CONV_CH, D_MODEL), CONV_CH ** -0.5),
        'q_norm_g': 1.0 + nrm(ks[14], (nl, HEAD_DIM), 0.02),
        'k_norm_g': 1.0 + nrm(ks[15], (nl, NSA_BRANCHES, HEAD_DIM), 0.02),
        'cmp_pe': nrm(ks[16], (nl, 2, CMP_BLOCK, HEAD_DIM), 0.1),
        'cmp_w1': nrm(ks[17], (nl, 2, CMP_BLOCK * HEAD_DIM, CMP_HIDDEN), (CMP_BLOCK * HEAD_DIM) ** -0.5),
        'cmp_w2': nrm(ks[18], (nl, 2, CMP_HIDDEN, HEAD_DIM), CMP_HIDDEN ** -0.5),
        'nsa_w_o': nrm(ks[19], (nl, ATTN_WIDTH, D_MODEL), ATTN_WIDTH ** -0.5),
        'w_out': nrm(ks[20], (nl, D_MODEL, D_MODEL), D_MODEL ** -0.5),
        'ffn_norm_g': 1.0 + nrm(ks[21], (nl, D_MODEL), 0.02),
        'ffn_w_gate_up': nrm(ks[22], (nl, D_MODEL, 2 * D_FF), D_MODEL ** -0.5),
        'ffn_w_down': nrm(ks[23], (nl, D_FF, D_MODEL), D_FF ** -0.5),
    }

def second_block(x, mix_norm_g, w_in, ssm_lam_re, ssm_lam_im, ssm_b_re, ssm_b_im, ssm_c_re, ssm_c_im,
              ssm_d, ssm_log_dt, ssm_w_glu, conv_w, conv_w_out, q_norm_g, k_norm_g, cmp_pe, cmp_w1,
              cmp_w2, nsa_w_o, w_out, ffn_norm_g, ffn_w_gate_up, ffn_w_down):
    bsz, seq, _ = x.shape
    for i in range(DEPTH_2):
        h = rms_norm_2(x, mix_norm_g[i])
        (u, c_b, c_c, c_x, q, k_c, v_c, k_s, v_s, k_w, v_w, nsa_gates, mix_gates) = split_projection(h @ w_in[i])
        y_ssm = s5_mixer(u, ssm_lam_re[i], ssm_lam_im[i], ssm_b_re[i], ssm_b_im[i], ssm_c_re[i], ssm_c_im[i],
                         ssm_d[i], ssm_log_dt[i], ssm_w_glu[i])
        y_conv = short_conv_mixer(c_x, c_b, c_c, conv_w[i], conv_w_out[i])
        y_attn = nsa_mixer(q, k_c, v_c, k_s, v_s, k_w, v_w, nsa_gates, q_norm_g[i], k_norm_g[i],
                           cmp_pe[i], cmp_w1[i], cmp_w2[i], nsa_w_o[i])
        gates = jax.nn.sigmoid(mix_gates.astype(jnp.float32)).astype(x.dtype).reshape(bsz, seq, MIX_BRANCHES, D_MODEL)
        mixed = gates[:, :, 0] * y_ssm + gates[:, :, 1] * y_conv + gates[:, :, 2] * y_attn
        x = x + mixed @ w_out[i]
        h = rms_norm_2(x, ffn_norm_g[i])
        f_gate, f_up = jnp.split(h @ ffn_w_gate_up[i], 2, axis=-1)
        x = x + (jax.nn.silu(f_gate) * f_up) @ ffn_w_down[i]
    return x


def setup_inputs(seed=0):
    out = dict(first_inputs(seed))
    for name, value in second_inputs(seed + 1).items():
        if name != "x":
            out[name + "_2"] = value
    return out


def reference(
    x, c, ctx, c_ctx, ada_w, ada_b, norm1_g, norm2_g, router_w, moe_w_gate, moe_w_up,
    moe_w_down, gdn_w_in, gdn_conv_w, gdn_a_log, gdn_dt_bias, gdn_norm_g, gdn_w_out, ssd_w_in,
    ssd_conv_w, ssd_conv_b, ssd_a_log, ssd_dt_bias, ssd_d, ssd_norm_g, ssd_w_out, mla_w_in,
    mla_q_norm_g, mla_w_uq, mla_kv_norm_g, mla_w_ukv, mla_w_out, final_norm_g, mix_norm_g_2,
    w_in_2, ssm_lam_re_2, ssm_lam_im_2, ssm_b_re_2, ssm_b_im_2, ssm_c_re_2, ssm_c_im_2, ssm_d_2,
    ssm_log_dt_2, ssm_w_glu_2, conv_w_2, conv_w_out_2, q_norm_g_2, k_norm_g_2, cmp_pe_2,
    cmp_w1_2, cmp_w2_2, nsa_w_o_2, w_out_2, ffn_norm_g_2, ffn_w_gate_up_2, ffn_w_down_2,
):
    x = first_block(
        x, c, ctx, c_ctx, ada_w, ada_b, norm1_g, norm2_g, router_w, moe_w_gate, moe_w_up,
        moe_w_down, gdn_w_in, gdn_conv_w, gdn_a_log, gdn_dt_bias, gdn_norm_g, gdn_w_out,
        ssd_w_in, ssd_conv_w, ssd_conv_b, ssd_a_log, ssd_dt_bias, ssd_d, ssd_norm_g, ssd_w_out,
        mla_w_in, mla_q_norm_g, mla_w_uq, mla_kv_norm_g, mla_w_ukv, mla_w_out, final_norm_g,
    )
    return second_block(
        x, mix_norm_g_2, w_in_2, ssm_lam_re_2, ssm_lam_im_2, ssm_b_re_2, ssm_b_im_2, ssm_c_re_2,
        ssm_c_im_2, ssm_d_2, ssm_log_dt_2, ssm_w_glu_2, conv_w_2, conv_w_out_2, q_norm_g_2,
        k_norm_g_2, cmp_pe_2, cmp_w1_2, cmp_w2_2, nsa_w_o_2, w_out_2, ffn_norm_g_2,
        ffn_w_gate_up_2, ffn_w_down_2,
    )


_drawn_inputs = setup_inputs


def setup_inputs(seed=0):
    import zlib

    import numpy as np

    out = dict(_drawn_inputs(seed))
    spreads = {}
    factors = {'norm2_g': 2.678,
     'gdn_norm_g': 3.623,
     'ssd_conv_b': 4.507,
     'ssd_d': 3.591,
     'ssd_norm_g': 2.787,
     'mix_norm_g_2': 2.871,
     'ssm_lam_re_2': 200.0,
     'q_norm_g_2': 25.196,
     'k_norm_g_2': 29.177,
     'cmp_pe_2': 12.184,
     'ffn_norm_g_2': 12.97,
     'ssm_lam_im_2': 38.728,
     'ssm_b_re_2': 52.136,
     'ssm_b_im_2': 51.456,
     'ssm_c_re_2': 52.352,
     'ssm_c_im_2': 51.784,
     'ssm_log_dt_2': 41.296}
    for name, (base, spread) in spreads.items():
        noise = np.random.default_rng([zlib.crc32(name.encode()), seed]).standard_normal(out[name].shape)
        drawn = base * np.exp(spread * noise) if base else spread * noise
        out[name] = jnp.asarray(drawn.astype(out[name].dtype))
    for name, factor in factors.items():
        out[name] = (out[name] * factor).astype(out[name].dtype)
    return out
```

```python
from contextlib import ExitStack

import numpy as np

import concourse.bass as bass
from concourse import mybir

F32 = mybir.dt.float32
ALU = mybir.AluOpType
ACT = mybir.ActivationFunctionType
AX = mybir.AxisListType

P = 128
D = 1024
KD = D // P
CTX, SEQ = 256, 512
N = CTX + SEQ
NT = N // P
XT0 = CTX // P
XSET, CSET = (CTX, SEQ, 0), (0, CTX, 1)
EPS = 1e-6

GH = 8
HG = 4
LEVELS = 7
CHUNK_OF = ([0, 1, 2, 3, 4, 5], [1, 0, 5, 4, 3, 2])

SG, SR, SP_ = 8, 4, 64
SH = SG * SR
SI = SH * SP_

NE = 16
CAPX, CAPC = 2 * SEQ // NE, 2 * CTX // NE
SLOTS = CAPX + CAPC
FF = 1024
EB = 4

FF2 = 2816
NH, HD = 8, 64
NCMP, CMPB = SEQ // 32, 32
WU, WCB, WCC, WCX, WQ = 0, 512, 1024, 1536, 2048
WKC, WVC, WKS, WVS, WKW, WVW, WNG, WMG = 2560, 2688, 2816, 2944, 3072, 3200, 3328, 3352
NST = 16
TURN = 6.2831850
ROUND = 12582912.0

CW = 256
CHUNK = KD * CW
RING = 6
NEG = -1e30

COLS = dict(
    cvec=16, ada_b=96, norm1=16, norm2=16, final=8, mixn=8, ffnn=8,
    gconv=72, galog=16, gdtb=16, gnorm=1,
    sconv=96, sconvb=32, salog=64, sdtb=64, sd=16, snorm=16,
    lamre=16, lamim=16, logdt=16, ssmd=4, conv2=12, qn=1, kn=3, pe=64,
)
AT, NCOLS = {}, 0
for _k, _w in COLS.items():
    AT[_k] = (NCOLS, _w)
    NCOLS += _w


def weight_plan():
    plan = [("ada", 0, n) for n in range(24)] + [("gtail",)]
    for hg in range(GH // HG):
        plan += [("gin", part, hg, n) for part in range(3) for n in range(2)]
        plan += [("ada", 1, hg * 12 + n) for n in range(12)]
        plan += [("gz", hg, n) for n in range(2)] + [("gout", hg, n) for n in range(2)]
    plan += [("moe", 0)]
    plan += [("stail", n) for n in range(2)]
    for g in range(SG):
        plan += [("sx", g), ("sb", g), ("sc", g)]
    plan += [("sz", n) for n in range(SI // CW)] + [("sout", m) for m in range(KD)]
    plan += [("moe", 1)]
    plan += [("bv", n) for n in range(3)]
    plan += [("bq", n) for n in range(2)] + [("bk", n) for n in range(4)]
    plan += [("c1", which, n) for which in range(2) for n in range(4)] + [("c2",)]
    plan += [("bu", n) for n in range(2)]
    for n in range(2):
        plan += [("cc", n), ("cx", n), ("cb", n)]
    for m in range(KD):
        plan += [("mg", i, m) for i in range(3)] + [("glu", m), ("cvo", m), ("nso", m)]
    plan += [("wo", n) for n in range(4)]
    for n in range(FF2 // CW):
        plan += [("fg", n), ("fu", n)]
    plan += [("fd", m, half) for m in range(KD) for half in range(2)]
    return plan


def chunks_of(item):
    return NE * 12 if item[0] == "moe" else 1


PLAN = weight_plan()
USED, CHUNKS = {}, 0
for _item in PLAN:
    CHUNKS += chunks_of(_item)
    USED[_item] = CHUNKS
RING0 = -(USED[("moe", 0)] - NE * 12) % RING


class Lane:

    def __init__(self, eng, steps):
        self.eng, self.steps, self.count, self.last = eng, steps, {}, None

    def do(self, ins, sem=None):
        sem = sem or self.steps
        self.count[sem.name] = self.count.get(sem.name, 0) + 1
        self.last = (sem, self.count[sem.name])
        ins.then_inc(sem, 1)

    def settle(self):
        self.eng.wait_ge(*self.last)


class Signals:

    def __init__(self, new):
        self.iota_done = new("iota_done")
        self.const_in = new("const_in")
        self.mask_done = new("mask_done")
        self.level_masks = new("level_masks")
        self.vec_steps = new("vec_steps")
        self.act_steps = new("act_steps")
        self.pool_steps = new("pool_steps")
        self.w_used = new("w_used")
        self.router_in = new("router_in")
        self.cv_done = new("cv_done")
        self.ada_copied = new("ada_copied")
        self.nsq = new("nsq")
        self.nsq_sum = new("nsq_sum")
        self.nrt = new("nrt")
        self.nstt = new("nstt")
        self.h_ready = new("h_ready")
        self.gp_mm = new("gp_mm")
        self.gp_pre = new("gp_pre")
        self.gp_conv = new("gp_conv")
        self.gp_act = new("gp_act")
        self.gp_sq = new("gp_sq")
        self.gp_sum = new("gp_sum")
        self.gp_rt = new("gp_rt")
        self.gp_norm = new("gp_norm")
        self.gt_bias = new("gt_bias")
        self.gt_e = new("gt_e")
        self.gt_sp = new("gt_sp")
        self.gt_g = new("gt_g")
        self.gc_mm = new("gc_mm")
        self.gc_cols = new("gc_cols")
        self.gr_mm = new("gr_mm")
        self.gr_rows = new("gr_rows")
        self.r_in = new("r_in")
        self.r_dm = new("r_dm")
        self.r_d = new("r_d")
        self.r_xt = new("r_xt")
        self.r_y = new("r_y")
        self.r_ym = new("r_ym")
        self.r_tu = new("r_tu")
        self.r_l = new("r_l")
        self.r_kv = new("r_kv")
        self.r_kvs = new("r_kvs")
        self.r_w = new("r_w")
        self.r_nw = new("r_nw")
        self.r_vn = new("r_vn")
        self.r_vnc = new("r_vnc")
        self.r_o = new("r_o")
        self.r_state = new("r_state")
        self.go_sq = new("go_sq")
        self.go_sum = new("go_sum")
        self.go_rt = new("go_rt")
        self.go_n = new("go_n")
        self.go_z = new("go_z")
        self.go_sz = new("go_sz")
        self.go_o = new("go_o")
        self.go_mm = new("go_mm")
        self.resid = new("resid")
        self.lg_mm = new("lg_mm")
        self.sm_sub = new("sm_sub")
        self.sm_exp = new("sm_exp")
        self.aff_ready = new("aff_ready")
        self.afft_mm = new("afft_mm")
        self.posm_ready = new("posm_ready")
        self.post_mm = new("post_mm")
        self.sel_ready = new("sel_ready")
        self.ht_mm = new("ht_mm")
        self.ht_copied = new("ht_copied")
        self.ga_mm = new("ga_mm")
        self.ga_copied = new("ga_copied")
        self.selg_ready = new("selg_ready")
        self.st_mm = new("st_mm")
        self.st_copied = new("st_copied")
        self.x_cur = new("x_cur")
        self.sg_ready = new("sg_ready")
        self.gu_free = new("gu_free")
        self.y_free = new("y_free")
        self.sc_mm = new("sc_mm")
        self.sc_free = new("sc_free")
        self.st_bias = new("st_bias")
        self.st_sp = new("st_sp")
        self.st_a = new("st_a")
        self.sa_mm = new("sa_mm")
        self.sa_cols = new("sa_cols")
        self.sa_e = new("sa_e")
        self.sr_mm = new("sr_mm")
        self.sr_rows = new("sr_rows")
        self.sp_mm = new("sp_mm")
        self.sp_pre = new("sp_pre")
        self.sp_conv = new("sp_conv")
        self.sp_act = new("sp_act")
        self.str_mm = new("str_mm")
        self.str_out = new("str_out")
        self.s_sel = new("s_sel")
        self.s_xend = new("s_xend")
        self.s_in = new("s_in")
        self.s_dm = new("s_dm")
        self.s_d = new("s_d")
        self.s_w = new("s_w")
        self.s_y = new("s_y")
        self.s_yacc = new("s_yacc")
        self.s_st = new("s_st")
        self.s_state = new("s_state")
        self.sy_mm = new("sy_mm")
        self.sy_out = new("sy_out")
        self.sz_mm = new("sz_mm")
        self.sz_act = new("sz_act")
        self.sz_u = new("sz_u")
        self.sz_sq = new("sz_sq")
        self.sz_n = new("sz_n")
        self.sz_sum = new("sz_sum")
        self.sz_rt = new("sz_rt")
        self.bv_out = new("bv_out")
        self.bq_copy = new("bq_copy")
        self.bq_sq = new("bq_sq")
        self.bq_sum = new("bq_sum")
        self.bq_rt = new("bq_rt")
        self.bq_n = new("bq_n")
        self.bc_vec = new("bc_vec")
        self.bc_act = new("bc_act")
        self.bc_sum = new("bc_sum")
        self.at_s = new("at_s")
        self.at_m = new("at_m")
        self.at_e = new("at_e")
        self.at_t = new("at_t")
        self.at_c = new("at_c")
        self.at_v = new("at_v")
        self.at_o = new("at_o")
        self.ao_mm = new("ao_mm")
        self.ao_copy = new("ao_copy")
        self.s5_ang = new("s5_ang")
        self.s5_act = new("s5_act")
        self.s5_tab = new("s5_tab")
        self.s5_b = new("s5_b")
        self.s5_w = new("s5_w")
        self.s5_x = new("s5_x")
        self.s5_y = new("s5_y")
        self.s5_yd = new("s5_yd")
        self.s5_gelu = new("s5_gelu")
        self.s5_u = new("s5_u")
        self.cv_mm = new("cv_mm")
        self.cv_cc = new("cv_cc")
        self.cv_out = new("cv_out")
        self.mg_act = new("mg_act")
        self.mg_mix = new("mg_mix")
        self.wo_mm = new("wo_mm")
        self.ff_mm = new("ff_mm")
        self.ff_act = new("ff_act")
        self.ff_hid = new("ff_hid")
        self.out_done = new("out_done")
        self.w_ready = [new(f"w_ready{i}") for i in range(RING)]


class Inverse:

    def __init__(self, new):
        self.D = new()
        self.EB = new()
        self.A = new()
        self.XT = new()
        self.T = new()
        self.U = new()
        self.Y = new()


class States:

    def __init__(self, new):
        self.zr, self.zi = new(), new()
        self.wr, self.wi = new(), new()
        self.xr, self.xi = new(), new()


class Position:

    def __init__(self):
        self.n, self.uses, self.w = 0, [0] * RING, None



def build(nc, A):
    with ExitStack() as stack:
        s = Signals(lambda name: stack.enter_context(nc.semaphore(name)))
        w_ready = s.w_ready

        arena = stack.enter_context(nc.sbuf_tensor("arena", [P, 53000], F32))
        top = [0]

        def carve(*shape):
            n = int(np.prod(shape))
            a = arena[:, top[0]:top[0] + n]
            top[0] += n
            assert top[0] <= 53000, top[0]
            if len(shape) == 2:
                return a.rearrange("p (a b) -> p a b", a=shape[0])
            if len(shape) == 3:
                return a.rearrange("p (a b c) -> p a b c", a=shape[0], b=shape[1])
            return a

        ps = stack.enter_context(nc.psum_tensor("ps", [P, 8, 512], F32))

        RT = carve(KD, N)
        cols = carve(NCOLS)
        ident = carve(P)
        ones = carve(P)
        cum = carve(2, P)
        negm = carve(2, P)
        epsc = carve(1)
        onec = carve(1)
        cact = carve(KD, 2)
        ada = carve(2, 48, 2)
        gs1 = carve(2, 2, 2 * KD)
        ring = carve(RING, CHUNK)
        base = top[0]
        ones2 = ones

        def col(name, i=0, w=1):
            a, n = AT[name]
            assert i + w <= n
            return cols[:, a + i:a + i + w]

        hT = carve(KD, N)
        g0 = top[0]
        qkv = [carve(HG, N) for _ in range(3)]
        oT = carve(HG, N)
        S = [carve(HG, P) for _ in range(2)]
        bmask = carve(2, LEVELS, 64)
        rmask = carve(2, LEVELS)
        sel = carve(GH, P)
        rows = carve(N)
        betag = carve(NT, 32)
        beta = carve(NT, 16)
        gsp = carve(NT, 16)
        gtmp = carve(NT, 16)
        gcum = carve(NT, 16)
        ngc = carve(NT, 16)
        beg = carve(NT, 16)
        ea = carve(16)
        el = carve(2, HG)
        kcol = carve(2, HG)
        g1 = top[0]
        sets = [Inverse(lambda: carve(HG, P)) for _ in range(2)]
        gend = top[0]
        top[0] = g1
        pre = [carve(N + 3) for _ in range(2)]
        cv = [carve(N + 1) for _ in range(3)]
        sq = [carve(N) for _ in range(2)]
        rt = [carve(N) for _ in range(2)]
        assert top[0] <= gend, (top[0], gend)
        top[0] = base
        xsT = carve(KD * NE * SLOTS)
        htok = carve(NT, D)
        selx = carve(NT - XT0, NE * CAPX)
        selc = carve(XT0, NE * CAPC)
        Yx = carve(2, D)
        Yc = carve(D)
        hid = carve(KD * SLOTS)
        xcur = [carve(KD * SLOTS) for _ in range(2)]
        sg = [carve(2 * SLOTS) for _ in range(2)]
        aff = carve(NT, NE)
        smx = carve(NT)
        post = carve(NT, NE)
        affT = carve(N)
        rank = carve(N)
        top8 = carve(8)
        iota = carve(CAPX)
        rw = carve(2, KD * NE)
        selxT = htok.rearrange("p a b -> p (a b)")[:, 0:8 * SEQ].rearrange("p (a b) -> p a b", a=8)
        selcT = htok.rearrange("p a b -> p (a b)")[:, 8 * SEQ:8 * SEQ + 4 * CTX].rearrange("p (a b) -> p a b", a=4)
        top[0] = base
        h2 = carve(KD, SEQ)
        qT = carve(4, SEQ)
        kS, kW, kC, vC = carve(SEQ), carve(SEQ), carve(SEQ), carve(SEQ)
        vS = carve(2, 4, P)
        ng = carve(4, 3 * NH)
        kcm = carve(NCMP)
        vcm = carve(P)
        hidc = carve(2, 4, NCMP)
        cmask = carve(4, NCMP)
        ones64 = carve(P)
        qg = carve(1)
        bsq = [carve(SEQ) for _ in range(2)]
        brt = [carve(SEQ) for _ in range(2)]
        Pb = bsq
        PTb = brt
        asum = carve(96)
        anm = carve(96)
        acoef = carve(32, 3)
        csc = [carve(NCMP) for _ in range(2)]
        oTok = carve(4, SEQ)
        oA = qT
        uT = carve(4, SEQ)
        yg = carve(4, SEQ)
        ycv = carve(4, SEQ)
        b_end = top[0]
        Ec, Es = carve(4, SEQ), carve(4, SEQ)
        Bbd = carve(2, 4, P)
        Cbd = carve(2, NST, 32)
        braw, craw = carve(2, 4, 64), carve(2, NST, 16)
        parb, parc = carve(2), carve(2)
        sk, ck, fk, fr = carve(9, NST), carve(9, NST), carve(9, NST), carve(9, NST)
        dt5, r5, f5, nr5, ni5, kr5, ki5, t5, den5 = (carve(NST) for _ in range(9))
        c1t, c2t = carve(NST, 16), carve(NST, 16)
        S5 = States(lambda: carve(SEQ))
        S5.t1, S5.t2 = kS, kW
        S5.t3, S5.t4 = (vS[:, i].rearrange("p a b -> p (a b)") for i in range(2))
        S5.p1, S5.p2 = kC, vC
        pt1, pt2 = (ycv[:, 2 * i:2 * i + 2, :].rearrange("p a b -> p (a b)").rearrange("p (a b) -> p a b", a=4) for i in range(2))
        s5_end = top[0]
        top[0] = b_end
        ccs = carve(SEQ)
        zpad = carve(SEQ + 2)
        cvt = carve(SEQ)
        top[0] = b_end
        mixed = carve(KD, SEQ)
        mact = [carve(SEQ) for _ in range(4)]
        mt1, mt2, mt3 = carve(SEQ), carve(SEQ), carve(SEQ)
        top[0] = base + KD * N + 6 * N
        fhid = carve(FF2 // P, SEQ)
        fact = [carve(SEQ) for _ in range(2)]
        top[0] = base + KD * N
        yT = carve(SI // P, SEQ)
        s_xT = carve(2, N)
        s_B = carve(N)
        s_C = carve(SEQ)
        s_xtok = carve(NT, SR * SP_)
        s_Btok = carve(NT, P)
        s_h = carve(2, SR * SP_)
        s_yt = carve(NT - XT0, SR * SP_)
        s_rows = carve(SEQ)
        s_sel = carve(SR, P)
        s_dt = carve(NT, 2 * SH)
        s_a = carve(NT, 2 * SH)
        s_te = carve(NT, 2 * SH)
        s_etot = carve(NT, 2 * SH)
        s_tmp = carve(NT, 2 * SH)
        s_A = carve(2 * SH)
        s_pre = [carve(N + 3) for _ in range(2)]
        s_cv = [carve(N + 1) for _ in range(2)]
        s_D = [carve(SR, P) for _ in range(2)]
        s_xdt = [carve(SR, SP_) for _ in range(2)]
        s_xe = [carve(SR, SP_) for _ in range(2)]
        s_yi = [carve(SR, SP_) for _ in range(2)]
        z_act = [s_pre[i][:, 0:SEQ] for i in range(2)]
        z_sq = [s_cv[i][:, 0:SEQ] for i in range(2)]
        z_rt, z_rs = s_D[0].rearrange("p a b -> p (a b)"), s_D[1].rearrange("p a b -> p (a b)")
        z_tmp = [s_xT[:, i, 0:SEQ] for i in range(2)]
        top[0] = g0
        nsqb = [carve(N) for _ in range(4)]
        nrtb = carve(N)
        nrsb = carve(N)


        def source(item):
            kind = item[0]
            if kind == "ada":
                _, l, n = item
                src = A["ada_w"][l].rearrange("(k p) n -> p k n", p=P)[:, :, n * CW:(n + 1) * CW]
            elif kind == "gtail":
                src = A["gdn_w_in"][0].rearrange("(k p) n -> p k n", p=P)[:, :, 4096:4128]
            elif kind == "gin":
                _, part, hg, n = item
                a = part * 1024 + hg * 512 + n * CW
                src = A["gdn_w_in"][0].rearrange("(k p) n -> p k n", p=P)[:, :, a:a + CW]
            elif kind == "gz":
                _, hg, n = item
                a = 3072 + hg * 512 + n * CW
                src = A["gdn_w_in"][0].rearrange("(k p) n -> p k n", p=P)[:, :, a:a + CW]
            elif kind == "gout":
                _, hg, n = item
                a = hg * 512 + n * CW
                src = A["gdn_w_out"][0].rearrange("(k p) n -> p k n", p=P)[:, 4 * hg + 2 * n:4 * hg + 2 * n + 2, :]
            elif kind == "stail":
                src = A["ssd_w_in"][0].rearrange("(k p) n -> p k n", p=P)[:, 4 * item[1]:4 * item[1] + 4, 6144:6208]
            elif kind in ("sx", "sz"):
                a = (SI if kind == "sx" else 0) + CW * item[1]
                src = A["ssd_w_in"][0].rearrange("(k p) n -> p k n", p=P)[:, :, a:a + CW]
            elif kind in ("sb", "sc"):
                a = 2 * SI + (SG * P if kind == "sc" else 0) + P * item[1]
                src = A["ssd_w_in"][0].rearrange("(k p) n -> p k n", p=P)[:, :, a:a + P]
            elif kind == "sout":
                src = A["ssd_w_out"][0].rearrange("(k p) n -> p k n", p=P)[:, :, P * item[1]:P * item[1] + P]
            else:
                return source2(item)
            return [(lambda w: w, src)]

        def source2(item):
            kind = item[0]
            win = A["w_in_2"][0].rearrange("(k p) n -> p k n", p=P)

            def whole(src):
                return [(lambda w: w, src)]

            if kind == "bv":
                a, w = ((WVS, P), (WVW, P), (WNG, 24))[item[1]]
                return whole(win[:, :, a:a + w])
            if kind == "bq":
                src = win[:, 4 * item[1]:4 * item[1] + 4, WQ:WQ + 512].rearrange("p k (two j c) -> p k two j c", two=2, j=4)
                return [((lambda v, x=x, k=k: v.rearrange("p k (j two c) -> p k two j c", two=2, j=4)[:, k, x]), src[:, k, x]) for x in range(2) for k in range(4)]
            if kind == "bk":
                a = (WKS, WKW, WKC, WVC)[item[1]]
                return whole(win[:, :, a:a + P])
            if kind == "c1":
                _, which, n = item
                src = A["cmp_w1_2"][0, which].rearrange("(i d) f -> d i f", d=HD)[:, 8 * n:8 * n + 8, :]
                return [(lambda w: w[0:HD], src), (lambda w: w[HD:P], src)]
            if kind == "c2":
                return [((lambda w, x=x: w[:, 2 * x:2 * x + 2, :]), A["cmp_w2_2"][0, x].rearrange("(c p) d -> p c d", p=P))
                        for x in range(2)]
            if kind in ("bu", "cc", "cx", "cb"):
                a = dict(bu=WU, cc=WCC, cx=WCX, cb=WCB)[kind] + CW * item[1]
                return whole(win[:, :, a:a + CW])
            if kind == "mg":
                a = WMG + D * item[1] + P * item[2]
                return whole(win[:, :, a:a + P])
            if kind == "glu":
                w = A["ssm_w_glu_2"][0].rearrange("(k p) n -> p k n", p=P)
                return [((lambda v, x=x: v[:, 4 * x:4 * x + 4, :]), w[:, :, D * x + P * item[1]:D * x + P * item[1] + P]) for x in range(2)]
            if kind in ("cvo", "nso"):
                w = (A["conv_w_out_2"] if kind == "cvo" else A["nsa_w_o_2"])[0].rearrange("(k p) n -> p k n", p=P)
                return whole(w[:, :, P * item[1]:P * item[1] + P])
            if kind == "wo":
                return whole(A["w_out_2"][0].rearrange("(k p) n -> p k n", p=P)[:, :, CW * item[1]:CW * item[1] + CW])
            if kind in ("fg", "fu"):
                a = (FF2 if kind == "fu" else 0) + CW * item[1]
                return whole(A["ffn_w_gate_up_2"][0].rearrange("(k p) n -> p k n", p=P)[:, :, a:a + CW])
            if kind == "fd":
                _, m, half = item
                return whole(A["ffn_w_down_2"][0].rearrange("(k p) n -> p k n", p=P)[:, 11 * half:11 * half + 11, P * m:P * m + P])
            raise KeyError(kind)

        def shape_of(item):
            if item[0] == "c2":
                return (4, HD)
            if item[0] == "glu":
                return (8, P)
            if item[0] == "bq":
                return (4, 512)
            return tuple(source(item)[0][1].shape[1:])

        def slot_view(slot, shape):
            n = int(np.prod(shape))
            return ring[:, slot, 0:n].rearrange("p (a b) -> p a b", a=shape[0])

        nstt0 = [0, 16, 32, 48, 56, 64, 72]
        nrt0 = [0, 2, 4, 6, 7, 8, 9]
        RES_GDN = 2 * KD * GH // HG
        GA = [24, 24 + 16]
        RES_SSD = RES_GDN + KD
        TILES = 7
        AFTER = (2, 4, 6, 7)
        MSETS = ((XSET, CSET), (XSET,))
        MOE0 = [USED[("moe", l)] - NE * 12 if ("moe", l) in USED else 0 for l in range(2)]

        nsqb_g = sq
        block = stack.enter_context(nc.Block())

        @block.sync
        def _(sp):
            sp.dma_start(cols, A["cols"]).then_inc(s.const_in, 16)
            sp.wait_ge(s.const_in, 16)
            sp.dma_start(RT, A["tokens"]).then_inc(s.const_in, 16)
            for l in range(2):
                sp.dma_start(rw[:, l, :].rearrange("p (k e) -> p k e", k=KD),
                             A["router_w"][l].rearrange("(k p) e -> p k e", p=P)).then_inc(s.router_in, 16)
            def load(item):
                n = USED[item] - 1
                slot = (n + RING0) % RING
                if n >= RING:
                    sp.wait_ge(s.w_used, n - RING + 1)
                whole = slot_view(slot, shape_of(item))
                for part, src in source(item):
                    sp.dma_start(part(whole), src).then_inc(w_ready[slot], 16)

            def load_experts(l):
                up = A["moe_w_up"][l].rearrange("e (k p) f -> p e k f", p=P)
                gate = A["moe_w_gate"][l].rearrange("e (k p) f -> p e k f", p=P)
                down = A["moe_w_down"][l].rearrange("e (k p) f -> p e k f", p=P)
                with sp.Fori(0, NE // EB) as it:
                    for j in range(EB):
                        e = bass.ds(it * EB + j, 1)
                        for n in range(12):
                            slot = (12 * j + n) % RING
                            sp.wait_ge(s.w_used, it * (12 * EB) + (MOE0[l] + 12 * j + n - RING + 1))
                            if n < 8:
                                src = (gate, up)[n % 2][:, e, :, CW * (n // 2):CW * (n // 2) + CW]
                                dst = slot_view(slot, (KD, CW))
                            else:
                                src = down[:, e, 2 * (n - 8):2 * (n - 8) + 2, :]
                                dst = slot_view(slot, (2, D))
                            sp.dma_start(dst.unsqueeze(1), src).then_inc(w_ready[slot], 16)
            for item in PLAN:
                if item[0] == "moe":
                    load_experts(item[1])
                    continue
                load(item)
            for m in range(KD):
                sp.wait_ge(s.resid, RES_SSD + KD + m + 1)
                sp.dma_start(A["out"][m], RT[:, m, CTX:N]).then_inc(s.out_done, 16)
            sp.wait_ge(s.out_done, 16 * KD)


        @block.gpsimd
        def _(pool):
            g = Lane(pool, s.pool_steps)
            g.do(pool.memset(ident, 0.0))
            g.do(pool.memset(cum, 1.0))
            g.do(pool.memset(negm, 0.0))
            g.do(pool.memset(ones, 1.0), s.mask_done)
            g.do(pool.memset(epsc, EPS), s.mask_done)
            g.do(pool.memset(onec, 1.0), s.mask_done)
            g.settle()
            keep = dict(compare_op=ALU.is_ge, base=0)
            g.do(pool.affine_select(out=ident, in_=ident, compare_op=ALU.not_equal, fill=1.0, base=0,
                                    pattern=[[-1, P]], channel_multiplier=1), s.mask_done)
            for d, sign in ((0, 1), (1, -1)):
                g.do(pool.affine_select(out=cum[:, d, :], in_=cum[:, d, :], fill=0.0, pattern=[[sign, P]],
                                        channel_multiplier=-sign, **keep), s.mask_done)
                g.do(pool.affine_select(out=negm[:, d, :], in_=negm[:, d, :], fill=NEG, pattern=[[sign, P]],
                                        channel_multiplier=-sign, **keep), s.mask_done)
            g.do(pool.memset(bmask, 1.0))
            g.do(pool.memset(sel, 0.0))
            for d in range(2):
                for l in range(LEVELS):
                    b, nb = 1 << l, 64 >> l
                    m = bmask[:, d, l, :].rearrange("p (n b) -> p n b", b=b)
                    lo, hi = (b, 2 * b - 1) if d == 0 else (0, b - 1)
                    g.settle()
                    g.do(pool.affine_select(out=m, in_=m, fill=0.0, pattern=[[-2 * b, nb], [0, b]],
                                            channel_multiplier=1, compare_op=ALU.is_ge, base=-lo))
                    g.settle()
                    g.do(pool.affine_select(out=m, in_=m, fill=0.0, pattern=[[2 * b, nb], [0, b]],
                                            channel_multiplier=-1, compare_op=ALU.is_ge, base=hi), s.level_masks)
            g.settle()
            pool.wait_ge(s.mask_done, 8)
            for q in range(4):
                g.do(pool.tensor_copy(sel[32 * q:32 * q + GH, :, :],
                                      ident[32 * q:32 * q + GH, 32 * q:32 * q + GH].unsqueeze(2)
                                      .to_broadcast([GH, GH, P])), s.mask_done)

            g.settle()
            g.do(pool.iota(iota, pattern=[[1, CAPX]], base=0, channel_multiplier=0, allow_small_or_imprecise_dtypes=True), s.iota_done)

            def current_rows(l):
                ns = sum(MSET[2] and CAPC or CAPX for MSET in MSETS[l])
                xs = xsT[:, 0:KD * NE * ns].rearrange("p (k e) -> p k e", k=KD)
                pool.wait_ge(s.ga_copied, GA[l])
                with pool.Fori(0, NE // EB) as it:
                    for j in range(EB):
                        pool.wait_ge(s.w_used, it * (12 * EB) + (MOE0[l] + 12 * (j - 2) + 8))
                        pool.tensor_copy(xcur[j % 2][:, 0:KD * ns].rearrange("p (k e) -> p k e", k=KD),
                                         xs[:, :, bass.ds(it * (EB * ns) + j * ns, ns)]).then_inc(s.x_cur, 1)

            current_rows(0)
            current_rows(1)

            pool.wait_ge(s.nstt, 72)
            g.do(pool.memset(cmask, 0.0))
            g.do(pool.memset(ones64, 0.0))
            g.settle()
            for q in range(4):
                g.do(pool.affine_select(out=cmask[:, q, :], in_=cmask[:, q, :], compare_op=ALU.is_ge, fill=NEG,
                                        base=P * q - (CMPB - 1), pattern=[[-CMPB, NCMP]], channel_multiplier=1), s.mask_done)
            g.settle()
            for half in range(2):
                g.do(pool.memset(ones64[HD * half:HD * half + HD, HD * half:HD * half + HD], 1.0), s.mask_done)
                g.settle()
            g.do(pool.memset(parc, 0.0))
            g.settle()
            for half in range(2):
                g.do(pool.memset(parc[HD * half:HD * half + HD, half:half + 1], 1.0), s.mask_done)
                g.settle()
            pool.wait_ge(s.s5_act, 4)

            def tables(b):
                g.do(pool.memset(Ec[:, :, 0:1], 1.0))
                g.do(pool.memset(Es[:, :, 0:1], 0.0))
                for k in range(9):
                    n = 1 << k
                    c = ck[:, k, 4 * b:4 * b + 4].unsqueeze(2).to_broadcast([P, 4, n])
                    si = sk[:, k, 4 * b:4 * b + 4].unsqueeze(2).to_broadcast([P, 4, n])
                    for out, f1, f2, op in ((Ec, c, si, ALU.subtract), (Es, si, c, ALU.add)):
                        g.settle()
                        g.do(pool.tensor_tensor(pt1[:, :, 0:n], Ec[:, :, 0:n], f1, ALU.mult))
                        g.do(pool.tensor_tensor(pt2[:, :, 0:n], Es[:, :, 0:n], f2, ALU.mult))
                        g.settle()
                        last = k == 8 and out is Es
                        g.do(pool.tensor_tensor(out[:, :, n:2 * n], pt1[:, :, 0:n], pt2[:, :, 0:n], op), s.s5_tab if last else None)

            def turn_back(st):
                c, si = Ec[:, st % 4, :], Es[:, st % 4, :]
                z = S5
                pool.wait_ge(s.s5_w, st + 1)
                if st:
                    pool.wait_ge(s.s5_y, st)
                for out, f1, f2, op in ((z.xr, c, si, ALU.subtract), (z.xi, si, c, ALU.add)):
                    g.settle()
                    g.do(pool.tensor_tensor(z.p1, z.wr, f1, ALU.mult))
                    g.do(pool.tensor_tensor(z.p2, z.wi, f2, ALU.mult))
                    g.settle()
                    g.do(pool.tensor_tensor(out, z.p1, z.p2, op), s.s5_x)
                g.settle()
                
            for st in range(NST):
                if st % 4 == 0:
                    tables(st // 4)
                turn_back(st)

        MASKS = 12

        @block.tensor
        def _(pe):
            state = Position()

            def take(item):
                assert PLAN[state.n] == item, (PLAN[state.n], item)
                slot = (USED[item] - 1 + RING0) % RING
                state.uses[slot] += len(source(item))
                state.n += 1
                pe.wait_ge(w_ready[slot], 16 * state.uses[slot])
                return slot_view(slot, shape_of(item))

            def ada_chunk(l, n):
                w = take(("ada", l, n))
                i = 24 * l + n
                if i >= 1:
                    pe.wait_ge(s.ada_copied, i)
                for m in range(2):
                    for k in range(KD):
                        mm = pe.matmul(ps[:, 7, 2 * m:2 * m + 2], w[:, k, m * P:(m + 1) * P], cact[:, k, :],
                                       start=(k == 0), stop=(k == KD - 1))
                mm.then_inc(s.w_used, 1)

            def norm_sums(call, sets):
                for k in range(KD):
                    pe.wait_ge(s.nsq, KD * call + k + 1)
                    for j, (c0, nc_, _) in enumerate(sets):
                        mm = pe.matmul(ps[:, j, 0:nc_], ones, nsqb[k % 4][:, c0:c0 + nc_],
                                       start=(k == 0), stop=(k == KD - 1))
                    mm.then_inc(s.nsq_sum, 1)

            pe.wait_ge(s.cv_done, 1)
            for n in range(24):
                ada_chunk(0, n)
            pe.wait_ge(s.mask_done, MASKS)
            norm_sums(0, (XSET, CSET))

            w = take(("gtail",))
            pe.wait_ge(s.h_ready, 16)
            for t in range(NT):
                for k in range(KD):
                    mm = pe.matmul(ps[:, 6, 32 * t:32 * t + 32], hT[:, k, t * P:(t + 1) * P], w[:, k, :],
                                   start=(k == 0), stop=(k == KD - 1))
            mm.then_inc(s.w_used, 1)
            pe.wait_ge(s.gt_g, 1)
            for t in range(NT):
                for d in range(2):
                    mm = pe.matmul(ps[:, 5, 16 * t + 8 * d:16 * t + 8 * d + 8], cum[:, d, :], gsp[:, t, 8 * d:8 * d + 8],
                                   start=True, stop=True)
            mm.then_inc(s.gc_mm, 1)
            for t in range(NT):
                bank, c = (3, t * P) if t < 4 else (4, (t - 4) * P)
                for d in range(2):
                    pe.matmul(ps[32 * d:32 * d + GH, bank, c:c + P], gsp[:, t, 8 * d:8 * d + 8], cum[:, d, :],
                              start=True, stop=True)
                    mm = pe.matmul(ps[64 + 32 * d:64 + 32 * d + GH, bank, c:c + P], beta[:, t, 8 * d:8 * d + 8],
                                   ident, start=True, stop=True)
            mm.then_inc(s.gr_mm, 1)
            pe.wait_ge(s.gr_rows, 8)

            def project(hg):
                def tile(i):
                    if i % 2 == 0:
                        state.w = take(("gin", i // 4, hg, (i // 2) % 2))
                    if i >= 2:
                        pe.wait_ge(s.gp_pre, 2 * (12 * hg + i - 1))
                    elif hg:
                        pe.wait_ge(s.resid, 16 * hg)
                    m = i % 2
                    for j, (c0, nn, _) in enumerate((XSET, CSET)):
                        for k in range(KD):
                            mm = pe.matmul(ps[:, 2 * (i % 2) + j, 0:nn], state.w[:, k, m * P:(m + 1) * P],
                                           hT[:, k, c0:c0 + nn], start=(k == 0), stop=(k == KD - 1))
                    mm.then_inc(s.w_used if i % 2 else s.gp_mm, 1)

                def sums(i):
                    pe.wait_ge(s.gp_sq, 8 * hg + i + 1)
                    if i >= 2:
                        pe.wait_ge(s.gp_rt, 2 * (8 * hg + i - 1))
                    for j, (c0, nn, _) in enumerate((XSET, CSET)):
                        mm = pe.matmul(ps[:, 4 + j + 2 * (i % 2), 0:nn], ones, sq[i % 2][:, c0:c0 + nn], start=True, stop=True)
                    mm.then_inc(s.gp_sum, 1)

                for i in range(14):
                    if i < 12:
                        tile(i)
                    if 2 <= i < 10:
                        sums(i - 2)

            def recurrence(hg):
                q, k_, v = qkv
                for st in range(6):
                    n = hg * 6 + st
                    cs = [slice(CHUNK_OF[d][st] * P, CHUNK_OF[d][st] * P + P) for d in range(2)]
                    for d in range(2):
                        if st == 0 and d == 0:
                            pe.wait_ge(s.gp_act, 24 * hg + 24)
                            pe.wait_ge(s.gp_norm, 8 * hg + 8)
                        if st > 0:
                            pe.wait_ge(s.r_state, 2 * (n - 1) + d + 1)
                        B = 4 * d
                        for j in range(HG):
                            h = hg * HG + j
                            o = slice(j * P, j * P + P)
                            pe.matmul(ps[:, B, o], sel[32 * d:32 * d + GH, h, :], rows[32 * d:32 * d + GH, cs[d]],
                                      start=True, stop=True)
                            pe.matmul(ps[:, B + 1, o], sel[64 + 32 * d:64 + 32 * d + GH, h, :],
                                      rows[64 + 32 * d:64 + 32 * d + GH, cs[d]], start=True, stop=True)
                            pe.matmul(ps[:, B + 2, o], k_[:, j, cs[d]], k_[:, j, cs[d]], start=True, stop=True)
                            mm = pe.matmul(ps[:, B + 3, o], k_[:, j, cs[d]], q[:, j, cs[d]], start=True, stop=True)
                        mm.then_inc(s.r_in, 1)
                    for l in range(LEVELS):
                        b = 1 << l

                        def half(x, j, odd):
                            return x[:, j, :].rearrange("p (n two b) -> p n two b", two=2, b=b)[:, :, odd, :]

                        for d in range(2):
                            z = sets[d]
                            if l == 0:
                                pe.wait_ge(s.r_xt, 2 * n + d + 1)
                            else:
                                pe.wait_ge(s.r_l, 2 * ((LEVELS - 1) * n + l - 1) + d + 1 + (2 * n))
                            for j in range(HG):
                                mm = pe.matmul(ps[:, 4 * d, 64 * j:64 * j + 64], z.XT[:, j, :], half(z.T, j, d),
                                               start=True, stop=True)
                            mm.then_inc(s.r_y, 1)
                        for d in range(2):
                            z = sets[d]
                            pe.wait_ge(s.r_ym, 2 * (LEVELS * n + l) + d + 1)
                            for j in range(HG):
                                if l < LEVELS - 1:
                                    pe.matmul(ps[:, 4 * d + 1, 64 * j:64 * j + 64], z.U[:, j, :], half(z.Y, j, d),
                                              start=True, stop=True)
                                mm = pe.matmul(ps[:, 4 * d + 2, 64 * j:64 * j + 64], z.Y[:, j, :], half(z.U, j, 1 - d),
                                               start=True, stop=True)
                            mm.then_inc(s.r_tu, 1)
                    for d in range(2):
                        pe.wait_ge(s.r_l, 2 * (LEVELS * n + LEVELS - 1) + d + 1)
                        for j in range(HG):
                            pe.transpose(ps[:, 4 * d, j * P:j * P + P], k_[:, j, cs[d]], ident)
                            mm = pe.transpose(ps[:, 4 * d + 1, j * P:j * P + P], v[:, j, cs[d]], ident)
                        mm.then_inc(s.r_kv, 1)
                    ada_chunk(1, hg * 12 + 2 * st)
                    for d in range(2):
                        z = sets[d]
                        pe.wait_ge(s.r_kvs, 2 * n + d + 1)
                        for j in range(HG):
                            mm = pe.matmul(ps[:, 4 * d + 2, j * P:j * P + P], z.XT[:, j, :], z.U[:, j, :], start=True, stop=True)
                        mm.then_inc(s.r_w, 1)
                    ada_chunk(1, hg * 12 + 2 * st + 1)
                    for d in range(2):
                        z = sets[d]
                        pe.wait_ge(s.r_nw, 2 * n + d + 1)
                        for j in range(HG):
                            o = ps[:, 4 * d + 3, j * P:j * P + P]
                            if d == 1:
                                pe.wait_ge(s.ada_copied, 24 + hg * 12 + 2 * st + 2)
                            pe.matmul(o, z.U[:, j, :], z.T[:, j, :], start=True, stop=False)
                            mm = pe.matmul(o, z.D[:, j, :], S[d][:, j, :], start=False, stop=True)
                        mm.then_inc(s.r_vn, 1)
                    for d in range(2):
                        z = sets[d]
                        pe.wait_ge(s.r_vnc, 2 * n + d + 1)
                        for j in range(HG):
                            o = ps[:, 4 * d, j * P:j * P + P]
                            pe.matmul(o, S[d][:, j, :], z.EB[:, j, :], start=True, stop=False)
                            pe.matmul(o, z.XT[:, j, :], z.A[:, j, :], start=False, stop=True)
                            mm = pe.matmul(ps[:, 4 * d + 1, j * P:j * P + P], z.Y[:, j, :], z.XT[:, j, :], start=True, stop=True)
                        mm.then_inc(s.r_o, 1)

            def gdn_out(hg):
                for j in range(HG):
                    i = hg * HG + j
                    pe.wait_ge(s.go_sq, i + 1)
                    if j >= 1:
                        pe.wait_ge(s.go_rt, 2 * i)
                    else:
                        pe.wait_ge(s.r_state, 12 * hg + 12)
                    for b, (c0, nn, _) in enumerate((XSET, CSET)):
                        mm = pe.matmul(ps[:, b, 0:nn], ones, nsqb_g[j % 2][:, c0:c0 + nn], start=True, stop=True)
                    mm.then_inc(s.go_sum, 1)
                    if j % 2 == 0:
                        state.w = take(("gz", hg, j // 2))
                    if i >= 2:
                        pe.wait_ge(s.go_sz, 2 * (i - 1))
                    for b, (c0, nn, _) in enumerate((XSET, CSET)):
                        for k in range(KD):
                            mm = pe.matmul(ps[:, 2 + b + 2 * (j % 2), 0:nn], state.w[:, k, (j % 2) * P:(j % 2) * P + P],
                                           hT[:, k, c0:c0 + nn], start=(k == 0), stop=(k == KD - 1))
                    mm.then_inc(s.w_used if j % 2 else s.go_z, 1)
                w = [take(("gout", hg, 0)), None]
                w[1] = take(("gout", hg, 1))
                pe.wait_ge(s.go_o, HG * (hg + 1))
                for m in range(KD):
                    i = hg * KD + m
                    if m >= 2:
                        pe.wait_ge(s.resid, 2 * (i - 1))
                    for b, (c0, nn, _) in enumerate((XSET, CSET)):
                        for j in range(HG):
                            mm = pe.matmul(ps[:, b + 2 * (m % 2), 0:nn], w[j // 2][:, j % 2, m * P:(m + 1) * P],
                                           oT[:, j, c0:c0 + nn], start=(j == 0), stop=(j == HG - 1))
                    if m == KD - 1:
                        mm.then_inc(s.w_used, 2)
                    else:
                        mm.then_inc(s.go_mm, 1)

            for hg in range(GH // HG):
                project(hg)
                recurrence(hg)
                gdn_out(hg)

            def route(l):
                msets = MSETS[l]
                tiles = list(range(XT0 if l else 0, NT))
                pe.wait_ge(s.h_ready, (32, 56)[l])
                pe.wait_ge(s.router_in, 32)
                for t in tiles:
                    for k in range(KD):
                        mm = pe.matmul(ps[:, 2, NE * t:NE * t + NE], hT[:, k, t * P:(t + 1) * P],
                                       rw[:, l, NE * k:NE * k + NE], start=(k == 0), stop=(k == KD - 1))
                mm.then_inc(s.lg_mm, 1)
                for i, (t, half) in enumerate([(t, half) for t in tiles for half in range(2)]):
                    if i >= 2:
                        pe.wait_ge(s.ht_copied, 12 * l + i - 1)
                    for k in range(4):
                        mm = pe.transpose(ps[:, 6 + i % 2, k * P:k * P + P], hT[:, 4 * half + k, t * P:(t + 1) * P], ident)
                    mm.then_inc(s.ht_mm, 1)
                pe.wait_ge(s.aff_ready, l + 1)
                for t in tiles:
                    bank, c = (3, (t - XT0) * P) if t >= XT0 else (4, t * P)
                    mm = pe.transpose(ps[0:NE, bank, c:c + P], aff[:, t, :], ident)
                mm.then_inc(s.afft_mm, 1)
                pe.wait_ge(s.posm_ready, len(msets) * (l + 1) - (l and 0) if l == 0 else 3)
                for t in tiles:
                    mm = pe.transpose(ps[:, 5, NE * t:NE * t + NE], rank[0:NE, t * P:(t + 1) * P], ident[0:NE, 0:NE])
                mm.then_inc(s.post_mm, 1)
                pe.wait_ge(s.sel_ready, (6, 10)[l])
                pe.wait_ge(s.ht_copied, (12, 20)[l])
                i = 0
                for m in range(KD):
                    for b in range(3 if l == 0 else 2):
                        if i >= 4:
                            pe.wait_ge(s.ga_copied, (0, 24)[l] + i - 3)
                        ts_ = range(XT0) if b == 2 else range(XT0, NT)
                        for t in ts_:
                            rhs = selc[:, t, :] if b == 2 else selx[:, t - XT0, 512 * b:512 * b + 512]
                            mm = pe.matmul(ps[:, i % 4, :], htok[:, t, m * P:(m + 1) * P], rhs,
                                           start=(t == ts_[0]), stop=(t == ts_[-1]))
                        mm.then_inc(s.ga_mm, 1)
                        i += 1
                pe.wait_ge(s.selg_ready, (6, 10)[l])
                pe.wait_ge(s.ga_copied, GA[l])
                for i in range(8 + (4 if l == 0 else 0)):
                    if i >= 2:
                        pe.wait_ge(s.st_copied, (0, 12)[l] + i - 1)
                    if i < 8:
                        for t in range(XT0, NT):
                            mm = pe.transpose(ps[:, 6 + i % 2, (t - XT0) * P:(t - XT0 + 1) * P], selx[:, t - XT0, i * P:(i + 1) * P], ident)
                    else:
                        for t in range(XT0):
                            mm = pe.transpose(ps[:, 6 + i % 2, t * P:(t + 1) * P], selc[:, t, (i - 8) * P:(i - 7) * P], ident)
                    mm.then_inc(s.st_mm, 1)

            def experts(l):
                ns = (SLOTS, CAPX)[l]
                first = state.n
                base_uses = list(state.uses)
                pe.wait_ge(s.st_copied, (12, 20)[l])
                with pe.Fori(0, NE // EB) as it:
                    pe.wait_ge(s.sc_free, it * KD + (2 + l * 34))
                    for j in range(EB):
                        xc = xcur[j % 2][:, 0:KD * ns].rearrange("p (k e) -> p k e", k=KD)
                        pe.wait_ge(s.x_cur, it * EB + (j + 1 + NE * l))

                        def chunk(n, shape):
                            slot = (12 * j + n) % RING
                            pe.wait_ge(w_ready[slot], it * (16 * 12 * EB // RING) + 16 * (base_uses[slot] + (12 * j + n) // RING + 1))
                            return slot_view(slot, shape)

                        for c in range(4):
                            pe.wait_ge(s.gu_free, it * (4 * EB) + (4 * j + c + 1 + l * 66))
                            for b in (0, 2):
                                w = chunk(2 * c + b // 2, (KD, CW))
                                for m in range(2):
                                    for k in range(KD):
                                        mm = pe.matmul(ps[:, b + c % 2, m * ns:(m + 1) * ns], w[:, k, m * P:(m + 1) * P], xc[:, k, :],
                                                       start=(k == 0), stop=(k == KD - 1))
                                mm.then_inc(s.w_used, 1)
                        pe.wait_ge(s.y_free, it * EB + (j + 1 + l * 18))
                        h3 = hid[:, 0:KD * ns].rearrange("p (k e) -> p k e", k=KD)
                        for d in range(4):
                            w = chunk(8 + d, (2, D))
                            pe.wait_ge(s.gu_free, it * (4 * EB) + (4 * j + d + 3 + l * 66))
                            for kk in range(2):
                                for half in range(2):
                                    mm = pe.matmul(ps[0:ns, 4 + 2 * (j % 2) + half, :], h3[:, 2 * d + kk, :], w[:, kk, 512 * half:512 * half + 512],
                                                   start=(d == 0 and kk == 0), stop=(d == 3 and kk == 1))
                            mm.then_inc(s.w_used, 1)
                    pe.wait_ge(s.y_free, it * EB + (EB + 2 + l * 18))
                    for m in range(KD):
                        pe.wait_ge(s.sc_free, it * KD + (m + 1 + l * 34))
                        for p in range(2):
                            mm = pe.matmul(ps[:, m % 2, :], Yx[:, p, m * P:(m + 1) * P], selxT[:, bass.ds(it * 2 + p, 1), :],
                                           start=(p == 0), stop=(p == 1))
                        if l == 0:
                            mm = pe.matmul(ps[:, 2 + m % 2, 0:CTX], Yc[:, m * P:(m + 1) * P], selcT[:, bass.ds(it, 1), :],
                                           start=True, stop=True)
                        mm.then_inc(s.sc_mm, 1)
                state.n += 1
                for slot in range(RING):
                    state.uses[slot] += NE * 12 // RING

            pe.wait_ge(s.resid, RES_GDN)
            norm_sums(1, MSETS[0])
            route(0)
            experts(0)

            def ssd_scalars():
                pe.wait_ge(s.h_ready, 48)
                w = [take(("stail", 0)), take(("stail", 1))]
                for t in range(NT):
                    for k in range(KD):
                        mm = pe.matmul(ps[:, 2, 64 * t:64 * t + 64], hT[:, k, t * P:(t + 1) * P], w[k // 4][:, k % 4, :],
                                       start=(k == 0), stop=(k == KD - 1))
                mm.then_inc(s.w_used, 2)
                pe.wait_ge(s.st_a, 1)
                for t in range(NT):
                    for d in range(2):
                        o = slice(64 * t + 32 * d, 64 * t + 32 * d + 32)
                        pe.matmul(ps[:, 3, o], cum[:, d, :], s_a[:, t, 32 * d:32 * d + 32], start=True, stop=True)
                        mm = pe.matmul(ps[:, 4, o], ones, s_a[:, t, 32 * d:32 * d + 32], start=True, stop=True)
                mm.then_inc(s.sa_mm, 1)
                for t in range(XT0, NT):
                    for d in range(2):
                        mm = pe.matmul(ps[32 * d:32 * d + 32, 5, (t - XT0) * P:(t - XT0 + 1) * P], s_a[:, t, 32 * d:32 * d + 32],
                                       cum[:, d, :], start=True, stop=True)
                mm.then_inc(s.sr_mm, 1)

            def ssd_group(g):
                for i in range(4):
                    if i != 1:
                        w = take((("sx", g), None, ("sb", g), ("sc", g))[i])
                    if i >= 2:
                        pe.wait_ge(s.sp_pre, TILES * g + AFTER[i - 2])
                    elif g:
                        pe.wait_ge(s.sy_out, 2 * g)
                    else:
                        pe.wait_ge(s.sr_rows, 2)
                    m = i if i == 1 else 0
                    for j, (c0, nn, _) in enumerate((XSET, CSET) if i < 3 else (XSET,)):
                        for k in range(KD):
                            mm = pe.matmul(ps[:, 2 * (i % 2) + j, 0:nn], w[:, k, m * P:(m + 1) * P], hT[:, k, c0:c0 + nn],
                                           start=(k == 0), stop=(k == KD - 1))
                    mm.then_inc(s.w_used if i else s.sp_mm, 1)
                pe.wait_ge(s.sp_act, TILES * g + 6)
                for t in range(NT):
                    if t >= 4:
                        pe.wait_ge(s.str_out, NT * g + t - 3)
                    c = slice(t * P, (t + 1) * P)
                    pe.transpose(ps[:, 4 + t % 4, 0:P], s_xT[:, 0, c], ident)
                    pe.transpose(ps[:, 4 + t % 4, P:2 * P], s_xT[:, 1, c], ident)
                    mm = pe.transpose(ps[:, 4 + t % 4, 2 * P:3 * P], s_B[:, c], ident)
                    mm.then_inc(s.str_mm, 1)
                pe.wait_ge(s.sp_act, TILES * g + 7)
                pe.wait_ge(s.str_out, NT * (g + 1))
                pe.wait_ge(s.s_sel, g + 1)
                for st in range(6):
                    tile = [CHUNK_OF[d][st] for d in range(2)]
                    nx, ns = 4 * g + st - 2, 5 * g + st
                    cx = [slice((t - XT0) * P, (t - XT0 + 1) * P) for t in tile]
                    cs = [slice(t * P, (t + 1) * P) for t in tile]
                    if st >= 2:
                        for d in range(2):
                            pe.wait_ge(s.s_state, 2 * (ns - 1) + d + 1)
                            if st > 2:
                                pe.wait_ge(s.s_yacc, 2 * (nx - 1) + d + 1)
                            for r in range(SR):
                                pe.matmul(ps[:, 4 * d, r * P:(r + 1) * P], s_sel[32 * d:32 * d + 32, r, :],
                                          s_rows[32 * d:32 * d + 32, cx[d]], start=True, stop=True)
                            mm = pe.matmul(ps[:, 4 * d + 1, 0:P], s_B[:, cs[d]], s_C[:, cx[d]], start=True, stop=True)
                            mm.then_inc(s.s_in, 1)
                        for d in range(2):
                            pe.wait_ge(s.s_w, 2 * nx + d + 1)
                            for r in range(SR):
                                pe.matmul(ps[:, 4 * d + 2, r * SP_:(r + 1) * SP_], s_D[d][:, r, :], s_xdt[d][:, r, :], start=True, stop=True)
                            mm = pe.matmul(ps[:, 4 * d + 3, 0:SR * SP_], s_C[:, cx[d]], s_h[:, d, :], start=True, stop=True)
                            mm.then_inc(s.s_y, 1)
                    if st < 5:
                        for d in range(2):
                            pe.wait_ge(s.s_xend, 2 * ns + d + 1)
                            if st:
                                pe.wait_ge(s.s_state, 2 * (ns - 1) + d + 1)
                            mm = pe.matmul(ps[:, 4 * d + 1, 256:512], s_Btok[:, tile[d], :], s_xe[d].rearrange("p a b -> p (a b)"),
                                           start=True, stop=True)
                            mm.then_inc(s.s_st, 1)
                pe.wait_ge(s.s_yacc, 8 * (g + 1))
                for i in range(2):
                    for t in range(NT - XT0):
                        mm = pe.transpose(ps[:, 4 * i, t * P:(t + 1) * P], s_yt[:, t, i * P:(i + 1) * P], ident)
                    mm.then_inc(s.sy_mm, 1)

            def ssd_out():
                pe.wait_ge(s.sy_out, 2 * SG)

                def sums(i):
                    pe.wait_ge(s.sz_sq, i + 1)
                    mm = pe.matmul(ps[:, 7, :], ones, z_sq[i % 2], start=(i == 0), stop=(i == 15))
                    mm.then_inc(s.sz_sum, 1)

                for i in range(16):
                    if i % 2 == 0:
                        w = take(("sz", i // 2))
                    if i >= 4:
                        pe.wait_ge(s.sz_act, i - 3)
                    for k in range(KD):
                        mm = pe.matmul(ps[:, i % 4, :], w[:, k, (i % 2) * P:(i % 2 + 1) * P], hT[:, k, CTX:N],
                                       start=(k == 0), stop=(k == KD - 1))
                    mm.then_inc(s.w_used if i % 2 else s.sz_mm, 1)
                    if i >= 2:
                        sums(i - 2)
                sums(14)
                sums(15)
                pe.wait_ge(s.sz_n, 16)
                for m in range(KD):
                    w = take(("sout", m))
                    if m >= 2:
                        pe.wait_ge(s.resid, RES_GDN + m - 1)
                    for k in range(16):
                        mm = pe.matmul(ps[:, m % 2, :], w[:, k, :], yT[:, k, :], start=(k == 0), stop=(k == 15))
                    mm.then_inc(s.w_used, 1)

            pe.wait_ge(s.sc_free, 34)
            norm_sums(2, (XSET, CSET))
            ssd_scalars()
            for g in range(SG):
                ssd_group(g)
            ssd_out()
            pe.wait_ge(s.resid, RES_SSD)
            norm_sums(3, MSETS[1])
            route(1)
            experts(1)

            def project2(w, banks, n=P):
                for i, bank in enumerate(banks):
                    for k in range(KD):
                        mm = pe.matmul(ps[:, bank, :], w[:, k, i * P:(i + 1) * P], h2[:, k, :], start=(k == 0), stop=(k == KD - 1))
                return mm

            def values():
                for n in range(3):
                    w = take(("bv", n))
                    nn = (P, P, 3 * NH)[n]
                    for t in range(4):
                        for k in range(KD):
                            mm = pe.matmul(ps[:, n, t * nn:(t + 1) * nn], h2[:, k, t * P:(t + 1) * P], w[:, k, :],
                                           start=(k == 0), stop=(k == KD - 1))
                    mm.then_inc(s.w_used, 1)

            def queries_keys():
                pe.wait_ge(s.bv_out, 3)
                for n in range(2):
                    w = take(("bq", n))
                    for j in range(4):
                        for k in range(4):
                            mm = pe.matmul(ps[:, j, :], w[:, k, j * P:(j + 1) * P], h2[:, 4 * n + k, :], start=(n == 0 and k == 0), stop=(n == 1 and k == 3))
                    mm.then_inc(s.w_used, 1)
                for n in range(4):
                    project2(take(("bk", n)), [4 + n]).then_inc(s.w_used, 1)
                for i in range(6):
                    pe.wait_ge(s.bq_sq, i + 1)
                    if i >= 2:
                        pe.wait_ge(s.bq_rt, i - 1)
                    pe.matmul(ps[:, i % 2, :], ones64, bsq[i % 2], start=True, stop=True).then_inc(s.bq_sum, 1)

            def compress():
                pe.wait_ge(s.bc_vec, 2)
                pe.wait_ge(s.bq_rt, 6)
                for which in range(2):
                    x = (kC, vC)[which].rearrange("p (b i) -> p b i", i=CMPB)
                    for n in range(4):
                        w = take(("c1", which, n))
                        for kv in range(2):
                            r = slice(HD * kv, HD * kv + HD)
                            for fc in range(2):
                                for i in range(8):
                                    mm = pe.matmul(ps[:, 4 * which + 2 * fc + kv, 0:NCMP], w[r, i, fc * P:(fc + 1) * P], x[r, :, 8 * n + i],
                                                   start=(n == 0 and i == 0), stop=(n == 3 and i == 7))
                        mm.then_inc(s.w_used, 1)
                w = take(("c2",))
                pe.wait_ge(s.bc_act, 8)
                for kv in range(2):
                    for fc in range(2):
                        pe.matmul(ps[HD * kv:HD * kv + HD, 0, 0:NCMP], w[:, fc, :], hidc[:, 0, 2 * fc + kv, :], start=(fc == 0), stop=(fc == 1))
                for kv in range(2):
                    for fc in range(2):
                        mm = pe.matmul(ps[0:NCMP, 1, HD * kv:HD * kv + HD], hidc[:, 1, 2 * fc + kv, :], w[:, 2 + fc, :], start=(fc == 0), stop=(fc == 1))
                mm.then_inc(s.w_used, 1)
                pe.wait_ge(s.bc_act, 11)
                pe.matmul(ps[:, 2, 0:NCMP], ones64, bsq[0][:, 0:NCMP], start=True, stop=True).then_inc(s.bc_sum, 1)

            def attention():
                pe.wait_ge(s.bc_vec, 3)
                pe.wait_ge(s.bq_n, 6)
                pe.wait_ge(s.bc_act, 10)

                def job(n):
                    u, b = n // 3, n % 3
                    qt, h = u // NH, u % NH
                    return u, b, qt, h, slice(HD * (h // 4), HD * (h // 4) + HD)

                for n in range(96 + 2):
                    if n < 96:
                        u, b, qt, h, r = job(n)
                        if n >= 2:
                            pe.wait_ge(s.at_e, n - 1)
                        key = (kS, kW, kcm)[b]
                        nk = NCMP if b == 2 else (qt + 1) * P
                        pe.matmul(ps[:, n % 2, 0:nk], qT[r, h % 4, qt * P:(qt + 1) * P], key[r, 0:nk], start=True, stop=True).then_inc(s.at_s, 1)
                    if 1 <= n <= 96:
                        u, b, qt, h, r = job(n - 1)
                        j = (n - 1) % 2
                        pe.wait_ge(s.at_e, n)
                        if n >= 3:
                            pe.wait_ge(s.at_c, n - 2)
                        if b == 2:
                            mm = pe.transpose(ps[0:NCMP, 2 + j, 0:P], Pb[j][:, 0:NCMP], ident)
                        else:
                            for kb in range(qt + 1):
                                mm = pe.transpose(ps[:, 2 + j, kb * P:(kb + 1) * P], Pb[j][:, kb * P:(kb + 1) * P], ident)
                        mm.then_inc(s.at_t, 1)
                    if n >= 2:
                        u, b, qt, h, r = job(n - 2)
                        j = n % 2
                        pe.wait_ge(s.at_c, n - 1)
                        if b == 0 and u >= 2:
                            pe.wait_ge(s.at_o, u - 1)
                        o = ps[:, 4 + u % 2, HD * b:HD * b + HD]
                        if b == 2:
                            mm = pe.matmul(o, PTb[j][0:NCMP, 0:P], vcm[0:NCMP, r], start=True, stop=True)
                        else:
                            for kb in range(qt + 1):
                                mm = pe.matmul(o, PTb[j][:, kb * P:(kb + 1) * P], vS[:, b, kb, r], start=(kb == 0), stop=(kb == qt))
                        mm.then_inc(s.at_v, 1)
                pe.wait_ge(s.at_o, 32)
                for c in range(4):
                    for t in range(4):
                        mm = pe.transpose(ps[:, c, t * P:(t + 1) * P], oTok[:, t, c * P:(c + 1) * P], ident)
                    mm.then_inc(s.ao_mm, 1)

            def s5():
                pe.wait_ge(s.ao_copy, 4)
                for n in range(2):
                    project2(take(("bu", n)), [2 * n, 2 * n + 1]).then_inc(s.w_used, 1)
                pe.wait_ge(s.s5_u, 4)
                pe.wait_ge(s.s5_ang, 3)
                for st in range(NST + 1):
                    if st < NST:
                        q = slice(32 * (st % 4), 32 * (st % 4) + 32)
                        if st >= 2:
                            pe.wait_ge(s.s5_w, st - 1)
                        for x in range(2):
                            mm = pe.matmul(ps[:, 2 * (st % 2) + x, :], Bbd[q, x, st // 4, :], uT[q, st // 4, :], start=True, stop=True)
                        mm.then_inc(s.s5_b, 1)
                    if st >= 1:
                        j = st - 1
                        q = slice(32 * (j % 4), 32 * (j % 4) + 32)
                        pe.wait_ge(s.s5_x, 2 * j + 2)
                        if j % 4 == 0 and j >= 8:
                            pe.wait_ge(s.s5_yd, j // 4 - 1)
                        o = ps[q, 4 + (j // 4) % 2, :]
                        pe.matmul(o, Cbd[:, 0, j, :], S5.xr, start=True, stop=False)
                        pe.matmul(o, Cbd[:, 1, j, :], S5.xi, start=False, stop=True).then_inc(s.s5_y, 1)

            def conv2():
                pe.wait_ge(s.s5_yd, 4)
                for n in range(2):
                    w = [take((x, n)) for x in ("cc", "cx", "cb")]
                    for m in range(2):
                        i = 2 * n + m
                        if i >= 2:
                            pe.wait_ge(s.cv_out, i - 1)
                        for x in range(3):
                            for k in range(KD):
                                mm = pe.matmul(ps[:, 3 * (i % 2) + x, :], w[x][:, k, m * P:(m + 1) * P], h2[:, k, :], start=(k == 0), stop=(k == KD - 1))
                        if m == 1:
                            mm.then_inc(s.w_used, 3)
                        else:
                            mm.then_inc(s.cv_mm, 1)

            def mix():
                pe.wait_ge(s.cv_out, 4)
                pe.wait_ge(s.s5_gelu, 4)
                for m in range(KD):
                    if m:
                        pe.wait_ge(s.mg_mix, m)
                    for i in range(3):
                        project2(take(("mg", i, m)), [i]).then_inc(s.w_used, 1)
                    w = take(("glu", m))
                    for x in range(2):
                        for k in range(4):
                            mm = pe.matmul(ps[:, 3 + x, :], w[:, 4 * x + k, :], yg[:, k, :], start=(k == 0), stop=(k == 3))
                    mm.then_inc(s.w_used, 1)
                    for x, (kind, src) in enumerate((("cvo", ycv), ("nso", oA))):
                        w = take((kind, m))
                        for k in range(4):
                            mm = pe.matmul(ps[:, 5 + x, :], w[:, k, :], src[:, k, :], start=(k == 0), stop=(k == 3))
                        mm.then_inc(s.w_used, 1)
                pe.wait_ge(s.mg_mix, KD)
                for n in range(4):
                    w = take(("wo", n))
                    for x in range(2):
                        m = 2 * n + x
                        if m >= 2:
                            pe.wait_ge(s.resid, RES_SSD + m - 1)
                        for k in range(KD):
                            mm = pe.matmul(ps[:, m % 2, :], w[:, k, x * P:(x + 1) * P], mixed[:, k, :], start=(k == 0), stop=(k == KD - 1))
                        mm.then_inc(s.w_used if x else s.wo_mm, 1)

            def ffn():
                pe.wait_ge(s.nstt, 80)
                for n in range(FF2 // CW):
                    wg, wu = take(("fg", n)), take(("fu", n))
                    for x in range(2):
                        i = 2 * n + x
                        if i >= 2:
                            pe.wait_ge(s.ff_hid, i - 1)
                        for b, w in enumerate((wg, wu)):
                            for k in range(KD):
                                mm = pe.matmul(ps[:, 2 * (i % 2) + b, :], w[:, k, x * P:(x + 1) * P], h2[:, k, :], start=(k == 0), stop=(k == KD - 1))
                        if x:
                            mm.then_inc(s.w_used, 2)
                        else:
                            mm.then_inc(s.ff_mm, 1)
                pe.wait_ge(s.ff_hid, FF2 // P)
                for m in range(KD):
                    if m >= 2:
                        pe.wait_ge(s.resid, RES_SSD + KD + m - 1)
                    for half in range(2):
                        w = take(("fd", m, half))
                        for k in range(11):
                            mm = pe.matmul(ps[:, 4 + m % 2, :], w[:, k, :], fhid[:, 11 * half + k, :], start=(half == 0 and k == 0), stop=(half == 1 and k == 10))
                        mm.then_inc(s.w_used, 1)

            pe.wait_ge(s.sc_free, 68)
            norm_sums(4, (XSET,))
            norm_sums(5, (XSET,))
            pe.wait_ge(s.nstt, 72)
            pe.wait_ge(s.mask_done, MASKS + 8)
            values()
            queries_keys()
            compress()
            attention()
            s5()
            conv2()
            mix()
            pe.wait_ge(s.resid, RES_SSD + KD)
            norm_sums(6, (XSET,))
            ffn()

        @block.scalar
        def _(act):
            a = Lane(act, s.act_steps)

            def norm(call, sets, layer=None, which=None):
                for k in range(KD):
                    if k >= 4 or call:
                        act.wait_ge(s.nsq_sum, KD * call + k - 3)
                    c0, c1 = min(x[0] for x in sets), max(x[0] + x[1] for x in sets)
                    a.do(act.activation(nsqb[k % 4][:, c0:c1], RT[:, k, c0:c1], ACT.Square), s.nsq)
                act.wait_ge(s.nsq_sum, KD * call + KD)
                for j, (c0, nn, _) in enumerate(sets):
                    a.do(act.activation(nrtb[:, c0:c0 + nn], ps[:, j, 0:nn], ACT.Sqrt, bias=epsc, scale=1.0 / D), s.nrt)
                if layer is None:
                    return
                for k in range(KD):
                    for j, (c0, nn, v) in enumerate(sets):
                        act.wait_ge(s.nstt, nstt0[call] + len(sets) * k + j + 1)
                        x = hT[:, k, c0:c0 + nn]
                        sh = ada[:, layer, 24 * which + k, v:v + 1]
                        a.do(act.activation(x, x, ACT.Identity, bias=sh), s.h_ready)

            act.wait_ge(s.const_in, 32)
            a.do(act.activation(cact.rearrange("p a b -> p (a b)"), col("cvec", 0, 16), ACT.Silu), s.cv_done)
            act.wait_ge(s.mask_done, 3)
            norm(0, (XSET, CSET), 0, 0)

            act.wait_ge(s.gt_bias, 1)
            a.do(act.activation(ea, col("galog", 0, 16), ACT.Exp))
            a.do(act.activation(beta, betag[:, :, 0:16], ACT.Sigmoid))
            a.do(act.activation(gtmp, betag[:, :, 16:32], ACT.Abs))
            a.settle()
            a.do(act.activation(gtmp, gtmp, ACT.Exp, scale=-1.0))
            a.settle()
            a.do(act.activation(gtmp, gtmp, ACT.Ln, bias=onec), s.gt_sp)
            act.wait_ge(s.gc_cols, 1)
            a.do(act.activation(beg, gcum, ACT.Exp), s.gt_e)
            act.wait_ge(s.gr_mm, 1)
            for q in range(4):
                a.do(act.activation(rows[32 * q:32 * q + GH, 0:512], ps[32 * q:32 * q + GH, 3, :], ACT.Copy), s.gr_rows)
                a.do(act.activation(rows[32 * q:32 * q + GH, 512:768], ps[32 * q:32 * q + GH, 4, 0:256], ACT.Copy), s.gr_rows)

            def project(hg):
                for i in range(14):
                    if i < 12:
                        if i % 2:
                            act.wait_ge(s.w_used, USED[("gin", i // 4, hg, (i // 2) % 2)])
                        else:
                            act.wait_ge(s.gp_mm, 6 * hg + i // 2 + 1)
                        if i >= 2:
                            act.wait_ge(s.gp_conv, 12 * hg + i - 1)
                        p = pre[i % 2]
                        a.do(act.activation(p[:, 1 + CTX + 1:1 + CTX + 1 + SEQ], ps[:, 2 * (i % 2), :], ACT.Copy), s.gp_pre)
                        a.do(act.activation(p[:, 1:1 + CTX], ps[:, 2 * (i % 2) + 1, 0:CTX], ACT.Copy), s.gp_pre)
                    if 1 <= i < 13:
                        t = i - 1
                        dst = qkv[t // 4][:, t % 4, :]
                        act.wait_ge(s.gp_conv, 12 * hg + t + 1)
                        a.do(act.activation(dst[:, 0:CTX], cv[t % 3][:, 0:CTX], ACT.Silu), s.gp_act)
                        a.do(act.activation(dst[:, CTX:N], cv[t % 3][:, CTX + 1:N + 1], ACT.Silu), s.gp_act)
                        if t < 8:
                            if t >= 2:
                                act.wait_ge(s.gp_sum, 8 * hg + t - 1)
                            a.settle()
                            a.do(act.activation(sq[t % 2], dst, ACT.Square), s.gp_sq)
                    if 2 <= i < 10:
                        t = i - 2
                        act.wait_ge(s.gp_sum, 8 * hg + t + 1)
                        if t >= 2:
                            act.wait_ge(s.gp_norm, 8 * hg + t - 1)
                        b = 4 + 2 * (t % 2)
                        a.do(act.activation(rt[t % 2][:, CTX:N], ps[:, b, :], ACT.Sqrt, bias=epsc), s.gp_rt)
                        a.do(act.activation(rt[t % 2][:, 0:CTX], ps[:, b + 1, 0:CTX], ACT.Sqrt, bias=epsc), s.gp_rt)

            def recurrence(hg):
                for st in range(6):
                    n = hg * 6 + st
                    tile = [CHUNK_OF[d][st] for d in range(2)]
                    for d in range(2):
                        z = sets[d]
                        act.wait_ge(s.r_dm, 2 * n + d + 1)
                        a.do(act.activation(z.EB.rearrange("p a b -> p (a b)"), ps[:, 4 * d, :], ACT.Exp))
                        for j in range(HG):
                            i = 8 * d + hg * HG + j
                            a.do(act.activation(z.D[:, j, :], z.D[:, j, :], ACT.Exp, bias=ngc[:, tile[d], i:i + 1]),
                                 s.r_d if j == HG - 1 else None)
                    for d in range(2):
                        z = sets[d]
                        act.wait_ge(s.r_w, 2 * n + d + 1)
                        a.do(act.activation(z.D.rearrange("p a b -> p (a b)"), ps[:, 4 * d + 2, :], ACT.Copy, scale=-1.0), s.r_nw)
                    for d in range(2):
                        z = sets[d]
                        act.wait_ge(s.r_vn, 2 * n + d + 1)
                        a.do(act.activation(z.XT.rearrange("p a b -> p (a b)"), ps[:, 4 * d + 3, :], ACT.Copy), s.r_vnc)

            def gdn_out(hg):
                act.wait_ge(s.r_state, 12 * hg + 12)
                for j in range(HG):
                    i = hg * HG + j
                    if j >= 2:
                        act.wait_ge(s.go_sum, i - 1)
                    a.do(act.activation(sq[j % 2], oT[:, j, :], ACT.Square), s.go_sq)
                    act.wait_ge(s.go_sum, i + 1)
                    if j >= 2:
                        act.wait_ge(s.go_n, i - 1)
                    for b, (c0, nn, _) in enumerate((XSET, CSET)):
                        a.do(act.activation(rt[j % 2][:, c0:c0 + nn], ps[:, b, 0:nn], ACT.Sqrt, bias=epsc, scale=1.0 / P), s.go_rt)
                    if j % 2:
                        act.wait_ge(s.w_used, USED[("gz", hg, j // 2)])
                    else:
                        act.wait_ge(s.go_z, i // 2 + 1)
                    if j >= 2:
                        act.wait_ge(s.go_o, i - 1)
                    for b, (c0, nn, _) in enumerate((XSET, CSET)):
                        a.do(act.activation(pre[j % 2][:, c0:c0 + nn], ps[:, 2 + b + 2 * (j % 2), 0:nn], ACT.Silu), s.go_sz)

            for hg in range(GH // HG):
                project(hg)
                recurrence(hg)
                gdn_out(hg)

            def route(l):
                tiles = list(range(XT0 if l else 0, NT))
                act.wait_ge(s.sm_sub, l + 1)
                x = aff[:, tiles[0]:NT, :]
                a.do(act.activation(x, x, ACT.Exp), s.sm_exp)
                for i, (t, half) in enumerate([(t, half) for t in tiles for half in range(2)]):
                    act.wait_ge(s.ht_mm, 12 * l + i + 1)
                    a.do(act.activation(htok[:, t, 512 * half:512 * half + 512], ps[:, 6 + i % 2, :], ACT.Copy), s.ht_copied)
                ns = (SLOTS, CAPX)[l]
                xs = xsT[:, 0:KD * NE * ns].rearrange("p (k e c) -> p k e c", k=KD, c=ns)
                i = (0, 24)[l]
                for m in range(KD):
                    for b in range(3 if l == 0 else 2):
                        act.wait_ge(s.ga_mm, i + 1)
                        bank = ps[:, (i - (0, 24)[l]) % 4, :]
                        if b < 2:
                            a.do(act.activation(xs[:, m, 8 * b:8 * b + 8, 0:CAPX], bank.rearrange("p (e c) -> p e c", c=CAPX), ACT.Copy), s.ga_copied)
                        else:
                            a.do(act.activation(xs[:, m, :, CAPX:ns], bank.rearrange("p (e c) -> p e c", c=CAPC), ACT.Copy), s.ga_copied)
                        i += 1
                for i in range(8 + (4 if l == 0 else 0)):
                    act.wait_ge(s.st_mm, (0, 12)[l] + i + 1)
                    if i < 8:
                        a.do(act.activation(selxT[:, i, :], ps[:, 6 + i % 2, :], ACT.Copy), s.st_copied)
                    else:
                        a.do(act.activation(selcT[:, i - 8, :], ps[:, 6 + i % 2, 0:CTX], ACT.Copy), s.st_copied)

            def experts(l):
                ns = (SLOTS, CAPX)[l]
                with act.Fori(0, NE // EB) as it:
                    for j in range(EB):
                        for c in range(4):
                            act.wait_ge(s.w_used, it * (12 * EB) + (MOE0[l] + 12 * j + 2 * c + 1))
                            act.wait_ge(s.gu_free, it * (4 * EB) + (4 * j + c + 1 + l * 66))
                            act.activation(sg[c % 2][:, 0:2 * ns], ps[:, c % 2, 0:2 * ns], ACT.Silu).then_inc(s.sg_ready, 1)
                        act.wait_ge(s.w_used, it * (12 * EB) + (MOE0[l] + 12 * j + 12))
                        act.wait_ge(s.sc_free, it * KD + (2 + l * 34))
                        y = ps[:, 4 + 2 * (j % 2):6 + 2 * (j % 2), :].rearrange("p a b -> p (a b)")
                        if l == 0:
                            act.activation(Yc[CAPC * j:CAPC * j + CAPC, :], y[CAPX:SLOTS, :], ACT.Copy)
                        act.activation(Yx[CAPX * (j % 2):CAPX * (j % 2) + CAPX, j // 2, :], y[0:CAPX, :], ACT.Copy).then_inc(s.y_free, 1)

            act.wait_ge(s.resid, RES_GDN)
            norm(1, MSETS[0], 0, 1)
            route(0)
            experts(0)

            def ssd_scalars():
                act.wait_ge(s.st_bias, 1)
                a.do(act.activation(s_A, col("salog", 0, 2 * SH), ACT.Exp))
                a.do(act.activation(s_tmp, s_dt, ACT.Abs))
                a.settle()
                a.do(act.activation(s_tmp, s_tmp, ACT.Exp, scale=-1.0))
                a.settle()
                a.do(act.activation(s_tmp, s_tmp, ACT.Ln, bias=onec), s.st_sp)
                act.wait_ge(s.sa_cols, 1)
                a.do(act.activation(s_te, s_te, ACT.Exp), s.sa_e)
                a.do(act.activation(s_etot, s_etot, ACT.Exp), s.sa_e)
                a.do(act.activation(s_tmp, s_a, ACT.Exp, scale=-1.0), s.sa_e)
                act.wait_ge(s.sr_mm, 1)
                for d in range(2):
                    a.do(act.activation(s_rows[32 * d:32 * d + 32, :], ps[32 * d:32 * d + 32, 5, :], ACT.Copy), s.sr_rows)

            def ssd_group(g):
                dst = [s_xT[:, 0, :], s_xT[:, 1, :], s_B, None]
                for i in range(5):
                    if i < 4:
                        if i == 0:
                            act.wait_ge(s.sp_mm, g + 1)
                        else:
                            act.wait_ge(s.w_used, USED[(("sx", g), ("sx", g), ("sb", g), ("sc", g))[i]])
                        if i >= 2 or g:
                            act.wait_ge(s.sp_conv, 4 * g + i - 1)
                        p = s_pre[i % 2]
                        a.do(act.activation(p[:, CTX + 2:N + 2], ps[:, 2 * (i % 2), :], ACT.Copy), s.sp_pre)
                        if i < 3:
                            a.do(act.activation(p[:, 1:CTX + 1], ps[:, 2 * (i % 2) + 1, 0:CTX], ACT.Copy), s.sp_pre)
                    if i >= 1:
                        j = i - 1
                        b = col("sconvb", (2 * g, 2 * g + 1, 16 + g, 24 + g)[j])
                        act.wait_ge(s.sp_conv, 4 * g + j + 1)
                        if j < 3:
                            a.do(act.activation(dst[j][:, 0:CTX], s_cv[j % 2][:, 0:CTX], ACT.Silu, bias=b), s.sp_act)
                            a.do(act.activation(dst[j][:, CTX:N], s_cv[j % 2][:, CTX + 1:N + 1], ACT.Silu, bias=b), s.sp_act)
                        else:
                            a.do(act.activation(s_C, s_cv[j % 2][:, CTX + 1:N + 1], ACT.Silu, bias=b), s.sp_act)
                for t in range(NT):
                    act.wait_ge(s.str_mm, NT * g + t + 1)
                    a.do(act.activation(s_xtok[:, t, :], ps[:, 4 + t % 4, 0:2 * P], ACT.Copy))
                    a.do(act.activation(s_Btok[:, t, :], ps[:, 4 + t % 4, 2 * P:3 * P], ACT.Copy), s.str_out)
                for st in range(2, 6):
                    nx = 4 * g + st - 2
                    for d in range(2):
                        act.wait_ge(s.s_dm, 2 * nx + d + 1)
                        for r in range(SR):
                            h = 32 * d + SR * g + r
                            x = s_D[d][:, r, :]
                            a.do(act.activation(x, x, ACT.Exp, bias=s_a[:, CHUNK_OF[d][st], h:h + 1]), s.s_d if r == SR - 1 else None)

            def ssd_out():
                for i in range(17):
                    if i < 16:
                        if i % 2:
                            act.wait_ge(s.w_used, USED[("sz", i // 2)])
                        else:
                            act.wait_ge(s.sz_mm, i // 2 + 1)
                        if i >= 2:
                            act.wait_ge(s.sz_u, i - 1)
                        a.do(act.activation(z_act[i % 2], ps[:, i % 4, :], ACT.Silu), s.sz_act)
                    if i >= 1:
                        j = i - 1
                        act.wait_ge(s.sz_u, j + 1)
                        if j >= 2:
                            act.wait_ge(s.sz_sum, j - 1)
                        a.do(act.activation(z_sq[j % 2], yT[:, j, :], ACT.Square), s.sz_sq)
                        a.do(act.activation(yT[:, j, :], yT[:, j, :], ACT.Copy, scale=col("snorm", j)), s.sz_n)
                act.wait_ge(s.sz_sum, 16)
                a.do(act.activation(z_rt, ps[:, 7, :], ACT.Sqrt, bias=epsc, scale=1.0 / SI), s.sz_rt)

            act.wait_ge(s.sc_free, 34)
            norm(2, (XSET, CSET), 1, 0)
            ssd_scalars()
            for g in range(SG):
                ssd_group(g)
            ssd_out()
            act.wait_ge(s.resid, RES_SSD)
            norm(3, MSETS[1], 1, 1)
            route(1)
            experts(1)

            def values():
                for n in range(3):
                    act.wait_ge(s.w_used, USED[("bv", n)])
                    if n < 2:
                        a.do(act.activation(vS[:, n, :, :].rearrange("p a b -> p (a b)"), ps[:, n, :], ACT.Copy), s.bv_out)
                    else:
                        a.do(act.activation(ng.rearrange("p a b -> p (a b)"), ps[:, n, 0:4 * 3 * NH], ACT.Sigmoid), s.bv_out)

            def queries_keys():
                dst = [qT[:, j, :] for j in range(4)] + [kS, kW, kC, vC]
                for i in range(8):
                    act.wait_ge(s.w_used, USED[("bq", 1) if i < 4 else ("bk", i - 4)])
                    a.do(act.activation(dst[i], ps[:, i, :], ACT.Copy), s.bq_copy)
                for i in range(6):
                    if i >= 2:
                        act.wait_ge(s.bq_sum, i - 1)
                    else:
                        a.settle()
                    a.do(act.activation(bsq[i % 2], dst[i], ACT.Square), s.bq_sq)
                    act.wait_ge(s.bq_sum, i + 1)
                    if i >= 2:
                        act.wait_ge(s.bq_n, i - 1)
                    a.do(act.activation(brt[i % 2], ps[:, i % 2, :], ACT.Sqrt, bias=epsc, scale=1.0 / HD), s.bq_rt)

            def compress():
                for which in range(2):
                    act.wait_ge(s.w_used, USED[("c1", which, 3)])
                    for x in range(4):
                        a.do(act.activation(hidc[:, which, x, :], ps[:, 4 * which + x, 0:NCMP], ACT.Gelu_apprx_tanh), s.bc_act)
                act.wait_ge(s.w_used, USED[("c2",)])
                a.do(act.activation(kcm, ps[:, 0, 0:NCMP], ACT.Copy), s.bc_act)
                a.do(act.activation(vcm[0:NCMP, :], ps[0:NCMP, 1, 0:P], ACT.Copy), s.bc_act)
                a.settle()
                a.do(act.activation(bsq[0][:, 0:NCMP], kcm, ACT.Square), s.bc_act)
                act.wait_ge(s.bc_sum, 1)
                act.wait_ge(s.bq_n, 6)
                a.do(act.activation(brt[0][:, 0:NCMP], ps[:, 2, 0:NCMP], ACT.Sqrt, bias=epsc, scale=1.0 / HD), s.bc_act)

            def attention():
                for n in range(96 + 1):
                    if n < 96:
                        u, b = n // 3, n % 3
                        nk = NCMP if b == 2 else (u // NH + 1) * P
                        act.wait_ge(s.at_m, n + 1)
                        if n >= 2:
                            act.wait_ge(s.at_t, n - 1)
                        src = csc[u % 2] if b == 2 else ps[:, n % 2, 0:nk]
                        a.do(act.activation(Pb[n % 2][:, 0:nk], src, ACT.Exp, bias=anm[:, n:n + 1], accum_out=asum[:, n:n + 1]), s.at_e)
                    if n >= 1:
                        m = n - 1
                        u, b = m // 3, m % 3
                        nk = P if b == 2 else (u // NH + 1) * P
                        rows_ = slice(0, NCMP) if b == 2 else slice(0, P)
                        act.wait_ge(s.at_t, n)
                        if m >= 2:
                            act.wait_ge(s.at_v, m - 1)
                        a.do(act.activation(PTb[m % 2][rows_, 0:nk], ps[rows_, 2 + m % 2, 0:nk], ACT.Copy), s.at_c)
                for c in range(4):
                    act.wait_ge(s.ao_mm, c + 1)
                    a.do(act.activation(oA[:, c, :], ps[:, c, :], ACT.Copy), s.ao_copy)

            def s5_prepare():
                act.dma_start(braw, A["s5b"].rearrange("x p a b -> p x a b")).then_inc(s.router_in, 16)
                act.dma_start(craw, A["s5c"].rearrange("x p a b -> p x a b")).then_inc(s.router_in, 16)
                a.do(act.activation(dt5, col("logdt", 0, NST), ACT.Exp), s.s5_act)
                act.wait_ge(s.s5_ang, 1)
                a.do(act.activation(r5, t5, ACT.Exp), s.s5_act)
                act.wait_ge(s.s5_ang, 2)
                a.do(act.activation(sk, fk, ACT.Sin, scale=TURN), s.s5_act)
                a.do(act.activation(ck, fr, ACT.Sin, scale=TURN), s.s5_act)

            def s5():
                for t in range(4):
                    act.wait_ge(s.w_used, USED[("bu", t // 2)])
                    a.do(act.activation(uT[:, t, :], ps[:, t, :], ACT.Copy), s.s5_u)
                for t in range(4):
                    act.wait_ge(s.s5_yd, t + 1)
                    a.do(act.activation(yg[:, t, :], yg[:, t, :], ACT.Gelu_apprx_tanh), s.s5_gelu)

            def conv2():
                for i in range(4):
                    if i % 2:
                        act.wait_ge(s.w_used, USED[("cb", i // 2)])
                    else:
                        act.wait_ge(s.cv_mm, i // 2 + 1)
                    if i:
                        act.wait_ge(s.cv_out, i)
                    a.do(act.activation(ccs, ps[:, 3 * (i % 2), :], ACT.Copy), s.cv_cc)

            def mix():
                for m in range(KD):
                    for i, item in enumerate([("mg", 0, m), ("mg", 1, m), ("mg", 2, m), ("glu", m)]):
                        act.wait_ge(s.w_used, USED[item])
                        if m:
                            act.wait_ge(s.mg_mix, m)
                        a.do(act.activation(mact[i], ps[:, i if i < 3 else 4, :], ACT.Sigmoid), s.mg_act)

            def ffn():
                for i in range(FF2 // P):
                    if i % 2:
                        act.wait_ge(s.w_used, USED[("fu", i // 2)])
                    else:
                        act.wait_ge(s.ff_mm, i // 2 + 1)
                    if i >= 2:
                        act.wait_ge(s.ff_hid, i - 1)
                    a.do(act.activation(fact[i % 2], ps[:, 2 * (i % 2), :], ACT.Silu), s.ff_act)

            act.wait_ge(s.sc_free, 68)
            norm(4, (XSET,))
            act.wait_ge(s.nstt, 64)
            norm(5, (XSET,))
            act.wait_ge(s.nstt, 72)
            s5_prepare()
            values()
            queries_keys()
            compress()
            attention()
            s5()
            conv2()
            mix()
            act.wait_ge(s.resid, RES_SSD + KD)
            norm(6, (XSET,))
            ffn()

        @block.vector
        def _(dve):
            v = Lane(dve, s.vec_steps)

            def ada_out(l, n):
                dve.wait_ge(s.w_used, USED[("ada", l, n)])
                for m in range(2):
                    i = 2 * n + m
                    ins = dve.tensor_scalar(ada[:, l, i, :], ps[:, 7, 2 * m:2 * m + 2], col("ada_b", 48 * l + i), None, ALU.add)
                    v.do(ins, s.ada_copied if m == 1 else None)

            def ada_gains(l):
                v.settle()
                for w, name in enumerate(("norm1", "norm2")):
                    for vec in range(2):
                        v.do(dve.scalar_tensor_tensor(out=gs1[:, l, w, :].rearrange("p (k v) -> p k v", v=2)[:, :, vec],
                                                      in0=ada[:, l, 24 * w + 8:24 * w + 16, vec], scalar=1.0,
                                                      in1=col(name, 8 * l, 8), op0=ALU.add, op1=ALU.mult))
                v.settle()

            def norm(call, sets, gain, dst):
                dve.wait_ge(s.nrt, nrt0[call] + len(sets))
                for j, (c0, nn, _) in enumerate(sets):
                    v.do(dve.reciprocal(nrsb[:, c0:c0 + nn], nrtb[:, c0:c0 + nn]))
                v.settle()
                for k in range(KD):
                    for j, (c0, nn, vec) in enumerate(sets):
                        v.do(dve.scalar_tensor_tensor(out=dst[:, k, c0:c0 + nn], in0=RT[:, k, c0:c0 + nn],
                                                      scalar=gain(k, vec), in1=nrsb[:, c0:c0 + nn],
                                                      op0=ALU.mult, op1=ALU.mult), s.nstt)

            dve.wait_ge(s.const_in, 32)
            for n in range(24):
                ada_out(0, n)
            ada_gains(0)
            norm(0, (XSET, CSET), lambda k, vec: gs1[:, 0, 0, 2 * k + vec:2 * k + vec + 1], hT)

            dve.wait_ge(s.w_used, USED[("gtail",)])
            v.do(dve.tensor_copy(betag[:, :, 0:16], ps[:, 6, 0:32 * NT].rearrange("p (t c) -> p t c", c=32)[:, :, 0:16]))
            v.do(dve.tensor_tensor(betag[:, :, 16:32], ps[:, 6, 0:32 * NT].rearrange("p (t c) -> p t c", c=32)[:, :, 16:32],
                                   col("gdtb", 0, 16).unsqueeze(1).to_broadcast([P, NT, 16]), ALU.add), s.gt_bias)
            dve.wait_ge(s.gt_sp, 1)
            v.settle()
            v.do(dve.scalar_tensor_tensor(out=gsp, in0=betag[:, :, 16:32], scalar=0.0, in1=gtmp, op0=ALU.max, op1=ALU.add))
            v.settle()
            v.do(dve.scalar_tensor_tensor(out=gsp, in0=gsp, scalar=-1.0, in1=ea.unsqueeze(1).to_broadcast([P, NT, 16]),
                                          op0=ALU.mult, op1=ALU.mult), s.gt_g)
            dve.wait_ge(s.gc_mm, 1)
            v.do(dve.tensor_copy(gcum, ps[:, 5, 0:16 * NT].rearrange("p (t c) -> p t c", c=16)), s.gc_cols)
            v.settle()
            v.do(dve.tensor_scalar(ngc, gcum, -1.0, None, ALU.mult))
            dve.wait_ge(s.gt_e, 1)
            v.do(dve.tensor_tensor(beg, beg, beta, ALU.mult))
            dve.wait_ge(s.mask_done, MASKS)
            dve.wait_ge(s.level_masks, 2 * LEVELS)
            for d in range(2):
                for l in range(LEVELS):
                    v.do(dve.tensor_reduce(rmask[:, d, l:l + 1], bmask[:, 1 - d, l, :], AX.X, ALU.max, negate=True))

            def project(hg):
                for p in pre:
                    for c in (0, CTX + 1, N + 2):
                        if hg == 1 and c == 0 and p is pre[0]:
                            dve.wait_ge(s.go_o, HG)
                        v.do(dve.memset(p[:, c:c + 1], 0.0))
                v.settle()
                for i in range(14):
                    if i < 12:
                        ch = (i // 4) * 8 + hg * HG + i % 4
                        dve.wait_ge(s.gp_pre, 2 * (12 * hg + i + 1))
                        if i >= 3:
                            dve.wait_ge(s.gp_act, 2 * (12 * hg + i - 2))
                        p, c = pre[i % 2], cv[i % 3]
                        w = [col("gconv", 3 * ch + t) for t in range(3)]
                        v.do(dve.tensor_scalar(c, p[:, 1:N + 2], w[1], None, ALU.mult))
                        v.settle()
                        v.do(dve.scalar_tensor_tensor(out=c, in0=p[:, 0:N + 1], scalar=w[0], in1=c, op0=ALU.mult, op1=ALU.add))
                        v.settle()
                        v.do(dve.scalar_tensor_tensor(out=c, in0=p[:, 2:N + 3], scalar=w[2], in1=c, op0=ALU.mult, op1=ALU.add), s.gp_conv)
                    if 2 <= i < 10:
                        t = i - 2
                        dve.wait_ge(s.gp_rt, 2 * (8 * hg + t + 1))
                        r = rt[t % 2]
                        dst = qkv[t // 4][:, t % 4, :]
                        v.do(dve.reciprocal(r, r))
                        v.settle()
                        scale = float(P) ** -0.5 if t < 4 else 1.0
                        v.do(dve.scalar_tensor_tensor(out=dst, in0=dst, scalar=scale, in1=r, op0=ALU.mult, op1=ALU.mult), s.gp_norm)

            def bc(colap, n=P):
                return colap.unsqueeze(2).to_broadcast([P, HG, n])

            def recurrence(hg):
                q, k_, vv = qkv
                dve.wait_ge(s.gp_act, 24 * hg + 24)
                v.do(dve.memset(oT, 0.0))
                for d in range(2):
                    v.do(dve.memset(S[d], 0.0))
                    v.do(dve.memset(sets[d].Y, 0.0))
                for st in range(6):
                    n = hg * 6 + st
                    tile = [CHUNK_OF[d][st] for d in range(2)]
                    cs = [slice(t * P, t * P + P) for t in tile]
                    for d in range(2):
                        z = sets[d]
                        dve.wait_ge(s.r_in, 2 * n + d + 1)
                        v.do(dve.tensor_tensor(z.D, ps[:, 4 * d, :].rearrange("p (j i) -> p j i", i=P),
                                               negm[:, d, :].unsqueeze(1).to_broadcast([P, HG, P]), ALU.add), s.r_dm)
                    for d in range(2):
                        z = sets[d]
                        last = P - 1 if d == 0 else 0
                        g3 = lambda b: ps[:, 4 * d + b, :].rearrange("p (j i) -> p j i", i=P)
                        dve.wait_ge(s.r_d, 2 * n + d + 1)
                        v.do(dve.tensor_tensor(z.A, g3(3), z.D, ALU.mult))
                        v.do(dve.tensor_tensor(z.XT, g3(2), z.D, ALU.mult))
                        v.do(dve.tensor_copy(kcol[:, d, :], z.D[:, :, last]))
                        v.do(dve.tensor_copy(el[:, d, :], z.EB[:, :, last]))
                        v.do(dve.tensor_copy(z.T, ident.unsqueeze(1).to_broadcast([P, HG, P])))
                        v.do(dve.tensor_copy(z.U, ident.unsqueeze(1).to_broadcast([P, HG, P])))
                        v.settle()
                        v.do(dve.tensor_tensor(z.XT, g3(1), z.XT, ALU.mult), s.r_xt)
                        v.do(dve.tensor_tensor(z.EB, q[:, :, cs[d]], z.EB, ALU.mult))
                    for l in range(LEVELS):
                        b = 1 << l

                        def half(x, odd):
                            return x.rearrange("p j (n two b) -> p (j n) two b", two=2, b=b)[:, :, odd, :]

                        def bank(d, i):
                            return ps[:, 4 * d + i, 0:64 * HG].rearrange("p (n b) -> p n b", b=b)

                        for d in range(2):
                            z = sets[d]
                            dve.wait_ge(s.r_y, 2 * (LEVELS * n + l) + d + 1)
                            y = z.Y.rearrange("p j (n two b) -> p j n two b", two=2, b=b)[:, :, :, d, :]
                            m = bmask[:, d, l, :].rearrange("p (n b) -> p n b", b=b).unsqueeze(1).to_broadcast([P, HG, 64 // b, b])
                            v.do(dve.tensor_tensor(y, ps[:, 4 * d, 0:64 * HG].rearrange("p (j n b) -> p j n b", j=HG, b=b), m, ALU.mult), s.r_ym)
                        for d in range(2):
                            z = sets[d]
                            dve.wait_ge(s.r_tu, 2 * (LEVELS * n + l) + d + 1)
                            if l < LEVELS - 1:
                                v.do(dve.tensor_tensor(half(z.T, d), half(z.T, d), bank(d, 1), ALU.subtract))
                            v.do(dve.scalar_tensor_tensor(out=half(z.U, 1 - d), in0=bank(d, 2), scalar=rmask[:, d, l:l + 1],
                                                          in1=half(z.U, 1 - d), op0=ALU.mult, op1=ALU.add), s.r_l)
                    for d in range(2):
                        z = sets[d]
                        i = 8 * d + hg * HG
                        g3 = lambda b: ps[:, 4 * d + b, :].rearrange("p (j i) -> p j i", i=P)
                        dve.wait_ge(s.r_kv, 2 * n + d + 1)
                        v.do(dve.tensor_tensor(z.XT, g3(0), bc(beg[:, tile[d], i:i + HG]), ALU.mult))
                        v.do(dve.tensor_tensor(z.Y, g3(0), bc(kcol[:, d, :]), ALU.mult))
                        v.do(dve.tensor_tensor(z.T, g3(1), bc(beta[:, tile[d], i:i + HG]), ALU.mult), s.r_kvs)
                    for x in range(2):
                        ada_out(1, hg * 12 + 2 * st + x)
                    for d in range(2):
                        z = sets[d]
                        g3 = lambda b: ps[:, 4 * d + b, :].rearrange("p (j i) -> p j i", i=P)
                        dve.wait_ge(s.r_o, 2 * n + d + 1)
                        v.settle()
                        v.do(dve.tensor_tensor(oT[:, :, cs[d]], oT[:, :, cs[d]], g3(0), ALU.add))
                        v.do(dve.tensor_tensor(S[d], S[d], bc(el[:, d, :]), ALU.mult))
                        v.settle()
                        v.do(dve.tensor_tensor(S[d], S[d], g3(1), ALU.add), s.r_state)

            def gdn_out(hg):
                for j in range(HG):
                    i = hg * HG + j
                    dve.wait_ge(s.go_rt, 2 * (i + 1))
                    r = rt[j % 2]
                    v.do(dve.reciprocal(r, r))
                    v.settle()
                    v.do(dve.scalar_tensor_tensor(out=oT[:, j, :], in0=oT[:, j, :], scalar=col("gnorm"), in1=r,
                                                  op0=ALU.mult, op1=ALU.mult), s.go_n)
                    v.settle()
                    dve.wait_ge(s.go_sz, 2 * (i + 1))
                    v.do(dve.tensor_tensor(oT[:, j, :], oT[:, j, :], pre[j % 2][:, 0:N], ALU.mult), s.go_o)
                for m in range(KD):
                    i = hg * KD + m
                    if m == KD - 1:
                        dve.wait_ge(s.w_used, USED[("gout", hg, 1)])
                    else:
                        dve.wait_ge(s.go_mm, (KD - 1) * hg + m + 1)
                    for b, (c0, nn, vec) in enumerate((XSET, CSET)):
                        x = RT[:, m, c0:c0 + nn]
                        v.do(dve.scalar_tensor_tensor(out=x, in0=ps[:, b + 2 * (m % 2), 0:nn], scalar=ada[:, 0, 16 + m, vec:vec + 1],
                                                      in1=x, op0=ALU.mult, op1=ALU.add), s.resid)

            for hg in range(GH // HG):
                project(hg)
                recurrence(hg)
                gdn_out(hg)
            ada_gains(1)

            def route(l):
                tiles = list(range(XT0 if l else 0, NT))
                t0, nt = tiles[0], len(tiles)
                x = aff[:, t0:NT, :]
                bcast = smx[:, t0:NT].unsqueeze(2).to_broadcast([P, nt, NE])
                lg = ps[:, 2, NE * t0:NE * NT].rearrange("p (t e) -> p t e", e=NE)
                dve.wait_ge(s.lg_mm, l + 1)
                v.do(dve.tensor_reduce(smx[:, t0:NT], lg, AX.X, ALU.max))
                v.settle()
                v.do(dve.tensor_tensor(x, lg, bcast, ALU.subtract), s.sm_sub)
                dve.wait_ge(s.sm_exp, l + 1)
                v.do(dve.tensor_reduce(smx[:, t0:NT], x, AX.X, ALU.add))
                v.settle()
                v.do(dve.reciprocal(smx[:, t0:NT], smx[:, t0:NT]))
                v.settle()
                v.do(dve.tensor_tensor(x, x, bcast, ALU.mult), s.aff_ready)
                dve.wait_ge(s.afft_mm, l + 1)
                for c0, nn, vec in MSETS[l]:
                    cap, bank = (CAPX, CAPC)[vec], 3 + vec
                    w, r = affT[0:NE, c0:c0 + nn], rank[0:NE, c0:c0 + nn]
                    v.do(dve.tensor_copy(w, ps[0:NE, bank, 0:nn]))
                    v.settle()
                    for _ in range(cap // 8):
                        v.do(dve.max(top8[0:NE, :], w))
                        v.settle()
                        v.do(dve.match_replace(w, top8[0:NE, :], w, -1.0))
                        v.settle()
                    v.do(dve.tensor_scalar(w, w, 0.0, None, ALU.is_lt))
                    v.settle()
                    v.do(dve.tensor_tensor_scan(r, ones[0:NE, 0:1].to_broadcast([NE, nn]), w, 0.0, ALU.mult, ALU.add))
                    v.settle()
                    v.do(dve.tensor_tensor(r, r, w, ALU.mult))
                    v.settle()
                    v.do(dve.tensor_scalar(r, r, -1.0, None, ALU.add), s.posm_ready)
                dve.wait_ge(s.post_mm, l + 1)
                v.do(dve.tensor_copy(post[:, t0:NT, :], ps[:, 5, NE * t0:NE * NT].rearrange("p (t e) -> p t e", e=NE)))
                dve.wait_ge(s.iota_done, 1)
                v.settle()

                def selection(t):
                    cap = CAPX if t >= XT0 else CAPC
                    m = selx[:, t - XT0, :] if t >= XT0 else selc[:, t, :]
                    return m.rearrange("p (e c) -> p e c", c=cap), cap

                for t in tiles:
                    m, cap = selection(t)
                    v.do(dve.tensor_tensor(m, iota[:, 0:cap].unsqueeze(1).to_broadcast([P, NE, cap]),
                                           post[:, t, :].unsqueeze(2).to_broadcast([P, NE, cap]), ALU.is_equal), s.sel_ready)
                dve.wait_ge(s.ga_mm, GA[l])
                for t in tiles:
                    m, cap = selection(t)
                    v.do(dve.tensor_tensor(m, m, aff[:, t, :].unsqueeze(2).to_broadcast([P, NE, cap]), ALU.mult), s.selg_ready)

            def experts(l):
                ns = (SLOTS, CAPX)[l]
                for i, sem in enumerate((s.gu_free, s.gu_free, s.y_free, s.y_free, s.sc_free, s.sc_free)):
                    dve.memset(top8[:, i:i + 1], 0.0).then_inc(sem, 1)
                h3 = hid[:, 0:KD * ns].rearrange("p (k e) -> p (k e)", k=KD)
                with dve.Fori(0, NE // EB) as it:
                    for j in range(EB):
                        for c in range(4):
                            dve.wait_ge(s.w_used, it * (12 * EB) + (MOE0[l] + 12 * j + 2 * c + 2))
                            dve.wait_ge(s.sg_ready, it * (4 * EB) + (4 * j + c + 1 + l * 64))
                            dve.tensor_tensor(hid[:, 2 * c * ns:(2 * c + 2) * ns], sg[c % 2][:, 0:2 * ns], ps[:, 2 + c % 2, 0:2 * ns],
                                              ALU.mult).then_inc(s.gu_free, 1)
                    for m in range(KD):
                        dve.wait_ge(s.sc_mm, it * KD + (m + 1 + l * 32))
                        sets = MSETS[l]
                        for i, (c0, nn, vec) in enumerate(sets):
                            x = RT[:, m, c0:c0 + nn]
                            ins = dve.scalar_tensor_tensor(out=x, in0=ps[:, (m % 2) + 2 * vec, 0:nn], scalar=ada[:, l, 40 + m, vec:vec + 1], in1=x,
                                                           op0=ALU.mult, op1=ALU.add)
                        ins.then_inc(s.sc_free, 1)

            norm(1, MSETS[0], lambda k, vec: gs1[:, 0, 1, 2 * k + vec:2 * k + vec + 1], hT)
            route(0)
            experts(0)

            def over(x):
                return x.unsqueeze(2).to_broadcast([P, SR, SP_])

            def ssd_scalars():
                x3 = lambda b: ps[:, b, 0:64 * NT].rearrange("p (t h) -> p t h", t=NT)
                dve.wait_ge(s.w_used, USED[("stail", 1)])
                v.do(dve.tensor_tensor(s_dt, x3(2), col("sdtb", 0, 64).unsqueeze(1).to_broadcast([P, NT, 64]), ALU.add), s.st_bias)
                dve.wait_ge(s.st_sp, 1)
                v.settle()
                v.do(dve.scalar_tensor_tensor(out=s_dt, in0=s_dt, scalar=0.0, in1=s_tmp, op0=ALU.max, op1=ALU.add))
                v.settle()
                v.do(dve.scalar_tensor_tensor(out=s_a, in0=s_dt, scalar=-1.0, in1=s_A.unsqueeze(1).to_broadcast([P, NT, 64]),
                                              op0=ALU.mult, op1=ALU.mult), s.st_a)
                dve.wait_ge(s.sa_mm, 1)
                dve.wait_ge(s.sr_mm, 1)
                v.do(dve.tensor_scalar(s_a, x3(3), -1.0, None, ALU.mult))
                v.settle()
                v.do(dve.tensor_tensor(s_te, x3(4), s_a, ALU.add))
                v.do(dve.tensor_copy(s_etot, x3(4)), s.sa_cols)
                dve.wait_ge(s.sa_e, 3)
                v.do(dve.tensor_tensor(s_te, s_te, s_dt, ALU.mult))
                for p in s_pre:
                    for c in (0, CTX + 1, N + 2):
                        v.do(dve.memset(p[:, c:c + 1], 0.0))
                v.settle()

            def ssd_group(g):
                hs = [slice(32 * d + SR * g, 32 * d + SR * g + SR) for d in range(2)]
                if g:
                    dve.wait_ge(s.sy_mm, 2 * g)
                for d in range(2):
                    q = slice(32 * d, 32 * d + 32)
                    v.do(dve.tensor_copy(s_sel[q, :, :], ident[q, 32 * d + SR * g:32 * d + SR * g + SR].unsqueeze(2)
                                         .to_broadcast([32, SR, P])))
                v.do(dve.memset(s_h, 0.0))
                v.do(dve.memset(s_yt, 0.0), s.s_sel)
                for i in range(4):
                    ch = (2 * g, 2 * g + 1, 16 + g, 24 + g)[i]
                    c0 = 0 if i < 3 else CTX + 1
                    dve.wait_ge(s.sp_pre, TILES * g + AFTER[i])
                    if i >= 2 or g:
                        dve.wait_ge(s.sp_act, TILES * g + ((-1, 0)[i] if i < 2 else AFTER[i - 2]))
                    p, c = s_pre[i % 2], s_cv[i % 2]
                    w = [col("sconv", 3 * ch + t) for t in range(3)]
                    o = c[:, c0:N + 1]
                    v.do(dve.tensor_scalar(o, p[:, c0 + 1:N + 2], w[1], None, ALU.mult))
                    v.settle()
                    v.do(dve.scalar_tensor_tensor(out=o, in0=p[:, c0:N + 1], scalar=w[0], in1=o, op0=ALU.mult, op1=ALU.add))
                    v.settle()
                    v.do(dve.scalar_tensor_tensor(out=o, in0=p[:, c0 + 2:N + 3], scalar=w[2], in1=o, op0=ALU.mult, op1=ALU.add), s.sp_conv)
                dve.wait_ge(s.str_out, NT * (g + 1))
                for st in range(6):
                    tile = [CHUNK_OF[d][st] for d in range(2)]
                    nx, ns = 4 * g + st - 2, 5 * g + st
                    xt = [s_xtok[:, t, :].rearrange("p (r c) -> p r c", r=SR) for t in tile]
                    if st < 5:
                        for d in range(2):
                            v.do(dve.tensor_tensor(s_xe[d], xt[d], over(s_te[:, tile[d], hs[d]]), ALU.mult), s.s_xend)
                    if st >= 2:
                        for d in range(2):
                            v.do(dve.tensor_tensor(s_xdt[d], xt[d], over(s_dt[:, tile[d], hs[d]]), ALU.mult))
                            dve.wait_ge(s.s_in, 2 * nx + d + 1)
                            v.do(dve.tensor_tensor(s_D[d], ps[:, 4 * d, :].rearrange("p (r i) -> p r i", i=P),
                                                   negm[:, d, :].unsqueeze(1).to_broadcast([P, SR, P]), ALU.add), s.s_dm)
                        for d in range(2):
                            dve.wait_ge(s.s_d, 2 * nx + d + 1)
                            v.do(dve.tensor_tensor(s_D[d], s_D[d], ps[:, 4 * d + 1, 0:P].unsqueeze(1).to_broadcast([P, SR, P]), ALU.mult), s.s_w)
                        for d in range(2):
                            dve.wait_ge(s.s_y, 2 * nx + d + 1)
                            y = s_yt[:, tile[d] - XT0, :].rearrange("p (r c) -> p r c", r=SR)
                            b3 = lambda b: ps[:, 4 * d + b, 0:SR * SP_].rearrange("p (r c) -> p r c", r=SR)
                            v.do(dve.tensor_tensor(s_yi[d], b3(3), over(s_tmp[:, tile[d], hs[d]]), ALU.mult))
                            v.do(dve.tensor_tensor(y, y, b3(2), ALU.add))
                            v.settle()
                            v.do(dve.tensor_tensor(y, y, s_yi[d], ALU.add), s.s_yacc)
                    if st < 5:
                        for d in range(2):
                            h = s_h[:, d, :].rearrange("p (r c) -> p r c", r=SR)
                            dve.wait_ge(s.s_st, 2 * ns + d + 1)
                            v.do(dve.tensor_tensor(h, h, over(s_etot[:, tile[d], hs[d]]), ALU.mult))
                            v.settle()
                            v.do(dve.tensor_tensor(h, h, ps[:, 4 * d + 1, 256:512].rearrange("p (r c) -> p r c", r=SR), ALU.add), s.s_state)
                for i in range(2):
                    dve.wait_ge(s.sy_mm, 2 * g + i + 1)
                    v.do(dve.scalar_tensor_tensor(out=yT[:, 2 * g + i, :], in0=s_xT[:, i, CTX:N], scalar=col("sd", 2 * g + i),
                                                  in1=ps[:, 4 * i, :], op0=ALU.mult, op1=ALU.add), s.sy_out)

            def ssd_out():
                for i in range(16):
                    dve.wait_ge(s.sz_act, i + 1)
                    v.do(dve.tensor_tensor(yT[:, i, :], yT[:, i, :], z_act[i % 2], ALU.mult), s.sz_u)
                dve.wait_ge(s.sz_rt, 1)
                v.do(dve.reciprocal(z_rs, z_rt))
                v.settle()
                for m in range(KD):
                    dve.wait_ge(s.w_used, USED[("sout", m)])
                    v.do(dve.tensor_tensor(z_tmp[m % 2], ps[:, m % 2, :], z_rs, ALU.mult))
                    v.settle()
                    x = RT[:, m, CTX:N]
                    v.do(dve.scalar_tensor_tensor(out=x, in0=z_tmp[m % 2], scalar=ada[:, 1, 16 + m, 0:1], in1=x,
                                                  op0=ALU.mult, op1=ALU.add), s.resid)

            norm(2, (XSET, CSET), lambda k, vec: gs1[:, 1, 0, 2 * k + vec:2 * k + vec + 1], hT)
            ssd_scalars()
            for g in range(SG):
                ssd_group(g)
            ssd_out()
            norm(3, MSETS[1], lambda k, vec: gs1[:, 1, 1, 2 * k + vec:2 * k + vec + 1], hT)
            route(1)
            experts(1)

            def norm2(call, gain, dst):
                dve.wait_ge(s.nrt, nrt0[call] + 1)
                v.do(dve.reciprocal(nrsb[:, CTX:N], nrtb[:, CTX:N]))
                v.settle()
                for k in range(KD):
                    v.do(dve.scalar_tensor_tensor(out=dst(k), in0=RT[:, k, CTX:N], scalar=col(gain, k), in1=nrsb[:, CTX:N],
                                                  op0=ALU.mult, op1=ALU.mult), s.nstt)

            def tt(out, a_, b_, op, sem=None):
                v.do(dve.tensor_tensor(out, a_, b_, op), sem)

            def ts(out, a_, c1, op0, c2=None, op1=None):
                if op1 is None:
                    v.do(dve.tensor_scalar(out, a_, c1, None, op0))
                else:
                    v.do(dve.tensor_scalar(out, a_, c1, c2, op0, op1))

            def s5_prepare():
                re, im = col("lamre", 0, NST), col("lamim", 0, NST)
                dve.wait_ge(s.s5_act, 1)
                tt(f5, im, dt5, ALU.mult)
                tt(t5, re, dt5, ALU.mult, s.s5_ang)
                v.settle()
                ts(f5, f5, 1.0 / (2.0 * np.pi), ALU.mult)
                v.settle()
                ts(den5, f5, ROUND, ALU.add)
                v.settle()
                ts(den5, den5, -ROUND, ALU.add)
                v.settle()
                tt(f5, f5, den5, ALU.subtract)
                v.settle()
                for k in range(9):
                    ts(fk[:, k, :], f5, float(1 << k), ALU.mult)
                v.settle()
                ts(fr, fk, ROUND, ALU.add)
                v.settle()
                ts(fr, fr, -ROUND, ALU.add)
                v.settle()
                tt(fk, fk, fr, ALU.subtract)
                v.settle()
                ts(fr, fk, 0.25, ALU.add)
                v.settle()
                ts(ck, fr, ROUND, ALU.add)
                v.settle()
                ts(ck, ck, -ROUND, ALU.add)
                v.settle()
                tt(fr, fr, ck, ALU.subtract, s.s5_ang)
                dve.wait_ge(s.s5_act, 2)
                dve.wait_ge(s.s5_act, 4)
                tt(nr5, r5, ck[:, 0, :], ALU.mult)
                tt(ni5, r5, sk[:, 0, :], ALU.mult)
                tt(den5, re, re, ALU.mult)
                tt(t5, im, im, ALU.mult)
                v.settle()
                tt(den5, den5, t5, ALU.add)
                ts(nr5, nr5, -1.0, ALU.add)
                v.settle()
                v.do(dve.reciprocal(den5, den5))
                tt(kr5, nr5, re, ALU.mult)
                tt(t5, ni5, im, ALU.mult)
                v.settle()
                tt(kr5, kr5, t5, ALU.add)
                v.settle()
                tt(kr5, kr5, den5, ALU.mult)
                tt(ki5, ni5, re, ALU.mult)
                tt(t5, nr5, im, ALU.mult)
                v.settle()
                tt(ki5, ki5, t5, ALU.subtract)
                v.settle()
                tt(ki5, ki5, den5, ALU.mult)
                v.settle()
                dve.wait_ge(s.router_in, 64)
                kr = kr5.unsqueeze(2).to_broadcast([P, NST, 16])
                ki = ki5.unsqueeze(2).to_broadcast([P, NST, 16])
                v.do(dve.tensor_reduce(parb, ident.rearrange("p (n two c) -> p two n c", two=2, c=16), AX.XY, ALU.add))
                v.settle()

                def blocks(out, x, par):
                    for y in range(2):
                        v.do(dve.tensor_scalar(out[:, :, y, :], x, par[:, y:y + 1], None, ALU.mult))

                for x in range(2):
                    blocks(Bbd[:, x, :, :].rearrange("p t (two c) -> p t two c", two=2), braw[:, x, :, :], parb)
                for x, (f1, f2) in enumerate(((kr, ki), (ki, kr))):
                    v.settle()
                    tt(c1t, craw[:, 0, :, :], f1, ALU.mult)
                    tt(c2t, craw[:, 1, :, :], f2, ALU.mult)
                    v.settle()
                    if x == 0:
                        tt(c1t, c1t, c2t, ALU.subtract)
                    else:
                        v.do(dve.scalar_tensor_tensor(out=c1t, in0=c1t, scalar=-1.0, in1=c2t, op0=ALU.mult, op1=ALU.subtract))
                    v.settle()
                    blocks(Cbd[:, x, :, :].rearrange("p t (two c) -> p t two c", two=2), c1t, parc)
                v.settle()
                v.do(dve.memset(t5, 0.0), s.s5_ang)

            def queries_keys():
                ts(qg, col("qn"), HD ** -0.5, ALU.mult)
                v.settle()
                gains = [qg] * 4 + [col("kn", 1), col("kn", 2)]
                dst = [qT[:, j, :] for j in range(4)] + [kS, kW]
                for i in range(6):
                    dve.wait_ge(s.bq_rt, i + 1)
                    r = brt[i % 2]
                    v.do(dve.reciprocal(r, r))
                    v.settle()
                    v.do(dve.scalar_tensor_tensor(out=dst[i], in0=dst[i], scalar=gains[i], in1=r, op0=ALU.mult, op1=ALU.mult), s.bq_n)
                dve.wait_ge(s.bq_copy, 8)
                for which, x in enumerate((kC, vC)):
                    y = x.rearrange("p (b i) -> p b i", i=CMPB)
                    tt(y, y, col("pe", CMPB * which, CMPB).unsqueeze(1).to_broadcast([P, NCMP, CMPB]), ALU.add, s.bc_vec)

            def compress():
                dve.wait_ge(s.bc_act, 12)
                r = brt[0][:, 0:NCMP]
                v.do(dve.reciprocal(r, r))
                v.settle()
                v.do(dve.scalar_tensor_tensor(out=kcm, in0=kcm, scalar=col("kn", 0), in1=r, op0=ALU.mult, op1=ALU.mult), s.bc_vec)

            def attention():
                def weigh(u):
                    qt, h = u // NH, u % NH
                    dve.wait_ge(s.at_e, 3 * u + 3)
                    c = acoef[:, u, :]
                    ts(c, asum[:, 3 * u:3 * u + 3], 1e-30, ALU.max)
                    v.settle()
                    v.do(dve.reciprocal(c, c))
                    v.settle()
                    for b in range(3):
                        tt(acoef[:, u, b:b + 1], acoef[:, u, b:b + 1], ng[:, qt, 3 * h + (b + 1) % 3:3 * h + (b + 1) % 3 + 1], ALU.mult)
                    dve.wait_ge(s.at_v, 3 * u + 3)
                    v.settle()
                    o = oTok[:, qt, HD * h:HD * h + HD]
                    E = lambda b: ps[:, 4 + u % 2, HD * b:HD * b + HD]
                    v.do(dve.tensor_scalar(o, E(0), acoef[:, u, 0:1], None, ALU.mult))
                    for b in (1, 2):
                        v.settle()
                        v.do(dve.scalar_tensor_tensor(out=o, in0=E(b), scalar=acoef[:, u, b:b + 1], in1=o, op0=ALU.mult, op1=ALU.add),
                             s.at_o if b == 2 else None)

                for n in range(96 + 3):
                    if n < 96:
                        u, b = n // 3, n % 3
                        qt = u // NH
                        dve.wait_ge(s.at_s, n + 1)
                        m = anm[:, n:n + 1]
                        if b < 2:
                            x = ps[:, n % 2, qt * P:(qt + 1) * P]
                            tt(x, x, negm[:, 1, :], ALU.add)
                            v.settle()
                            v.do(dve.tensor_reduce(m, ps[:, n % 2, 0:(qt + 1) * P], AX.X, ALU.max, negate=True), s.at_m)
                        else:
                            x = csc[u % 2]
                            if u >= 2:
                                dve.wait_ge(s.at_e, n - 5)
                            tt(x, ps[:, n % 2, 0:NCMP], cmask[:, qt, :], ALU.add)
                            v.settle()
                            v.do(dve.tensor_reduce(m, x, AX.X, ALU.max, negate=True))
                            v.settle()
                            v.do(dve.tensor_scalar(m, m, 1e25, None, ALU.min), s.at_m)
                    if n >= 5 and (n - 5) % 3 == 0:
                        weigh((n - 5) // 3)

            def s5():
                z = S5
                for st in range(NST):
                    c, si = Ec[:, st % 4, :], Es[:, st % 4, :]
                    if st % 4 == 0:
                        dve.wait_ge(s.s5_tab, st // 4 + 1)
                    dve.wait_ge(s.s5_b, st + 1)
                    br, bi = ps[:, 2 * (st % 2), :], ps[:, 2 * (st % 2) + 1, :]
                    tt(z.t1, br, c, ALU.mult)
                    tt(z.t2, bi, si, ALU.mult)
                    tt(z.t3, bi, c, ALU.mult)
                    tt(z.t4, br, si, ALU.mult)
                    v.settle()
                    tt(z.zr, z.t1, z.t2, ALU.add)
                    tt(z.zi, z.t3, z.t4, ALU.subtract)
                    v.settle()
                    r = r5[:, st:st + 1].to_broadcast([P, SEQ])
                    if st:
                        dve.wait_ge(s.s5_x, 2 * st)
                    v.do(dve.tensor_tensor_scan(z.wr, r, z.zr, 0.0, ALU.mult, ALU.add))
                    v.do(dve.tensor_tensor_scan(z.wi, r, z.zi, 0.0, ALU.mult, ALU.add), s.s5_w)
                    if st % 4 == 0 and st:
                        own_part(st // 4 - 1)
                dve.wait_ge(s.s5_x, 2 * NST)
                own_part(3)

            def own_part(t):
                dve.wait_ge(s.s5_y, 4 * t + 4)
                v.do(dve.scalar_tensor_tensor(out=yg[:, t, :], in0=uT[:, t, :], scalar=col("ssmd", t), in1=ps[:, 4 + t % 2, :],
                                              op0=ALU.mult, op1=ALU.add), s.s5_yd)

            def conv2():
                v.settle()
                v.do(dve.memset(zpad[:, 0:2], 0.0))
                v.settle()
                for i in range(4):
                    dve.wait_ge(s.cv_cc, i + 1)
                    w = [col("conv2", 3 * i + x) for x in range(3)]
                    tt(zpad[:, 2:SEQ + 2], ccs, ps[:, 3 * (i % 2) + 1, :], ALU.mult)
                    v.settle()
                    v.do(dve.tensor_scalar(cvt, zpad[:, 2:SEQ + 2], w[2], None, ALU.mult))
                    for x in (1, 0):
                        v.settle()
                        v.do(dve.scalar_tensor_tensor(out=cvt, in0=zpad[:, x:x + SEQ], scalar=w[x], in1=cvt, op0=ALU.mult, op1=ALU.add))
                    v.settle()
                    tt(ycv[:, i, :], cvt, ps[:, 3 * (i % 2) + 2, :], ALU.mult, s.cv_out)

            def mix():
                for m in range(KD):
                    dve.wait_ge(s.mg_act, 4 * m + 4)
                    if m:
                        v.settle()
                    tt(mt1, mact[3], ps[:, 3, :], ALU.mult)
                    dve.wait_ge(s.w_used, USED[("nso", m)])
                    tt(mt2, mact[1], ps[:, 5, :], ALU.mult)
                    tt(mt3, mact[2], ps[:, 6, :], ALU.mult)
                    v.settle()
                    tt(mt1, mt1, mact[0], ALU.mult)
                    tt(mt2, mt2, mt3, ALU.add)
                    v.settle()
                    tt(mixed[:, m, :], mt1, mt2, ALU.add, s.mg_mix)
                for m in range(KD):
                    if m % 2:
                        dve.wait_ge(s.w_used, USED[("wo", m // 2)])
                    else:
                        dve.wait_ge(s.wo_mm, m // 2 + 1)
                    x = RT[:, m, CTX:N]
                    tt(x, x, ps[:, m % 2, :], ALU.add, s.resid)

            def ffn():
                for i in range(FF2 // P):
                    dve.wait_ge(s.ff_act, i + 1)
                    tt(fhid[:, i, :], fact[i % 2], ps[:, 2 * (i % 2) + 1, :], ALU.mult, s.ff_hid)
                for m in range(KD):
                    dve.wait_ge(s.w_used, USED[("fd", m, 1)])
                    x = RT[:, m, CTX:N]
                    tt(x, x, ps[:, 4 + m % 2, :], ALU.add, s.resid)

            norm2(4, "final", lambda k: RT[:, k, CTX:N])
            norm2(5, "mixn", lambda k: h2[:, k, :])
            dve.wait_ge(s.mask_done, MASKS + 8)
            s5_prepare()
            queries_keys()
            compress()
            attention()
            s5()
            conv2()
            mix()
            norm2(6, "ffnn", lambda k: h2[:, k, :])
            ffn()


def pack_cols(i):
    def chan(a, lead=()):
        a = np.asarray(a)
        n = a.shape[-1] // P
        a = a.reshape(a.shape[:-1] + (n, P))
        return np.moveaxis(a, -1, 0)

    def row(a):
        a = np.asarray(a).reshape(1, -1)
        return np.broadcast_to(a, (P, a.shape[1]))

    c2 = np.stack([np.asarray(i["c"])[0], np.asarray(i["c_ctx"])])
    cols = dict(
        cvec=np.moveaxis(chan(c2), 1, 2),
        ada_b=chan(i["ada_b"]), norm1=chan(i["norm1_g"]), norm2=chan(i["norm2_g"]),
        final=chan(i["final_norm_g"]), mixn=chan(i["mix_norm_g_2"][0]), ffnn=chan(i["ffn_norm_g_2"][0]),
        gconv=np.moveaxis(chan(i["gdn_conv_w"][0]), 1, 2), galog=row(i["gdn_a_log"]), gdtb=row(i["gdn_dt_bias"]),
        gnorm=chan(i["gdn_norm_g"][0]),
        sconv=np.moveaxis(chan(i["ssd_conv_w"][0]), 1, 2), sconvb=chan(i["ssd_conv_b"][0]),
        salog=row(i["ssd_a_log"]), sdtb=row(i["ssd_dt_bias"]),
        sd=chan(np.repeat(np.asarray(i["ssd_d"][0]), SP_)), snorm=chan(i["ssd_norm_g"][0]),
    )
    g = lambda a: np.asarray(a)[0].reshape(16, P).T
    cols.update(
        lamre=g(i["ssm_lam_re_2"]), lamim=g(i["ssm_lam_im_2"]),
        logdt=np.repeat(np.asarray(i["ssm_log_dt_2"])[0], 64).reshape(16, P).T,
        ssmd=chan(i["ssm_d_2"][0]), conv2=np.moveaxis(chan(i["conv_w_2"][0]), 1, 2),
        qn=np.concatenate([np.asarray(i["q_norm_g_2"])[0]] * 2)[:, None],
        kn=np.concatenate([np.asarray(i["k_norm_g_2"])[0]] * 2, axis=1).T,
        pe=np.concatenate([np.moveaxis(np.asarray(i["cmp_pe_2"])[0], 2, 0)] * 2),
    )
    out = np.empty((P, NCOLS), np.float32)
    for k, (a, w) in AT.items():
        out[:, a:a + w] = np.asarray(cols[k]).reshape(P, w)
    return out


WEIGHTS = ["ada_w", "router_w", "moe_w_gate", "moe_w_up", "moe_w_down", "gdn_w_in", "gdn_w_out", "ssd_w_in",
           "ssd_w_out", "w_in_2", "ssm_w_glu_2", "conv_w_out_2", "cmp_w1_2", "cmp_w2_2", "nsa_w_o_2", "w_out_2",
           "ffn_w_gate_up_2", "ffn_w_down_2"]


def lay_out(inputs):
    tokens = np.concatenate([np.asarray(inputs["ctx"])[0], np.asarray(inputs["x"])[0]])
    pair = lambda a: np.asarray(a)[0]
    s5b = np.stack([pair(inputs[n]).transpose(0, 2, 1).reshape(4, P, 64).transpose(1, 0, 2) for n in ("ssm_b_re_2", "ssm_b_im_2")])
    s5c = np.stack([pair(inputs[n]).transpose(0, 2, 1).reshape(NST, P, 16).transpose(1, 0, 2) for n in ("ssm_c_re_2", "ssm_c_im_2")])
    arrays = {"s5b": s5b, "s5c": s5c, "tokens": np.ascontiguousarray(tokens.T.reshape(KD, P, N).transpose(1, 0, 2)), "cols": pack_cols(inputs)}
    for n in WEIGHTS:
        arrays[n] = np.ascontiguousarray(inputs[n])
    return arrays


def kernel(**inputs):
    import concourse.bacc as bacc
    from concourse.bass_utils import run_bass_kernel_spmd

    arrays = {n: np.ascontiguousarray(a) for n, a in lay_out(inputs).items()}
    nc = bacc.Bacc("TRN2", target_bir_lowering=False, num_devices=1)
    aps = {n: nc.dram_tensor(n, a.shape, F32, kind="ExternalInput").ap() for n, a in arrays.items()}
    aps["out"] = nc.dram_tensor("out", (KD, P, SEQ), F32, kind="ExternalOutput").ap()
    build(nc, aps)
    got = run_bass_kernel_spmd(nc, [arrays], core_ids=[0]).results[0]["out"]
    return np.ascontiguousarray(np.asarray(got).reshape(D, SEQ).T)[None]
```

```python
from contextlib import ExitStack

import numpy as np

import concourse.bass as bass
from concourse import mybir

F32 = mybir.dt.float32
F32R = mybir.dt.float32r
ALU = mybir.AluOpType
ACT = mybir.ActivationFunctionType
AX = mybir.AxisListType

P = 128
D = 1024
KD = D // P
CTX, SEQ = 256, 512
N = CTX + SEQ
NT = N // P
XT0 = CTX // P
XSET, CSET = (CTX, SEQ, 0), (0, CTX, 1)
EPS = 1e-6

GH = 8
HG = 4
LEVELS = 7
CHUNK_OF = ([0, 1, 2, 3, 4, 5], [1, 0, 5, 4, 3, 2])

SG, SR, SP_ = 8, 4, 64
SH = SG * SR
SI = SH * SP_

NE = 16
CAPX, CAPC = 2 * SEQ // NE, 2 * CTX // NE
SLOTS = CAPX + CAPC
FF = 1024
EB = 4

FF2 = 2816
FF_PARTS = [range(n, min(n + 4, FF2 // 256)) for n in range(0, FF2 // 256, 4)]
NH, HD = 8, 64
NCMP, CMPB = SEQ // 32, 32
WU, WCB, WCC, WCX, WQ = 0, 512, 1024, 1536, 2048
WKC, WVC, WKS, WVS, WKW, WVW, WNG, WMG = 2560, 2688, 2816, 2944, 3072, 3200, 3328, 3352
NST = 16
TURN = 6.2831850
HALF = dict(ssd=12, ssd_z=12 + SG, conv=20 + SG, mix=22 + SG, ffn=26 + SG)
JOBS = SEQ // P * NH * 2
H2 = SI // P
UNITS = 4 + KD
ROUND = 12582912.0

ARENA = 53000
CW = 256
CHUNK = KD * CW
RING = 6
NEG = -1e30

COLS = dict(
    cvec=16, ada_b=96, norm1=16, norm2=16, final=8, mixn=8, ffnn=8,
    gconv=72, galog=16, gdtb=16, gnorm=1,
    sconv=96, sconvb=32, salog=64, sdtb=64, sd=16, snorm=16,
    lamre=16, lamim=16, logdt=16, ssmd=4, conv2=12, qn=1, kn=3, pe=32,
)
AT, NCOLS = {}, 0
for _k, _w in COLS.items():
    AT[_k] = (NCOLS, _w)
    NCOLS += _w


ADA = [[("ada", l, n), ("ada", l, n + 1)] for l in range(2) for n in range(0, 24, 2)]
ADA_FIRST = 4
ADA_GDN = [{2 * n + 1: 4 + n for n in range(6)}, {1: 10, 3: 11, 5: 12, 7: 13, 9: 14, 11: 15, 12: 16, 13: 17}]
ADA_SSD = {g: 18 + g for g in range(6)}


def weight_plan():
    plan = sum(ADA[:ADA_FIRST], []) + [("gtail",)]
    for hg in range(GH // HG):
        for i in range(14):
            if i % 2 == 0 and i < 12:
                plan += [("gin", i // 4, hg, (i // 2) % 2)]
            if i in ADA_GDN[hg]:
                plan += ADA[ADA_GDN[hg][i]]
        plan += [("gz", hg, n) for n in range(2)] + [("gout", hg, n) for n in range(2)]
    plan += [("moe", 0)]
    plan += [("stail", n) for n in range(2)]
    for g in range(SG):
        plan += [("sx", g), ("sb", g), ("sc", g)] + (ADA[ADA_SSD[g]] if g in ADA_SSD else [])
    plan += [("sz", n) for n in range(SI // CW)] + [("sout", m) for m in range(KD)]
    plan += [("moe", 1)]
    plan += [("bv", n) for n in range(3)]
    plan += [("bq", n) for n in range(2)] + [("bk", n) for n in range(4)]
    plan += [("c1", which, n) for which in range(2) for n in range(2)] + [("c2",)]
    plan += [("bu", n) for n in range(2)]
    for n in range(2):
        plan += [("cc", n), ("cx", n), ("cb", n)]
    for m in range(KD):
        plan += [("mg", 1, m), ("mg", 2, m), ("cvo", m), ("nso", m)]
    for m in range(KD):
        plan += [("mg", 0, m), ("glu", m)]
    plan += [("wo", n) for n in range(4)]
    for part, pairs in enumerate(FF_PARTS):
        for n in pairs:
            plan += [("fg", n), ("fu", n)]
        plan += [("fd", part, m) for m in range(KD)]
    return plan


FFN = [x for x in weight_plan() if x[0] in ("fg", "fu", "fd")]
SPLIT = [x for x in weight_plan() if x[0] == "sout"] + FFN


def chunks_of(item):
    return NE * 12 if item[0] == "moe" else 1


PLAN = weight_plan()
USED, CHUNKS = {}, 0
for _item in PLAN:
    CHUNKS += chunks_of(_item)
    USED[_item] = CHUNKS
RING0 = -(USED[("moe", 0)] - NE * 12) % RING


class Lane:

    def __init__(self, eng, steps):
        self.eng, self.steps, self.count, self.last = eng, steps, {}, None

    def do(self, ins, sem=None):
        sem = sem or self.steps
        self.count[sem.name] = self.count.get(sem.name, 0) + 1
        self.last = (sem, self.count[sem.name])
        ins.then_inc(sem, 1)

    def settle(self):
        self.eng.wait_ge(*self.last)


class Signals:

    def __init__(self, new):
        self.const_in = new("const_in")
        self.mask_done = new("mask_done")
        self.level_masks = new("level_masks")
        self.vec_steps = new("vec_steps")
        self.act_steps = new("act_steps")
        self.pool_steps = new("pool_steps")
        self.w_used = new("w_used")
        self.router_in = new("router_in")
        self.cv_done = new("cv_done")
        self.ada_row = new("ada_row")
        self.ada_cols = new("ada_cols")
        self.ada_copied = new("ada_copied")
        self.nsq = new("nsq")
        self.nsq_sum = new("nsq_sum")
        self.nrt = new("nrt")
        self.nstt = new("nstt")
        self.h_ready = new("h_ready")
        self.half_done = new("half_done")
        self.gp_pre = new("gp_pre")
        self.gp_conv = new("gp_conv")
        self.gp_act = new("gp_act")
        self.gp_sq = new("gp_sq")
        self.gp_sum = new("gp_sum")
        self.gp_rt = new("gp_rt")
        self.gp_norm = new("gp_norm")
        self.gt_bias = new("gt_bias")
        self.gt_act = new("gt_act")
        self.gt_g = new("gt_g")
        self.gc_mm = new("gc_mm")
        self.gc_cols = new("gc_cols")
        self.gr_mm = new("gr_mm")
        self.gr_rows = new("gr_rows")
        self.r_in = new("r_in")
        self.r_dm = new("r_dm")
        self.r_kq = new("r_kq")
        self.r_kk = new("r_kk")
        self.r_bt = new("r_bt")
        self.r_in2 = new("r_in2")
        self.r_eb = new("r_eb")
        self.r_q = new("r_q")
        self.r_d = new("r_d")
        self.r_xt = new("r_xt")
        self.r_y = new("r_y")
        self.r_ym = new("r_ym")
        self.r_tu = new("r_tu")
        self.r_l = new("r_l")
        self.r_kv = new("r_kv")
        self.r_kvs = new("r_kvs")
        self.r_w = new("r_w")
        self.r_nw = new("r_nw")
        self.r_vn = new("r_vn")
        self.r_vnc = new("r_vnc")
        self.r_o = new("r_o")
        self.r_state = new("r_state")
        self.go_sq = new("go_sq")
        self.go_sum = new("go_sum")
        self.go_rt = new("go_rt")
        self.go_n = new("go_n")
        self.go_z = new("go_z")
        self.go_sz = new("go_sz")
        self.go_o = new("go_o")
        self.go_mm = new("go_mm")
        self.resid = new("resid")
        self.lg_mm = new("lg_mm")
        self.sm_sub = new("sm_sub")
        self.sm_exp = new("sm_exp")
        self.aff_ready = new("aff_ready")
        self.afft_mm = new("afft_mm")
        self.posm_ready = new("posm_ready")
        self.post_mm = new("post_mm")
        self.sel_ready = new("sel_ready")
        self.ht_mm = new("ht_mm")
        self.ht_lead = new("ht_lead")
        self.ht_copied = new("ht_copied")
        self.ga_mm = new("ga_mm")
        self.ga_copied = new("ga_copied")
        self.selg_ready = new("selg_ready")
        self.st_mm = new("st_mm")
        self.st_copied = new("st_copied")
        self.x_cur = new("x_cur")
        self.sg_ready = new("sg_ready")
        self.gu_free = new("gu_free")
        self.y_free = new("y_free")
        self.sc_mm = new("sc_mm")
        self.sc_free = new("sc_free")
        self.st_bias = new("st_bias")
        self.st_sp = new("st_sp")
        self.st_a = new("st_a")
        self.sa_mm = new("sa_mm")
        self.sa_cols = new("sa_cols")
        self.sa_e = new("sa_e")
        self.sr_mm = new("sr_mm")
        self.sr_rows = new("sr_rows")
        self.sp_pre = new("sp_pre")
        self.sp_conv = new("sp_conv")
        self.sp_act = new("sp_act")
        self.str_mm = new("str_mm")
        self.str_out = new("str_out")
        self.s_xend = new("s_xend")
        self.s_in = new("s_in")
        self.s_dm = new("s_dm")
        self.s_d = new("s_d")
        self.s_e = new("s_e")
        self.s_w = new("s_w")
        self.s_y = new("s_y")
        self.s_yacc = new("s_yacc")
        self.s_st = new("s_st")
        self.s_state = new("s_state")
        self.sz_act = new("sz_act")
        self.sz_u = new("sz_u")
        self.sz_sq = new("sz_sq")
        self.sz_n = new("sz_n")
        self.sz_sum = new("sz_sum")
        self.sz_rt = new("sz_rt")
        self.bv_out = new("bv_out")
        self.bq_copy = new("bq_copy")
        self.bq_sq = new("bq_sq")
        self.bq_sum = new("bq_sum")
        self.bq_rt = new("bq_rt")
        self.bq_n = new("bq_n")
        self.bc_vec = new("bc_vec")
        self.bc_act = new("bc_act")
        self.bc_sum = new("bc_sum")
        self.at_s = new("at_s")
        self.at_m = new("at_m")
        self.at_e = new("at_e")
        self.at_t = new("at_t")
        self.at_c = new("at_c")
        self.at_v = new("at_v")
        self.at_o = new("at_o")
        self.ao_mm = new("ao_mm")
        self.ao_copy = new("ao_copy")
        self.s5_ang = new("s5_ang")
        self.s5_act = new("s5_act")
        self.s5_tab = new("s5_tab")
        self.s5_b = new("s5_b")
        self.s5_w = new("s5_w")
        self.s5_x = new("s5_x")
        self.s5_y = new("s5_y")
        self.s5_yd = new("s5_yd")
        self.s5_gelu = new("s5_gelu")
        self.s5_u = new("s5_u")
        self.cv_cc = new("cv_cc")
        self.cv_out = new("cv_out")
        self.mg_act = new("mg_act")
        self.mg_mix = new("mg_mix")
        self.ff_act = new("ff_act")
        self.ff_hid = new("ff_hid")
        self.w_split = new("w_split")
        self.out_done = new("out_done")
        self.w_ready = [new(f"w_ready{i}") for i in range(RING)]


class Inverse:

    def __init__(self, new):
        self.A = new()
        self.XT = new()
        self.T = new()
        self.U = new()
        self.Y = new()


class States:

    def __init__(self, new):
        self.zr, self.zi = new(), new()
        self.wr, self.wi = new(), new()
        self.xr, self.xi = new(), new()


class Position:

    def __init__(self):
        self.n, self.uses, self.w = 0, [0] * RING, None



def build(nc, A):
    with ExitStack() as stack:
        s = Signals(lambda name: stack.enter_context(nc.semaphore(name)))
        w_ready = s.w_ready

        with nc.sbuf_tensor("arena", [P, ARENA], F32) as arena:
            pass
        top = [0]

        def rounded_tiles(name, count, start, size=CHUNK):
            with ExitStack() as scope:
                scope.enter_context(nc.sbuf_tensor("before_" + name, [P, start], F32))
                return [scope.enter_context(nc.sbuf_tensor(f"{name}{i}", [P, size], F32R)) for i in range(count)]

        def carve(*shape):
            n = int(np.prod(shape))
            a = arena[:, top[0]:top[0] + n]
            top[0] += n
            assert top[0] <= ARENA, top[0]
            if len(shape) == 2:
                return a.rearrange("p (a b) -> p a b", a=shape[0])
            if len(shape) == 3:
                return a.rearrange("p (a b c) -> p a b c", a=shape[0], b=shape[1])
            return a

        ps = stack.enter_context(nc.psum_tensor("ps", [P, 8, 512], F32))

        RT = carve(KD, N)
        cols = carve(NCOLS)
        ident = carve(P)
        ones = carve(P)
        cum = carve(2, P)
        negm = carve(2, P)
        epsc = carve(1)
        onec = carve(1)
        cact = carve(KD, 2)
        ada = carve(2, 48, 2)
        gs1 = carve(2, 2, 2 * KD)
        top[0] += -top[0] % 8
        ring_at = top[0]
        ring = carve(RING, CHUNK)
        base = top[0]

        def col(name, i=0, w=1):
            a, n = AT[name]
            assert i + w <= n
            return cols[:, a + i:a + i + w]

        hT = carve(KD, N)
        g0 = top[0]
        qkv = [carve(HG, N) for _ in range(3)]
        oT = carve(HG, N)
        S = [carve(HG, P) for _ in range(2)]
        bmask = carve(2, LEVELS, 64)
        rmask = carve(2, LEVELS)
        rows = carve(N)
        beta = carve(NT, 16)
        gcum = carve(NT, 16)
        ngc = carve(NT, 16)
        beg = carve(NT, 16)
        ea = carve(16)
        el = carve(2, HG)
        kcol = carve(4, HG)
        g1 = top[0]
        sets = [Inverse(lambda: carve(HG, P)) for _ in range(4)]
        qE = [carve(HG, P) for _ in range(2)]
        gend = top[0]
        top[0] = gend - 4 * NT * 16
        betag = carve(NT, 32)
        gsp = carve(NT, 16)
        gtmp = carve(NT, 16)
        scalars = gend - 4 * NT * 16
        top[0] = g1
        pre = [carve(N + 3) for _ in range(2)]
        cv = [carve(N + 1) for _ in range(3)]
        sq = [carve(N) for _ in range(2)]
        rt = [carve(N) for _ in range(2)]
        assert top[0] <= scalars
        arow_at = ARENA - 4 * CW
        top[0] = arow_at
        arow = carve(2, 2 * CW)
        top[0] = base
        xsT = carve(KD * NE * SLOTS)
        top[0] += -top[0] % 8
        h_lo = rounded_tiles("h_rest", NT, top[0], D)
        htok = carve(NT, D)
        sel_r = rounded_tiles("picked_x", NT - XT0, top[0], NE * CAPX)
        selx = carve(NT - XT0, NE * CAPX)
        sel_r = rounded_tiles("picked_c", XT0, top[0], NE * CAPC) + sel_r
        selc = carve(XT0, NE * CAPC)
        h_lead = rounded_tiles("h_lead", 1, base + KD * N, (KD - 1) * N)[0][:, :].rearrange("p (m t c) -> p m t c", m=KD - 1, c=P)
        Yx = carve(2, D)
        Yc = carve(D)
        hid = carve(KD * SLOTS)
        xcur = [carve(KD * SLOTS) for _ in range(2)]
        sg = [carve(2 * SLOTS) for _ in range(2)]
        aff = carve(NT, NE)
        smx = carve(NT)
        post = carve(NT, NE)
        affT = carve(N)
        rank = carve(N)
        top8 = carve(8)
        iota = carve(CAPX)
        rw = carve(2, KD * NE)
        h_lead_last = rounded_tiles("h_lead_last", 1, top[0] + -top[0] % 8, N)[0][:, :].rearrange("p (m t c) -> p m t c", m=1, c=P)
        selxT = htok.rearrange("p a b -> p (a b)")[:, 0:8 * SEQ].rearrange("p (a b) -> p a b", a=8)
        selcT = htok.rearrange("p a b -> p (a b)")[:, 8 * SEQ:8 * SEQ + 4 * CTX].rearrange("p (a b) -> p a b", a=4)
        top[0] = base
        h2 = carve(KD, SEQ)
        qT = carve(4, SEQ)
        kS, kW, kC, vC = carve(SEQ), carve(SEQ), carve(SEQ), carve(SEQ)
        vS = carve(2, 4, P)
        ng = carve(4, 3 * NH)
        kcm = carve(NCMP)
        vcm = carve(P)
        hidc = carve(2, 4, NCMP)
        cmask = carve(4, NCMP)
        ones64 = carve(P)
        qg = carve(1)
        btmp = carve(4 * SEQ)
        bsq = [btmp[:, x * SEQ:(x + 1) * SEQ] for x in range(2)]
        brt = [btmp[:, (2 + x) * SEQ:(3 + x) * SEQ] for x in range(2)]
        PTb = brt
        asum = carve(96)
        anm = carve(96)
        mixed = carve(KD, SEQ)
        Pb = [mixed[:, x, :] for x in range(4)]
        oA = qT
        hrow = [mixed[0:2 * NCMP, x, 0:CW] for x in range(2)]
        cP, cPT = mixed[:, 4, :], mixed[:, 5, :]
        cV = mixed[:, 6, :].rearrange("p (h d) -> p h d", h=NH)
        cRep, cHead = mixed[0:NCMP, 7, 0:P], mixed[:, 7, P:P + NH]
        uT = carve(4, SEQ)
        yg = uT
        ycv = carve(4, SEQ)
        Ec, Es = carve(4, SEQ), carve(4, SEQ)
        Bbd = carve(2, 4, P)
        Cbd = carve(2, NST, 32)
        braw, craw = carve(2, 4, 64), carve(2, NST, 16)
        parb, parc = carve(2), carve(2)
        sk, ck, fk, fr = carve(9, NST), carve(9, NST), carve(9, NST), carve(9, NST)
        dt5, r5, f5, nr5, ni5, kr5, ki5, t5, den5 = (carve(NST) for _ in range(9))
        c1t, c2t = carve(NST, 16), carve(NST, 16)
        S5 = States(lambda: carve(SEQ))
        S5.t1, S5.t2 = kS, kW
        S5.t3, S5.t4 = (vS[:, i].rearrange("p a b -> p (a b)") for i in range(2))
        pt1, pt2 = carve(2, CW), carve(2, CW)
        ccs, cvt, zpad = btmp[:, 0:SEQ], btmp[:, SEQ:2 * SEQ], btmp[:, 2 * SEQ:3 * SEQ + 2]
        mact = [kC, vC]
        mt1, mt2 = braw.rearrange("p a b c -> p (a b c)"), craw.rearrange("p a b c -> p (a b c)")
        top[0] = base + KD * N + 6 * N
        top[0] += -top[0] % 8
        leading_at = top[0]
        carve(10, CHUNK)
        fact = [carve(SEQ) for _ in range(2)]
        w_lo = rounded_tiles("w_rest", RING, ring_at)
        h2_lo = rounded_tiles("h2_rest", KD * SEQ // CHUNK, base)
        h2_hi = rounded_tiles("h2_lead", KD * SEQ // CHUNK, leading_at)
        f_hi, f_lo = rounded_tiles("f_lead", 2, leading_at + 2 * CHUNK), rounded_tiles("f_rest", 2, leading_at + 4 * CHUNK)
        w_hi = rounded_tiles("w_lead", 4, leading_at + 6 * CHUNK)
        f = arena[:, leading_at + 4 * CHUNK:leading_at + 6 * CHUNK].rearrange("p (a b) -> p a b", a=8)

        def tile_of(parts, k):
            k, per = k % (len(parts) * CHUNK // SEQ), CHUNK // SEQ
            return parts[k // per][:, k % per * SEQ:(k % per + 1) * SEQ]

        top[0] = base + KD * N
        top[0] += -top[0] % 8
        y_lo = rounded_tiles("y_rest", SI // P * SEQ // CHUNK, top[0])
        yT = carve(SI // P, SEQ)
        s_xT = carve(2, N)
        y_hi = rounded_tiles("y_lead", SI // P * SEQ // CHUNK, top[0] + -top[0] % 8)
        s_Bc = carve(CTX)
        s_B = [carve(SEQ) for _ in range(2)]
        s_C = carve(SEQ)
        s_xtok = [carve(NT, SR * SP_) for _ in range(2)]
        s_Btok = [carve(NT, P) for _ in range(2)]
        s_h = carve(2, SR * SP_)
        s_rows = carve(SEQ)
        s_dt = carve(NT, 2 * SH)
        s_a = carve(NT, 2 * SH)
        s_te = carve(NT, 2 * SH)
        s_etot = carve(NT, 2 * SH)
        s_tmp = carve(NT, 2 * SH)
        s_pre = [carve(N + 3) for _ in range(2)]
        s_cv = [carve(N + 1) for _ in range(2)]
        s_D = [carve(SR, P) for _ in range(2)]
        assert (SI // P * SEQ) <= sum((CTX, 3 * SEQ, 2 * NT * SR * SP_, 2 * NT * P, 2 * SR * SP_, SEQ, 10 * NT * SH)) - 8
        so_hi = rounded_tiles("so_lead", 1, top[0] + -top[0] % 8) + rounded_tiles("so_lead_h", 3, base)
        s_xdt = [carve(SR, SP_) for _ in range(2)]
        s_xe = [carve(SR, SP_) for _ in range(2)]
        s_Ce = [carve(SR, P) for _ in range(2)]
        s_A = s_Ce[0].rearrange("p a b -> p (a b)")[:, 0:2 * SH]
        assert top[0] <= arow_at
        z_act = [s_pre[i][:, 0:SEQ] for i in range(2)]
        z_sq = [s_cv[i][:, 0:SEQ] for i in range(2)]
        z_rt, z_rs = s_D[0].rearrange("p a b -> p (a b)"), s_D[1].rearrange("p a b -> p (a b)")
        z_tmp = [s_xT[:, i, 0:SEQ] for i in range(2)]
        top[0] = g0
        nsqb = [carve(N) for _ in range(4)]
        nrtb = carve(N)
        nrsb = carve(N)


        def source(item):
            kind = item[0]
            if kind == "ada":
                _, l, n = item
                src = A["ada_w"][l].rearrange("(k p) n -> p k n", p=P)[:, :, n * CW:(n + 1) * CW]
            elif kind == "gtail":
                src = A["gdn_w_in"][0].rearrange("(k p) n -> p k n", p=P)[:, :, 4096:4128]
            elif kind == "gin":
                _, part, hg, n = item
                a = part * 1024 + hg * 512 + n * CW
                src = A["gdn_w_in"][0].rearrange("(k p) n -> p k n", p=P)[:, :, a:a + CW]
            elif kind == "gz":
                _, hg, n = item
                a = 3072 + hg * 512 + n * CW
                src = A["gdn_w_in"][0].rearrange("(k p) n -> p k n", p=P)[:, :, a:a + CW]
            elif kind == "gout":
                _, hg, n = item
                a = hg * 512 + n * CW
                src = A["gdn_w_out"][0].rearrange("(k p) n -> p k n", p=P)[:, 4 * hg + 2 * n:4 * hg + 2 * n + 2, :]
            elif kind == "stail":
                src = A["ssd_w_in"][0].rearrange("(k p) n -> p k n", p=P)[:, 4 * item[1]:4 * item[1] + 4, 6144:6208]
            elif kind in ("sx", "sz"):
                a = (SI if kind == "sx" else 0) + CW * item[1]
                src = A["ssd_w_in"][0].rearrange("(k p) n -> p k n", p=P)[:, :, a:a + CW]
            elif kind in ("sb", "sc"):
                a = 2 * SI + (SG * P if kind == "sc" else 0) + P * item[1]
                src = A["ssd_w_in"][0].rearrange("(k p) n -> p k n", p=P)[:, :, a:a + P]
            elif kind == "sout":
                src = A["ssd_w_out"][0].rearrange("(k p) n -> p k n", p=P)[:, :, P * item[1]:P * item[1] + P]
            else:
                return source2(item)
            return [(lambda w: w, src)]

        def source2(item):
            kind = item[0]
            win = A["w_in_2"][0].rearrange("(k p) n -> p k n", p=P)

            def whole(src):
                return [(lambda w: w, src)]

            if kind == "bv":
                a, w = ((WVS, P), (WVW, P), (WNG, 24))[item[1]]
                return whole(win[:, :, a:a + w])
            if kind == "bq":
                src = win[:, 4 * item[1]:4 * item[1] + 4, WQ:WQ + 512].rearrange("p k (two j c) -> p k two j c", two=2, j=4)
                return [((lambda v, x=x, k=k: v.rearrange("p k (j two c) -> p k two j c", two=2, j=4)[:, k, x]), src[:, k, x]) for x in range(2) for k in range(4)]
            if kind == "bk":
                a = (WKS, WKW, WKC, WVC)[item[1]]
                return whole(win[:, :, a:a + P])
            if kind == "c1":
                _, which, n = item
                return whole(A["cmp_w1_2"][0, which].rearrange("(i p) f -> p i f", p=P)[:, 8 * n:8 * n + 8, :])
            if kind == "c2":
                return [((lambda w, x=x: w[:, 2 * x:2 * x + 2, :]), A["cmp_w2_2"][0, x].rearrange("(c p) d -> p c d", p=P))
                        for x in range(2)]
            if kind in ("bu", "cc", "cx", "cb"):
                a = dict(bu=WU, cc=WCC, cx=WCX, cb=WCB)[kind] + CW * item[1]
                return whole(win[:, :, a:a + CW])
            if kind == "mg":
                a = WMG + D * item[1] + P * item[2]
                return whole(win[:, :, a:a + P])
            if kind == "glu":
                w = A["ssm_w_glu_2"][0].rearrange("(k p) n -> p k n", p=P)
                return [((lambda v, x=x: v[:, 4 * x:4 * x + 4, :]), w[:, :, D * x + P * item[1]:D * x + P * item[1] + P]) for x in range(2)]
            if kind in ("cvo", "nso"):
                w = (A["conv_w_out_2"] if kind == "cvo" else A["nsa_w_o_2"])[0].rearrange("(k p) n -> p k n", p=P)
                return whole(w[:, :, P * item[1]:P * item[1] + P])
            if kind == "wo":
                return whole(A["w_out_2"][0].rearrange("(k p) n -> p k n", p=P)[:, :, CW * item[1]:CW * item[1] + CW])
            if kind in ("fg", "fu"):
                a = (FF2 if kind == "fu" else 0) + CW * item[1]
                return whole(A["ffn_w_gate_up_2"][0].rearrange("(k p) n -> p k n", p=P)[:, :, a:a + CW])
            if kind == "fd":
                _, part, m = item
                a, n = 2 * FF_PARTS[part][0], 2 * len(FF_PARTS[part])
                return whole(A["ffn_w_down_2"][0].rearrange("(k p) n -> p k n", p=P)[:, a:a + n, P * m:P * m + P])
            raise KeyError(kind)

        def shape_of(item):
            if item[0] == "c2":
                return (4, HD)
            if item[0] == "glu":
                return (8, P)
            if item[0] == "bq":
                return (4, 512)
            return tuple(source(item)[0][1].shape[1:])

        def lead(t, half):
            if half == 0:
                return [(0, 4, h_lead[:, 0:4, t, :])]
            return [(0, KD - 5, h_lead[:, 4:KD - 1, t, :]), (KD - 5, 1, h_lead_last[:, :, t, :])]

        def slot_view(slot, shape):
            n = int(np.prod(shape))
            return ring[:, slot, 0:n].rearrange("p (a b) -> p a b", a=shape[0])

        def halves(item):
            a, b = shape_of(item)
            high = so_hi[item[1] % 4] if item[0] == "sout" else w_hi[FFN.index(item) % 4]
            return [x[:, 0:a * b].rearrange("p (a b) -> p a b", a=a) for x in (high, w_lo[place(item)])]

        nstt0 = [0, 16, 32, 48, 56, 64, 72]
        nrt0 = [0, 2, 4, 6, 7, 8, 9]
        RES_GDN = 2 * KD * GH // HG
        GA = [24, 24 + 16]
        RES_SSD = RES_GDN + KD
        TILES = 7
        AFTER = (2, 4, 6, 7)
        MSETS = ((XSET, CSET), (XSET,))
        MOE0 = [USED[("moe", l)] - NE * 12 if ("moe", l) in USED else 0 for l in range(2)]

        def place(item):
            return (USED[item] - 1 + RING0) % RING

        filled, FILLED = [0] * RING, {}
        for item in PLAN:
            if item[0] == "moe":
                filled = [x + NE * 12 // RING for x in filled]
            else:
                filled[place(item)] += len(source(item))
                FILLED[item] = filled[place(item)]

        nsqb_g = sq
        block = stack.enter_context(nc.Block())

        @block.sync
        def _(sp):
            sp.dma_start(cols, A["cols"]).then_inc(s.const_in, 16)
            sp.wait_ge(s.const_in, 16)
            sp.dma_start(RT, A["tokens"]).then_inc(s.const_in, 16)
            def load(item):
                n = USED[item] - 1
                slot = (n + RING0) % RING
                if n >= RING:
                    sp.wait_ge(s.w_used, n - RING + 1)
                whole = slot_view(slot, shape_of(item))
                for part, src in source(item):
                    sp.dma_start(part(whole), src).then_inc(w_ready[slot], 16)

            def load_experts(l):
                up = A["moe_w_up"][l].rearrange("e (k p) f -> p e k f", p=P)
                gate = A["moe_w_gate"][l].rearrange("e (k p) f -> p e k f", p=P)
                down = A["moe_w_down"][l].rearrange("e (k p) f -> p e k f", p=P)
                with sp.Fori(0, NE // EB) as it:
                    for j in range(EB):
                        e = bass.ds(it * EB + j, 1)
                        for n in range(12):
                            slot = (12 * j + n) % RING
                            sp.wait_ge(s.w_used, it * (12 * EB) + (MOE0[l] + 12 * j + n - RING + 1))
                            if n < 8:
                                src = (gate, up)[n % 2][:, e, :, CW * (n // 2):CW * (n // 2) + CW]
                                dst = slot_view(slot, (KD, CW))
                            else:
                                src = down[:, e, 2 * (n - 8):2 * (n - 8) + 2, :]
                                dst = slot_view(slot, (2, D))
                            sp.dma_start(dst.unsqueeze(1), src).then_inc(w_ready[slot], 16)
            for item in PLAN:
                if item[0] == "moe":
                    load_experts(item[1])
                    continue
                load(item)
            for m in range(KD):
                sp.wait_ge(s.resid, RES_SSD + KD * len(FF_PARTS) + m + 1)
                sp.dma_start(A["out"][m], RT[:, m, CTX:N]).then_inc(s.out_done, 16)
            sp.wait_ge(s.out_done, 16 * KD)


        @block.gpsimd
        def _(pool):
            g = Lane(pool, s.pool_steps)
            g.do(pool.memset(ident, 0.0))
            g.do(pool.memset(cum, 1.0))
            g.do(pool.memset(negm, 0.0))
            g.do(pool.memset(ones, 1.0), s.mask_done)
            g.do(pool.memset(epsc, EPS), s.mask_done)
            g.do(pool.memset(onec, 1.0), s.mask_done)
            g.settle()
            keep = dict(compare_op=ALU.is_ge, base=0)
            g.do(pool.affine_select(out=ident, in_=ident, compare_op=ALU.not_equal, fill=1.0, base=0,
                                    pattern=[[-1, P]], channel_multiplier=1), s.mask_done)
            for d, sign in ((0, 1), (1, -1)):
                g.do(pool.affine_select(out=cum[:, d, :], in_=cum[:, d, :], fill=0.0, pattern=[[sign, P]],
                                        channel_multiplier=-sign, **keep), s.mask_done)
                g.do(pool.affine_select(out=negm[:, d, :], in_=negm[:, d, :], fill=NEG, pattern=[[sign, P]],
                                        channel_multiplier=-sign, **keep), s.mask_done)
            g.do(pool.memset(bmask, 1.0))
            for d in range(2):
                for l in range(LEVELS):
                    b, nb = 1 << l, 64 >> l
                    m = bmask[:, d, l, :].rearrange("p (n b) -> p n b", b=b)
                    lo, hi = (b, 2 * b - 1) if d == 0 else (0, b - 1)
                    g.settle()
                    g.do(pool.affine_select(out=m, in_=m, fill=0.0, pattern=[[-2 * b, nb], [0, b]],
                                            channel_multiplier=1, compare_op=ALU.is_ge, base=-lo))
                    g.settle()
                    g.do(pool.affine_select(out=m, in_=m, fill=0.0, pattern=[[2 * b, nb], [0, b]],
                                            channel_multiplier=-1, compare_op=ALU.is_ge, base=hi), s.level_masks)
            def current_rows(l):
                ns = sum(MSET[2] and CAPC or CAPX for MSET in MSETS[l])
                xs = xsT[:, 0:KD * NE * ns].rearrange("p (k e) -> p k e", k=KD)
                pool.wait_ge(s.resid, (RES_GDN, RES_SSD)[l])
                g.do(pool.iota(iota, pattern=[[1, CAPX]], base=0, channel_multiplier=0, allow_small_or_imprecise_dtypes=True), s.mask_done)
                pool.wait_ge(s.ga_copied, GA[l])
                with pool.Fori(0, NE // EB) as it:
                    for j in range(EB):
                        pool.wait_ge(s.w_used, it * (12 * EB) + (MOE0[l] + 12 * (j - 2) + 8))
                        pool.tensor_copy(xcur[j % 2][:, 0:KD * ns].rearrange("p (k e) -> p k e", k=KD),
                                         xs[:, :, bass.ds(it * (EB * ns) + j * ns, ns)]).then_inc(s.x_cur, 1)

            current_rows(0)
            current_rows(1)

            pool.wait_ge(s.nstt, 72)
            g.do(pool.memset(cmask, 0.0))
            g.do(pool.memset(ones64, 0.0))
            g.settle()
            for q in range(4):
                g.do(pool.affine_select(out=cmask[:, q, :], in_=cmask[:, q, :], compare_op=ALU.is_ge, fill=NEG,
                                        base=P * q - (CMPB - 1), pattern=[[-CMPB, NCMP]], channel_multiplier=1), s.mask_done)
            g.settle()
            for half in range(2):
                g.do(pool.memset(ones64[HD * half:HD * half + HD, HD * half:HD * half + HD], 1.0), s.mask_done)
                g.settle()
            g.do(pool.memset(parc, 0.0))
            g.settle()
            for half in range(2):
                g.do(pool.memset(parc[HD * half:HD * half + HD, half:half + 1], 1.0), s.mask_done)
                g.settle()
            pool.wait_ge(s.s5_act, 4)

            def tables(b):
                if b >= 2:
                    pool.wait_ge(s.s5_x, 2 * b - 2)
                pair = slice(2 * (b % 2), 2 * (b % 2) + 2)
                ec, es = Ec[:, pair, :], Es[:, pair, :]
                g.do(pool.memset(ec[:, :, 0:1], 1.0))
                g.do(pool.memset(es[:, :, 0:1], 0.0))
                for k in range(9):
                    n = 1 << k
                    c = ck[:, k, 2 * b:2 * b + 2].unsqueeze(2).to_broadcast([P, 2, n])
                    si = sk[:, k, 2 * b:2 * b + 2].unsqueeze(2).to_broadcast([P, 2, n])
                    for out, f1, f2, op in ((ec, c, si, ALU.subtract), (es, si, c, ALU.add)):
                        g.settle()
                        g.do(pool.tensor_tensor(pt1[:, :, 0:n], ec[:, :, 0:n], f1, ALU.mult))
                        g.do(pool.tensor_tensor(pt2[:, :, 0:n], es[:, :, 0:n], f2, ALU.mult))
                        g.settle()
                        last = k == 8 and out is es
                        g.do(pool.tensor_tensor(out[:, :, n:2 * n], pt1[:, :, 0:n], pt2[:, :, 0:n], op), s.s5_tab if last else None)
                g.settle()

            for b in range(NST // 2):
                tables(b)

        MASKS = 8

        @block.tensor
        def _(pe):
            state = Position()

            def take(item):
                assert PLAN[state.n] == item, (PLAN[state.n], item)
                slot = (USED[item] - 1 + RING0) % RING
                state.uses[slot] += len(source(item))
                state.n += 1
                pe.wait_ge(w_ready[slot], 16 * state.uses[slot])
                return slot_view(slot, shape_of(item))

            def ada_products(b):
                if b:
                    pe.wait_ge(s.ada_row, b)
                for x, item in enumerate(ADA[b]):
                    w = take(item)
                    for k in range(KD):
                        mm = pe.matmul(ps[0:2, 6, CW * x:CW * x + CW], cact[:, k, :], w[:, k, :], start=(k == 0), stop=(k == KD - 1))
                    mm.then_inc(s.w_used, 1)

            def ada_turn(b):
                pe.wait_ge(s.ada_row, b + 1)
                if b:
                    pe.wait_ge(s.ada_copied, b)
                for m in range(4):
                    mm = pe.matmul(ps[:, 7, 2 * m:2 * m + 2], arow[0:2, b % 2, m * P:(m + 1) * P], ident[0:2, 0:2], start=True, stop=True)
                mm.then_inc(s.ada_cols, 1)

            def norm_sums(call, sets):
                for k in range(KD):
                    pe.wait_ge(s.nsq, KD * call + k + 1)
                    for j, (c0, nc_, _) in enumerate(sets):
                        mm = pe.matmul(ps[:, j, 0:nc_], ones, nsqb[k % 4][:, c0:c0 + nc_],
                                       start=(k == 0), stop=(k == KD - 1))
                    mm.then_inc(s.nsq_sum, 1)

            pe.wait_ge(s.cv_done, 1)
            pe.wait_ge(s.mask_done, MASKS)
            for b in range(ADA_FIRST):
                ada_products(b)
                if b:
                    ada_turn(b - 1)
            ada_turn(ADA_FIRST - 1)
            norm_sums(0, (XSET, CSET))

            w = take(("gtail",))
            pe.wait_ge(s.h_ready, 16)
            for t in range(NT):
                for k in range(KD):
                    mm = pe.matmul(ps[:, 6, 32 * t:32 * t + 32], hT[:, k, t * P:(t + 1) * P], w[:, k, :],
                                   start=(k == 0), stop=(k == KD - 1))
            mm.then_inc(s.w_used, 1)
            pe.wait_ge(s.gt_g, 1)
            for t in range(NT):
                for d in range(2):
                    mm = pe.matmul(ps[:, 5, 16 * t + 8 * d:16 * t + 8 * d + 8], cum[:, d, :], gsp[:, t, 8 * d:8 * d + 8],
                                   start=True, stop=True)
            mm.then_inc(s.gc_mm, 1)
            for t in range(NT):
                bank, c = (3, t * P) if t < 4 else (4, (t - 4) * P)
                for d in range(2):
                    pe.matmul(ps[32 * d:32 * d + GH, bank, c:c + P], gsp[:, t, 8 * d:8 * d + 8], cum[:, d, :],
                              start=True, stop=True)
                    mm = pe.matmul(ps[64 + 32 * d:64 + 32 * d + GH, bank, c:c + P], beta[:, t, 8 * d:8 * d + 8],
                                   ident, start=True, stop=True)
            mm.then_inc(s.gr_mm, 1)
            pe.wait_ge(s.gr_rows, 8)

            def project(hg):
                def tile(i):
                    if i % 2 == 0:
                        state.w = take(("gin", i // 4, hg, (i // 2) % 2))
                    if i >= 2:
                        pe.wait_ge(s.gp_pre, 2 * (12 * hg + i - 1))
                    elif hg:
                        pe.wait_ge(s.resid, 16 * hg)
                    m = i % 2
                    for j, (c0, nn, _) in enumerate((XSET, CSET)):
                        for k in range(KD):
                            mm = pe.matmul(ps[:, 2 * (i % 2) + j, 0:nn], state.w[:, k, m * P:(m + 1) * P],
                                           hT[:, k, c0:c0 + nn], start=(k == 0), stop=(k == KD - 1))
                    mm.then_inc(s.w_used if i % 2 else s.half_done, 1)

                def sums(i):
                    pe.wait_ge(s.gp_sq, 8 * hg + i + 1)
                    if i >= 1:
                        pe.wait_ge(s.gp_rt, 2 * (8 * hg + i))
                    for j, (c0, nn, _) in enumerate((XSET, CSET)):
                        mm = pe.matmul(ps[:, 4 + j, 0:nn], ones, sq[i % 2][:, c0:c0 + nn], start=True, stop=True)
                    mm.then_inc(s.gp_sum, 1)

                for i in range(14):
                    if i < 12:
                        tile(i)
                    if i in ADA_GDN[hg]:
                        b = ADA_GDN[hg][i]
                        if b > ADA_GDN[hg][1]:
                            ada_turn(b - 1)
                        ada_products(b)
                    if 2 <= i < 10:
                        sums(i - 2)
                ada_turn(b)

            def recurrence(hg):
                q, k_, v = qkv
                heads = [slice(j * P, j * P + P) for j in range(HG)]

                def spread(first, bank, tokens):
                    for j in range(HG):
                        h = first + hg * HG + j
                        mm = pe.matmul(ps[:, bank, heads[j]], ident[first:first + GH, h:h + 1].to_broadcast([GH, P]),
                                       rows[first:first + GH, tokens], start=True, stop=True)
                    return mm

                for pr in range(3):
                    n = hg * 3 + pr
                    cs = [slice(CHUNK_OF[c % 2][2 * pr + c // 2] * P, CHUNK_OF[c % 2][2 * pr + c // 2] * P + P) for c in range(4)]
                    for c in range(4):
                        if pr == 0 and c == 0:
                            pe.wait_ge(s.ada_copied, (10, 18)[hg])
                            pe.wait_ge(s.gp_act, 24 * hg + 24)
                            pe.wait_ge(s.gp_norm, 8 * hg + 8)
                        if pr > 0:
                            pe.wait_ge(s.r_state, 4 * (n - 1) + c + 1)
                        spread(32 * (c % 2), 2 * c, cs[c])
                        for j in range(HG):
                            mm = pe.matmul(ps[:, 2 * c + 1, heads[j]], k_[:, j, cs[c]], k_[:, j, cs[c]], start=True, stop=True)
                        mm.then_inc(s.r_in, 1)
                    for c in range(4):
                        pe.wait_ge(s.r_dm, 4 * n + c + 1)
                        for j in range(HG):
                            mm = pe.matmul(ps[:, 2 * c, heads[j]], k_[:, j, cs[c]], q[:, j, cs[c]], start=True, stop=True)
                        mm.then_inc(s.r_kq, 1)
                    for c in range(4):
                        pe.wait_ge(s.r_kk, 4 * n + c + 1)
                        spread(64 + 32 * (c % 2), 2 * c + 1, cs[c]).then_inc(s.r_bt, 1)
                    for l in range(LEVELS):
                        for c in range(4):
                            z = sets[c]
                            if l == 0:
                                pe.wait_ge(s.r_xt, 4 * n + c + 1)
                            else:
                                pe.wait_ge(s.r_l, 4 * (LEVELS * n + l - 1) + c + 1)
                            for j in range(HG):
                                mm = pe.matmul(ps[:, 2 * c, heads[j]], z.XT[:, j, :], z.T[:, j, :],
                                               start=True, stop=True)
                            mm.then_inc(s.r_y, 1)
                        for c in range(4 if l > 0 else 0):
                            z = sets[c]
                            pe.wait_ge(s.r_ym, 4 * ((LEVELS - 1) * n + l - 1) + c + 1)
                            for j in range(HG):
                                if l < LEVELS - 1:
                                    pe.matmul(ps[:, 2 * c + 1, heads[j]], z.U[:, j, :], z.Y[:, j, :],
                                              start=True, stop=True)
                                mm = pe.matmul(ps[:, 2 * c, heads[j]], z.Y[:, j, :], z.U[:, j, :],
                                               start=True, stop=True)
                            mm.then_inc(s.r_tu, 1)
                    for c in range(4):
                        pe.wait_ge(s.r_l, 4 * (LEVELS * n + LEVELS - 1) + c + 1)
                        for j in range(HG):
                            pe.transpose(ps[:, 2 * c, heads[j]], k_[:, j, cs[c]], ident)
                            mm = pe.transpose(ps[:, 2 * c + 1, heads[j]], v[:, j, cs[c]], ident)
                        mm.then_inc(s.r_kv, 1)
                    for c in range(4):
                        z = sets[c]
                        pe.wait_ge(s.r_kvs, 4 * n + c + 1)
                        for j in range(HG):
                            mm = pe.matmul(ps[:, 2 * c, heads[j]], z.XT[:, j, :], z.U[:, j, :], start=True, stop=True)
                        mm.then_inc(s.r_w, 1)
                    for step in range(2):
                        pair = (2 * step, 2 * step + 1)
                        for c in pair:
                            pe.wait_ge(s.r_nw, 4 * n + c + 1)
                            spread(32 * (c % 2), 2 * c, cs[c]).then_inc(s.r_in2, 1)
                        for c in pair:
                            z = sets[c]
                            if step or pr:
                                pe.wait_ge(s.r_state, 4 * n + c - 1)
                            for j in range(HG):
                                o = ps[:, 2 * c + 1, heads[j]]
                                pe.matmul(o, z.U[:, j, :], z.T[:, j, :], start=True, stop=False)
                                mm = pe.matmul(o, z.XT[:, j, :], S[c % 2][:, j, :], start=False, stop=True)
                            mm.then_inc(s.r_vn, 1)
                        for c in pair:
                            z = sets[c]
                            pe.wait_ge(s.r_vnc, 4 * n + c + 1)
                            pe.wait_ge(s.r_q, 4 * n + c + 1)
                            for j in range(HG):
                                o = ps[:, 2 * c, heads[j]]
                                pe.matmul(o, S[c % 2][:, j, :], qE[c % 2][:, j, :], start=True, stop=False)
                                pe.matmul(o, z.T[:, j, :], z.A[:, j, :], start=False, stop=True)
                                mm = pe.matmul(ps[:, 2 * c + 1, heads[j]], z.Y[:, j, :], z.T[:, j, :], start=True, stop=True)
                            mm.then_inc(s.r_o, 1)

            def gdn_out(hg):
                for j in range(HG):
                    i = hg * HG + j
                    pe.wait_ge(s.go_sq, i + 1)
                    if j >= 1:
                        pe.wait_ge(s.go_rt, 2 * i)
                    else:
                        pe.wait_ge(s.r_state, 12 * hg + 12)
                    for b, (c0, nn, _) in enumerate((XSET, CSET)):
                        mm = pe.matmul(ps[:, b, 0:nn], ones, nsqb_g[j % 2][:, c0:c0 + nn], start=True, stop=True)
                    mm.then_inc(s.go_sum, 1)
                    if j % 2 == 0:
                        state.w = take(("gz", hg, j // 2))
                    if i >= 2:
                        pe.wait_ge(s.go_sz, 2 * (i - 1))
                    for b, (c0, nn, _) in enumerate((XSET, CSET)):
                        for k in range(KD):
                            mm = pe.matmul(ps[:, 2 + b + 2 * (j % 2), 0:nn], state.w[:, k, (j % 2) * P:(j % 2) * P + P],
                                           hT[:, k, c0:c0 + nn], start=(k == 0), stop=(k == KD - 1))
                    mm.then_inc(s.w_used if j % 2 else s.go_z, 1)
                w = [take(("gout", hg, 0)), None]
                w[1] = take(("gout", hg, 1))
                pe.wait_ge(s.go_o, HG * (hg + 1))
                for m in range(KD):
                    i = hg * KD + m
                    if m >= 2:
                        pe.wait_ge(s.resid, 2 * (i - 1))
                    for b, (c0, nn, _) in enumerate((XSET, CSET)):
                        for j in range(HG):
                            mm = pe.matmul(ps[:, b + 2 * (m % 2), 0:nn], w[j // 2][:, j % 2, m * P:(m + 1) * P],
                                           oT[:, j, c0:c0 + nn], start=(j == 0), stop=(j == HG - 1))
                    if m == KD - 1:
                        mm.then_inc(s.w_used, 2)
                    else:
                        mm.then_inc(s.go_mm, 1)

            for hg in range(GH // HG):
                project(hg)
                recurrence(hg)
                gdn_out(hg)

            def route(l):
                tiles = list(range(XT0 if l else 0, NT))
                pe.wait_ge(s.h_ready, (32, 56)[l])
                pe.wait_ge(s.router_in, 16 * (l + 1))
                for t in tiles:
                    for k in range(KD):
                        mm = pe.matmul(ps[:, 2, NE * t:NE * t + NE], hT[:, k, t * P:(t + 1) * P],
                                       rw[:, l, NE * k:NE * k + NE], start=(k == 0), stop=(k == KD - 1))
                mm.then_inc(s.lg_mm, 1)
                for i, (t, half) in enumerate([(t, half) for t in tiles for half in range(2)]):
                    if i >= 2:
                        pe.wait_ge(s.ht_copied, 12 * l + i - 1)
                    for k in range(4):
                        mm = pe.transpose(ps[:, 6 + i % 2, k * P:k * P + P], hT[:, 4 * half + k, t * P:(t + 1) * P], ident)
                    mm.then_inc(s.ht_mm, 1)
                pe.wait_ge(s.aff_ready, l + 1)
                for t in tiles:
                    bank, c = (3, (t - XT0) * P) if t >= XT0 else (4, t * P)
                    mm = pe.transpose(ps[0:NE, bank, c:c + P], aff[:, t, :], ident)
                mm.then_inc(s.afft_mm, 1)
                pe.wait_ge(s.posm_ready, (2, 3)[l])
                for t in tiles:
                    mm = pe.transpose(ps[:, 5, NE * t:NE * t + NE], rank[0:NE, t * P:(t + 1) * P], ident[0:NE, 0:NE])
                mm.then_inc(s.post_mm, 1)
                pe.wait_ge(s.sel_ready, (6, 10)[l])
                pe.wait_ge(s.ht_copied, (12, 20)[l])
                i = 0
                for m in range(KD):
                    for b in range(3 if l == 0 else 2):
                        if i >= 4:
                            pe.wait_ge(s.ga_copied, (0, 24)[l] + i - 3)
                        ts_ = range(XT0) if b == 2 else range(XT0, NT)
                        for t in ts_:
                            rhs = sel_r[t][:, :] if b == 2 else sel_r[t][:, 512 * b:512 * b + 512]
                            high = h_lead[:, m, t, :] if m < KD - 1 else h_lead_last[:, 0, t, :]
                            pe.matmul(ps[:, i % 4, :], high, rhs, start=(t == ts_[0]), stop=False)
                            mm = pe.matmul(ps[:, i % 4, :], h_lo[t][:, m * P:(m + 1) * P], rhs, start=False, stop=(t == ts_[-1]))
                        mm.then_inc(s.ga_mm, 1)
                        i += 1
                pe.wait_ge(s.selg_ready, (6, 10)[l])
                pe.wait_ge(s.ga_copied, GA[l])
                for i in range(8 + (4 if l == 0 else 0)):
                    if i >= 2:
                        pe.wait_ge(s.st_copied, (0, 12)[l] + i - 1)
                    if i < 8:
                        for t in range(XT0, NT):
                            mm = pe.transpose(ps[:, 6 + i % 2, (t - XT0) * P:(t - XT0 + 1) * P], selx[:, t - XT0, i * P:(i + 1) * P], ident)
                    else:
                        for t in range(XT0):
                            mm = pe.transpose(ps[:, 6 + i % 2, t * P:(t + 1) * P], selc[:, t, (i - 8) * P:(i - 7) * P], ident)
                    mm.then_inc(s.st_mm, 1)

            def experts(l):
                ns = (SLOTS, CAPX)[l]
                first = state.n
                base_uses = list(state.uses)
                pe.wait_ge(s.st_copied, (12, 20)[l])
                with pe.Fori(0, NE // EB) as it:
                    pe.wait_ge(s.sc_free, it * KD + (2 + l * 34))
                    for j in range(EB):
                        xc = xcur[j % 2][:, 0:KD * ns].rearrange("p (k e) -> p k e", k=KD)
                        pe.wait_ge(s.x_cur, it * EB + (j + 1 + NE * l))

                        def chunk(n, shape):
                            slot = (12 * j + n) % RING
                            pe.wait_ge(w_ready[slot], it * (16 * 12 * EB // RING) + 16 * (base_uses[slot] + (12 * j + n) // RING + 1))
                            return slot_view(slot, shape)

                        for c in range(4):
                            pe.wait_ge(s.gu_free, it * (4 * EB) + (4 * j + c + 1 + l * 66))
                            for b in (0, 2):
                                w = chunk(2 * c + b // 2, (KD, CW))
                                for m in range(2):
                                    for k in range(KD):
                                        mm = pe.matmul(ps[:, b + c % 2, m * ns:(m + 1) * ns], w[:, k, m * P:(m + 1) * P], xc[:, k, :],
                                                       start=(k == 0), stop=(k == KD - 1))
                                mm.then_inc(s.w_used, 1)
                        pe.wait_ge(s.y_free, it * EB + (j + 1 + l * 18))
                        h3 = hid[:, 0:KD * ns].rearrange("p (k e) -> p k e", k=KD)
                        for d in range(4):
                            w = chunk(8 + d, (2, D))
                            pe.wait_ge(s.gu_free, it * (4 * EB) + (4 * j + d + 3 + l * 66))
                            for kk in range(2):
                                for half in range(2):
                                    mm = pe.matmul(ps[0:ns, 4 + 2 * (j % 2) + half, :], h3[:, 2 * d + kk, :], w[:, kk, 512 * half:512 * half + 512],
                                                   start=(d == 0 and kk == 0), stop=(d == 3 and kk == 1))
                            mm.then_inc(s.w_used, 1)
                    pe.wait_ge(s.y_free, it * EB + (EB + 2 + l * 18))
                    for m in range(KD):
                        pe.wait_ge(s.sc_free, it * KD + (m + 1 + l * 34))
                        for p in range(2):
                            mm = pe.matmul(ps[:, m % 2, :], Yx[:, p, m * P:(m + 1) * P], selxT[:, bass.ds(it * 2 + p, 1), :],
                                           start=(p == 0), stop=(p == 1))
                        if l == 0:
                            mm = pe.matmul(ps[:, 2 + m % 2, 0:CTX], Yc[:, m * P:(m + 1) * P], selcT[:, bass.ds(it, 1), :],
                                           start=True, stop=True)
                        mm.then_inc(s.sc_mm, 1)
                state.n += 1
                for slot in range(RING):
                    state.uses[slot] += NE * 12 // RING

            pe.wait_ge(s.resid, RES_GDN)
            norm_sums(1, MSETS[0])
            route(0)
            experts(0)

            def ssd_scalars():
                pe.wait_ge(s.h_ready, 48)
                w = [take(("stail", 0)), take(("stail", 1))]
                for t in range(NT):
                    for k in range(KD):
                        mm = pe.matmul(ps[:, 2, 64 * t:64 * t + 64], hT[:, k, t * P:(t + 1) * P], w[k // 4][:, k % 4, :],
                                       start=(k == 0), stop=(k == KD - 1))
                mm.then_inc(s.w_used, 2)
                pe.wait_ge(s.st_a, 1)
                for t in range(NT):
                    for d in range(2):
                        o = slice(64 * t + 32 * d, 64 * t + 32 * d + 32)
                        pe.matmul(ps[:, 3, o], cum[:, d, :], s_a[:, t, 32 * d:32 * d + 32], start=True, stop=True)
                        mm = pe.matmul(ps[:, 4, o], ones, s_a[:, t, 32 * d:32 * d + 32], start=True, stop=True)
                mm.then_inc(s.sa_mm, 1)
                for t in range(XT0, NT):
                    for d in range(2):
                        mm = pe.matmul(ps[32 * d:32 * d + 32, 5, (t - XT0) * P:(t - XT0 + 1) * P], s_a[:, t, 32 * d:32 * d + 32],
                                       cum[:, d, :], start=True, stop=True)
                mm.then_inc(s.sr_mm, 1)

            def ssd_tile(g, i, part):
                if part == 0:
                    if i != 1:
                        state.w = take((("sx", g), None, ("sb", g), ("sc", g))[i])
                    if i >= 2:
                        pe.wait_ge(s.sp_pre, TILES * g + AFTER[i - 2])
                    elif g == 0:
                        pe.wait_ge(s.sr_rows, 2)
                    else:
                        pe.wait_ge(s.str_out, NT * g)
                        if i == 1 and g - 1 in ADA_SSD:
                            pe.wait_ge(s.ada_copied, ADA_SSD[g - 1] + 1)
                m = i if i == 1 else 0
                c0, nn, _ = (XSET, CSET)[part]
                if part == 0 or i < 3:
                    for k in range(KD):
                        mm = pe.matmul(ps[:, 4 + 2 * (i % 2) + part, 0:nn], state.w[:, k, m * P:(m + 1) * P], hT[:, k, c0:c0 + nn],
                                       start=(k == 0), stop=(k == KD - 1))
                    if part == (1 if i < 3 else 0):
                        mm.then_inc(s.w_used if i else s.half_done, 1)

            def ssd_tokens(g):
                pe.wait_ge(s.sp_pre, TILES * (g + 1))
                if g in ADA_SSD:
                    ada_products(ADA_SSD[g])
                    pe.wait_ge(s.ada_row, ADA_SSD[g] + 1)
                pe.wait_ge(s.sp_act, TILES * g + 6)
                for t in range(NT):
                    if t >= 4:
                        pe.wait_ge(s.str_out, NT * g + t - 3)
                    c = slice(t * P, (t + 1) * P)
                    pe.transpose(ps[:, 4 + t % 4, 0:P], s_xT[:, 0, c], ident)
                    pe.transpose(ps[:, 4 + t % 4, P:2 * P], s_xT[:, 1, c], ident)
                    b = s_Bc[:, c] if t < XT0 else s_B[g % 2][:, (t - XT0) * P:(t - XT0 + 1) * P]
                    mm = pe.transpose(ps[:, 4 + t % 4, 2 * P:3 * P], b, ident)
                    mm.then_inc(s.str_mm, 1)

            def ssd_scores(g, st):
                nx, ns = 4 * g + st - 2, 5 * g + st
                if st == 2:
                    pe.wait_ge(s.sp_act, TILES * (g + 1))
                for d in range(2):
                    cx = slice((CHUNK_OF[d][st] - XT0) * P, (CHUNK_OF[d][st] - XT0 + 1) * P)
                    pe.wait_ge(s.s_state, 2 * (ns - 1) + d + 1)
                    if nx:
                        pe.wait_ge(s.s_yacc, 2 * (nx - 1) + d + 1)
                    for r in range(SR):
                        h = 32 * d + SR * g + r
                        pe.matmul(ps[:, 2 * d, r * P:(r + 1) * P], ident[32 * d:32 * d + 32, h:h + 1].to_broadcast([32, P]),
                                  s_rows[32 * d:32 * d + 32, cx], start=True, stop=True)
                    mm = pe.matmul(ps[:, 2 * d + 1, 0:P], s_B[g % 2][:, cx], s_C[:, cx], start=True, stop=True)
                    mm.then_inc(s.s_in, 1)

            def ssd_outputs(g, st):
                nx = 4 * g + st - 2
                for d in range(2):
                    pe.wait_ge(s.s_w, 2 * nx + d + 1)
                    for r in range(SR):
                        o = ps[SP_ * (r % 2):SP_ * (r % 2) + SP_, 2 * d, (r // 2) * P:(r // 2 + 1) * P]
                        pe.matmul(o, s_xdt[d][:, r, :], s_D[d][:, r, :], start=True, stop=False)
                        mm = pe.matmul(o, s_h[:, d, r * SP_:(r + 1) * SP_], s_Ce[d][:, r, :], start=False, stop=True)
                    mm.then_inc(s.s_y, 1)

            def ssd_states(g, st):
                ns = 5 * g + st
                for d in range(2):
                    pe.wait_ge(s.s_xend, 2 * ns + d + 1)
                    if ns:
                        pe.wait_ge(s.s_state, 2 * (ns - 1) + d + 1)
                    mm = pe.matmul(ps[:, 2 * d + 1, 256:512], s_Btok[g % 2][:, CHUNK_OF[d][st], :], s_xe[d].rearrange("p a b -> p (a b)"),
                                   start=True, stop=True)
                    mm.then_inc(s.s_st, 1)

            def ssd_groups():
                for i in range(4):
                    ssd_tile(0, i, 0)
                    ssd_tile(0, i, 1)
                ssd_tokens(0)
                for g in range(SG):
                    def fill(i, part):
                        if g + 1 < SG:
                            ssd_tile(g + 1, i, part)

                    ssd_states(g, 0)
                    fill(0, 0)
                    ssd_states(g, 1)
                    if g in ADA_SSD:
                        ada_turn(ADA_SSD[g])
                    ssd_scores(g, 2)
                    fill(0, 1)
                    ssd_outputs(g, 2)
                    ssd_states(g, 2)
                    for st in range(3, 6):
                        ssd_scores(g, st)
                        fill(st - 2, 0)
                        ssd_outputs(g, st)
                        if st < 5:
                            ssd_states(g, st)
                        fill(st - 2, 1)
                    if g + 1 < SG:
                        ssd_tokens(g + 1)

            def take_halves(item):
                assert PLAN[state.n] == item
                state.uses[place(item)] += len(source(item))
                state.n += 1
                pe.wait_ge(s.w_split, SPLIT.index(item) + 1)
                return halves(item)

            def product(out, w, cols_, x, tiles, before=None):
                (wh, wl), (xh, xl) = w, x
                for k in range(tiles):
                    if before:
                        before(k)
                    for n, (a, b) in enumerate(((wh, xh), (wh, xl), (wl, xh))):
                        mm = pe.matmul(out, a[:, k, cols_], tile_of(b, k),
                                       start=(k == 0 and n == 0), stop=(k == tiles - 1 and n == 2))
                return mm

            def ssd_out():
                pe.wait_ge(s.s_yacc, 8 * SG)
                pe.wait_ge(s.sp_pre, TILES * SG)

                def sums(i):
                    pe.wait_ge(s.sz_sq, i + 1)
                    mm = pe.matmul(ps[:, 7, :], ones, z_sq[i % 2], start=(i == 0), stop=(i == 15))
                    mm.then_inc(s.sz_sum, 1)

                for i in range(16):
                    if i % 2 == 0:
                        w = take(("sz", i // 2))
                    if i >= 4:
                        pe.wait_ge(s.sz_act, i - 3)
                    for k in range(KD):
                        mm = pe.matmul(ps[:, i % 4, :], w[:, k, (i % 2) * P:(i % 2 + 1) * P], hT[:, k, CTX:N],
                                       start=(k == 0), stop=(k == KD - 1))
                    mm.then_inc(s.w_used if i % 2 else s.half_done, 1)
                    if i >= 2:
                        sums(i - 2)
                sums(14)
                sums(15)
                for m in range(KD):
                    w = take_halves(("sout", m))
                    if m >= 2:
                        pe.wait_ge(s.resid, RES_GDN + m - 1)
                    split_ready = (lambda k: pe.wait_ge(s.ff_hid, k + 1)) if m == 0 else None
                    product(ps[:, m % 2, :], w, slice(0, P), (y_hi, y_lo), SI // P, split_ready).then_inc(s.w_used, 1)

            pe.wait_ge(s.sc_free, 34)
            norm_sums(2, (XSET, CSET))
            ssd_scalars()
            ssd_groups()
            ssd_out()
            pe.wait_ge(s.resid, RES_SSD)
            norm_sums(3, MSETS[1])
            route(1)
            experts(1)

            def project2(w, banks, n=P):
                for i, bank in enumerate(banks):
                    for k in range(KD):
                        mm = pe.matmul(ps[:, bank, :], w[:, k, i * P:(i + 1) * P], h2[:, k, :], start=(k == 0), stop=(k == KD - 1))
                return mm

            def values():
                for n in range(3):
                    w = take(("bv", n))
                    nn = (P, P, 3 * NH)[n]
                    for t in range(4):
                        for k in range(KD):
                            mm = pe.matmul(ps[:, n, t * nn:(t + 1) * nn], h2[:, k, t * P:(t + 1) * P], w[:, k, :],
                                           start=(k == 0), stop=(k == KD - 1))
                    mm.then_inc(s.w_used, 1)

            def queries_keys():
                pe.wait_ge(s.bv_out, 3)
                for n in range(2):
                    w = take(("bq", n))
                    for j in range(4):
                        for k in range(4):
                            mm = pe.matmul(ps[:, j, :], w[:, k, j * P:(j + 1) * P], h2[:, 4 * n + k, :], start=(n == 0 and k == 0), stop=(n == 1 and k == 3))
                    mm.then_inc(s.w_used, 1)
                for n in range(4):
                    w = take(("bk", n))
                    if n < 2:
                        mm = project2(w, [4 + n])
                    else:
                        for kv in range(2):
                            for par in range(2):
                                for k in range(KD):
                                    tokens = h2[:, k, :].rearrange("p (n two) -> p two n", two=2)[:, par, :]
                                    mm = pe.matmul(ps[HD * par:HD * par + HD, 4 + n, CW * kv:CW * kv + CW], w[:, k, HD * kv:HD * kv + HD],
                                                   tokens, start=(k == 0), stop=(k == KD - 1))
                    mm.then_inc(s.w_used, 1)
                for i in range(6):
                    pe.wait_ge(s.bq_sq, i + 1)
                    if i >= 2:
                        pe.wait_ge(s.bq_rt, i - 1)
                    pe.matmul(ps[:, i % 2, :], ones64, bsq[i % 2], start=True, stop=True).then_inc(s.bq_sum, 1)
                    if 1 <= i <= 4:
                        which, n = (i - 1) // 2, (i - 1) % 2
                        w = take(("c1", which, n))
                        pe.wait_ge(s.bc_vec, which + 1)
                        x = (kC, vC)[which].rearrange("p (b i) -> p b i", i=CMPB // 2)
                        for k in range(8):
                            mm = pe.matmul(ps[0:2 * NCMP, 4 + which, 0:CW], x[:, :, 8 * n + k], w[:, k, :], start=(n == 0 and k == 0), stop=(n == 1 and k == 7))
                        mm.then_inc(s.w_used, 1)

            def compress():
                for which in range(2):
                    pe.wait_ge(s.bc_act, which + 1)
                    for fc in range(2):
                        mm = pe.transpose(ps[:, 6 + which, 2 * NCMP * fc:2 * NCMP * (fc + 1)], hrow[which][:, fc * P:(fc + 1) * P], ident[0:2 * NCMP, 0:2 * NCMP])
                    mm.then_inc(s.bc_sum, 1)
                pe.wait_ge(s.bq_rt, 6)
                w = take(("c2",))
                pe.wait_ge(s.bc_act, 4)
                for kv in range(2):
                    for fc in range(2):
                        pe.matmul(ps[HD * kv:HD * kv + HD, 0, 0:NCMP], w[:, fc, :], hidc[:, 0, 2 * fc + kv, :], start=(fc == 0), stop=(fc == 1))
                for kv in range(2):
                    for fc in range(2):
                        mm = pe.matmul(ps[0:NCMP, 1, HD * kv:HD * kv + HD], hidc[:, 1, 2 * fc + kv, :], w[:, 2 + fc, :], start=(fc == 0), stop=(fc == 1))
                mm.then_inc(s.w_used, 1)
                pe.wait_ge(s.bc_act, 7)
                pe.matmul(ps[:, 2, 0:NCMP], ones64, bsq[0][:, 0:NCMP], start=True, stop=True).then_inc(s.bc_sum, 1)

            def attention():
                pe.wait_ge(s.bc_vec, 3)
                pe.wait_ge(s.bq_n, 6)
                pe.wait_ge(s.bc_act, 6)
                kv = lambda h: slice(HD * (h // 4), HD * (h // 4) + HD)
                for u in range(4 * NH):
                    qt, h = u // NH, u % NH
                    at = NCMP * (4 * qt + h % 4)
                    mm = pe.matmul(ps[:, (7, 4)[h // 4], at:at + NCMP], qT[kv(h), h % 4, qt * P:(qt + 1) * P], kcm[kv(h), :], start=True, stop=True)
                mm.then_inc(s.ao_mm, 1)
                pe.matmul(ps[:, 6, 0:P], cRep, vcm[0:NCMP, :], start=True, stop=True).then_inc(s.ao_mm, 1)

                def job(n):
                    u, b = n // 2, n % 2
                    return b, u // NH, u % NH

                for n in range(JOBS + 4):
                    if n < JOBS:
                        b, qt, h = job(n)
                        if n >= 3:
                            pe.wait_ge(s.at_e, n - 2)
                        nk = (qt + 1) * P
                        pe.matmul(ps[:, n % 3, 0:nk], qT[kv(h), h % 4, qt * P:(qt + 1) * P], (kS, kW)[b][kv(h), 0:nk], start=True, stop=True).then_inc(s.at_s, 1)
                    if n == 3:
                        pe.wait_ge(s.bc_vec, 5)
                        for q in range(4):
                            mm = pe.transpose(ps[:, 7, q * P:(q + 1) * P], cP[:, q * P:(q + 1) * P], ident)
                        mm.then_inc(s.ao_mm, 1)
                    if 3 <= n < JOBS + 3:
                        m = n - 3
                        b, qt, h = job(m)
                        pe.wait_ge(s.at_o, m + 1)
                        if m >= 2:
                            pe.wait_ge(s.at_c, m - 1)
                        for kb in range(qt + 1):
                            mm = pe.transpose(ps[:, 3 + m % 2, kb * P:(kb + 1) * P], Pb[m % 4][:, kb * P:(kb + 1) * P], ident)
                        mm.then_inc(s.at_t, 1)
                    if n >= 4:
                        m = n - 4
                        b, qt, h = job(m)
                        out = ps[:, 5 + qt % 2, :]
                        c = h // 2
                        if b == 0 and h % 2 == 0:
                            if qt == 0 and h == 0:
                                pe.wait_ge(s.bc_act, 10)
                            if qt >= 2 and h == 0:
                                pe.wait_ge(s.ao_copy, qt - 1)
                            pe.matmul(out[:, c * P:(c + 1) * P], cV[:, 2 * c:2 * c + 2, :].rearrange("p h d -> p (h d)"), cPT[:, qt * P:(qt + 1) * P],
                                      start=True, stop=False)
                        pe.wait_ge(s.at_c, m + 1)
                        o = out[HD * (h % 2):HD * (h % 2) + HD, c * P:(c + 1) * P]
                        for kb in range(qt + 1):
                            mm = pe.matmul(o, vS[:, b, kb, kv(h)], PTb[m % 2][:, kb * P:(kb + 1) * P], start=False, stop=(b == 1 and kb == qt))
                        mm.then_inc(s.at_v, 1)

            def s5_input():
                pe.wait_ge(s.ao_copy, 4)
                for n in range(2):
                    project2(take(("bu", n)), [2 * n, 2 * n + 1]).then_inc(s.w_used, 1)
                pe.wait_ge(s.s5_u, 4)
                pe.wait_ge(s.s5_ang, 3)

            def s5_step(st):
                if st < NST:
                    q = slice(32 * (st % 4), 32 * (st % 4) + 32)
                    if st:
                        pe.wait_ge(s.s5_w, st)
                    for x in range(2):
                        mm = pe.matmul(ps[:, 5 + x, :], Bbd[q, x, st // 4, :], uT[q, st // 4, :], start=True, stop=True)
                    mm.then_inc(s.s5_b, 1)
                if st >= 1:
                    j = st - 1
                    q = slice(32 * (j % 4), 32 * (j % 4) + 32)
                    pe.wait_ge(s.s5_x, st)
                    if j % 4 == 0 and j:
                        pe.wait_ge(s.s5_yd, j // 4)
                    pe.matmul(ps[q, 7, :], Cbd[:, 0, j, :], S5.xr, start=True, stop=False)
                    pe.matmul(ps[q, 7, :], Cbd[:, 1, j, :], S5.xi, start=False, stop=True).then_inc(s.s5_y, 1)

            def conv_tile(i, x, w):
                if x == 0 and i >= 2:
                    pe.wait_ge(s.cv_out, i - 1)
                if x == 2 and i >= 1:
                    pe.wait_ge(s.cv_cc, i)
                for k in range(KD):
                    mm = pe.matmul(ps[:, (3 * i + x) % 5, :], w[:, k, (i % 2) * P:(i % 2 + 1) * P], h2[:, k, :], start=(k == 0), stop=(k == KD - 1))
                return mm

            def mix_tile(m, x):
                if m == 0:
                    pe.wait_ge(*((s.cv_out, 3), (s.cv_out, 3), (s.cv_cc, 4), (s.cv_out, 4))[x])
                elif x == 1:
                    pe.wait_ge(s.mg_mix, m)
                bank = (12 + 4 * m + x) % 5
                if x < 2:
                    project2(take(("mg", 1 + x, m)), [bank]).then_inc(s.w_used, 1)
                else:
                    w, src = take((("cvo", "nso")[x - 2], m)), (ycv, oA)[x - 2]
                    for k in range(4):
                        mm = pe.matmul(ps[:, bank, :], w[:, k, :], src[:, k, :], start=(k == 0), stop=(k == 3))
                    mm.then_inc(s.w_used, 1)

            def branches():
                for u in range(UNITS):
                    if u < 4:
                        if u % 2 == 0:
                            state.w = [take((x, u // 2)) for x in ("cc", "cx", "cb")]
                        tile = lambda x: conv_tile(u, x, state.w[x])
                        n = 3
                    else:
                        tile = lambda x: mix_tile(u - 4, x)
                        n = 4
                    mm = tile(0)
                    if n == 4:
                        tile(1)
                    if 2 * u <= NST:
                        s5_step(2 * u)
                    for x in range(n - 2, n):
                        mm = tile(x)
                    if n == 3:
                        if u % 2:
                            mm.then_inc(s.w_used, 3)
                        else:
                            mm.then_inc(s.half_done, 1)
                    if 2 * u + 1 <= NST:
                        s5_step(2 * u + 1)

            def mix():
                pe.wait_ge(s.s5_gelu, 4)
                pe.wait_ge(s.mg_mix, KD)
                for m in range(KD):
                    if m >= 2:
                        pe.wait_ge(s.mg_mix, KD + m - 1)
                    b = 3 * (m % 2)
                    project2(take(("mg", 0, m)), [b]).then_inc(s.w_used, 1)
                    w = take(("glu", m))
                    for x in range(2):
                        for k in range(4):
                            mm = pe.matmul(ps[:, b + 1 + x, :], w[:, 4 * x + k, :], yg[:, k, :], start=(k == 0), stop=(k == 3))
                    mm.then_inc(s.w_used, 1)
                pe.wait_ge(s.mg_mix, 2 * KD)
                for n in range(4):
                    w = take(("wo", n))
                    for x in range(2):
                        m = 2 * n + x
                        if m >= 2:
                            pe.wait_ge(s.resid, RES_SSD + m - 1)
                        for k in range(KD):
                            mm = pe.matmul(ps[:, m % 2, :], w[:, k, x * P:(x + 1) * P], mixed[:, k, :], start=(k == 0), stop=(k == KD - 1))
                        mm.then_inc(s.w_used if x else s.half_done, 1)

            def ffn():
                for part, pairs in enumerate(FF_PARTS):
                    for n in pairs:
                        w = take_halves(("fg", n)), take_halves(("fu", n))
                        for x in range(2):
                            i = 2 * n + x
                            if i >= 2:
                                pe.wait_ge(s.ff_hid, H2 + KD - 1 + i)
                            for b in range(2):
                                if i == 0 and b == 0:
                                    split_ready = lambda k: pe.wait_ge(s.ff_hid, H2 + k + 1)
                                else:
                                    split_ready = None
                                mm = product(ps[:, 2 * (i % 2) + b, :], w[b], slice(x * P, (x + 1) * P), (h2_hi, h2_lo), KD, split_ready)
                            if x:
                                mm.then_inc(s.w_used, 2)
                            else:
                                mm.then_inc(s.half_done, 1)
                    pe.wait_ge(s.ff_hid, H2 + KD + 2 * pairs[-1] + 2)
                    for m in range(KD):
                        i = KD * part + m
                        if i >= 2:
                            pe.wait_ge(s.resid, RES_SSD + KD + i - 1)
                        product(ps[:, 4 + m % 2, :], take_halves(("fd", part, m)), slice(0, P), (f_hi, f_lo), 2 * len(pairs)).then_inc(s.w_used, 1)

            pe.wait_ge(s.sc_free, 68)
            norm_sums(4, (XSET,))
            norm_sums(5, (XSET,))
            pe.wait_ge(s.nstt, 72)
            pe.wait_ge(s.mask_done, MASKS + 10)
            values()
            queries_keys()
            compress()
            attention()
            s5_input()
            branches()
            mix()
            pe.wait_ge(s.resid, RES_SSD + KD)
            norm_sums(6, (XSET,))
            ffn()

        @block.scalar
        def _(act):
            a = Lane(act, s.act_steps)

            def norm(call, sets, layer=None, which=None):
                for k in range(KD):
                    if k >= 4 or call:
                        act.wait_ge(s.nsq_sum, KD * call + k - 3)
                    c0, c1 = min(x[0] for x in sets), max(x[0] + x[1] for x in sets)
                    a.do(act.activation(nsqb[k % 4][:, c0:c1], RT[:, k, c0:c1], ACT.Square), s.nsq)
                act.wait_ge(s.nsq_sum, KD * call + KD)
                for j, (c0, nn, _) in enumerate(sets):
                    a.do(act.activation(nrtb[:, c0:c0 + nn], ps[:, j, 0:nn], ACT.Sqrt, bias=epsc, scale=1.0 / D), s.nrt)
                if layer is None:
                    return
                for k in range(KD):
                    for j, (c0, nn, v) in enumerate(sets):
                        act.wait_ge(s.nstt, nstt0[call] + len(sets) * k + j + 1)
                        x = hT[:, k, c0:c0 + nn]
                        sh = ada[:, layer, 24 * which + k, v:v + 1]
                        a.do(act.activation(x, x, ACT.Identity, bias=sh), s.h_ready)

            act.wait_ge(s.const_in, 32)
            a.do(act.activation(cact.rearrange("p a b -> p (a b)"), col("cvec", 0, 16), ACT.Silu), s.cv_done)
            act.wait_ge(s.mask_done, 3)

            def ada_row(b):
                act.wait_ge(s.w_used, USED[ADA[b][1]])
                if b >= 2:
                    act.wait_ge(s.ada_copied, b - 1)
                a.do(act.activation(arow[0:2, b % 2, :], ps[0:2, 6, :], ACT.Copy), s.ada_row)

            for b in range(ADA_FIRST):
                ada_row(b)
            norm(0, (XSET, CSET), 0, 0)

            act.wait_ge(s.gt_bias, 1)
            a.do(act.activation(ea, col("galog", 0, 16), ACT.Exp))
            a.do(act.activation(beta, betag[:, :, 0:16], ACT.Sigmoid))
            a.do(act.activation(gtmp, betag[:, :, 16:32], ACT.Abs))
            a.settle()
            a.do(act.activation(gtmp, gtmp, ACT.Exp, scale=-1.0))
            a.settle()
            a.do(act.activation(gtmp, gtmp, ACT.Ln, bias=onec), s.gt_act)
            act.wait_ge(s.gc_cols, 1)
            a.do(act.activation(beg, gcum, ACT.Exp), s.gt_act)
            act.wait_ge(s.gr_mm, 1)
            for q in range(4):
                a.do(act.activation(rows[32 * q:32 * q + GH, 0:512], ps[32 * q:32 * q + GH, 3, :], ACT.Copy), s.gr_rows)
                a.do(act.activation(rows[32 * q:32 * q + GH, 512:768], ps[32 * q:32 * q + GH, 4, 0:256], ACT.Copy), s.gr_rows)

            def project(hg):
                for i in range(14):
                    if i < 12:
                        if i % 2:
                            act.wait_ge(s.w_used, USED[("gin", i // 4, hg, (i // 2) % 2)])
                        else:
                            act.wait_ge(s.half_done, 6 * hg + i // 2 + 1)
                        if i >= 2:
                            act.wait_ge(s.gp_conv, 12 * hg + i - 1)
                        p = pre[i % 2]
                        a.do(act.activation(p[:, 1 + CTX + 1:1 + CTX + 1 + SEQ], ps[:, 2 * (i % 2), :], ACT.Copy), s.gp_pre)
                        a.do(act.activation(p[:, 1:1 + CTX], ps[:, 2 * (i % 2) + 1, 0:CTX], ACT.Copy), s.gp_pre)
                    if i in ADA_GDN[hg]:
                        ada_row(ADA_GDN[hg][i])
                    if 1 <= i < 13:
                        t = i - 1
                        dst = qkv[t // 4][:, t % 4, :]
                        act.wait_ge(s.gp_conv, 12 * hg + t + 1)
                        a.do(act.activation(dst[:, 0:CTX], cv[t % 3][:, 0:CTX], ACT.Silu), s.gp_act)
                        a.do(act.activation(dst[:, CTX:N], cv[t % 3][:, CTX + 1:N + 1], ACT.Silu), s.gp_act)
                        if t < 8:
                            if t >= 2:
                                act.wait_ge(s.gp_sum, 8 * hg + t - 1)
                            a.settle()
                            a.do(act.activation(sq[t % 2], dst, ACT.Square), s.gp_sq)
                    if 2 <= i < 10:
                        t = i - 2
                        act.wait_ge(s.gp_sum, 8 * hg + t + 1)
                        if t >= 2:
                            act.wait_ge(s.gp_norm, 8 * hg + t - 1)
                        a.do(act.activation(rt[t % 2][:, CTX:N], ps[:, 4, :], ACT.Sqrt, bias=epsc), s.gp_rt)
                        a.do(act.activation(rt[t % 2][:, 0:CTX], ps[:, 5, 0:CTX], ACT.Sqrt, bias=epsc), s.gp_rt)

            def recurrence(hg):
                for pr in range(3):
                    n = hg * 3 + pr
                    tile = [CHUNK_OF[c % 2][2 * pr + c // 2] for c in range(4)]
                    flat = lambda x: x.rearrange("p a b -> p (a b)")
                    for c in range(4):
                        z = sets[c]
                        act.wait_ge(s.r_dm, 4 * n + c + 1)
                        for j in range(HG):
                            i = 8 * (c % 2) + hg * HG + j
                            a.do(act.activation(z.T[:, j, :], z.T[:, j, :], ACT.Exp, bias=ngc[:, tile[c], i:i + 1]),
                                 s.r_d if j == HG - 1 else None)
                    for c in range(4):
                        act.wait_ge(s.r_w, 4 * n + c + 1)
                        a.do(act.activation(flat(sets[c].XT), ps[:, 2 * c, :], ACT.Copy, scale=-1.0), s.r_nw)
                    for step in range(2):
                        pair = (2 * step, 2 * step + 1)
                        for c in pair:
                            act.wait_ge(s.r_in2, 4 * n + c + 1)
                            if step or pr:
                                act.wait_ge(s.r_o, 4 * n + c - 1)
                            a.do(act.activation(flat(qE[c % 2]), ps[:, 2 * c, :], ACT.Exp), s.r_eb)
                        for c in pair:
                            act.wait_ge(s.r_vn, 4 * n + c + 1)
                            a.do(act.activation(flat(sets[c].T), ps[:, 2 * c + 1, :], ACT.Copy), s.r_vnc)

            def gdn_out(hg):
                act.wait_ge(s.r_state, 12 * hg + 12)
                for j in range(HG):
                    i = hg * HG + j
                    if j >= 2:
                        act.wait_ge(s.go_sum, i - 1)
                    a.do(act.activation(sq[j % 2], oT[:, j, :], ACT.Square), s.go_sq)
                    act.wait_ge(s.go_sum, i + 1)
                    if j >= 2:
                        act.wait_ge(s.go_n, i - 1)
                    for b, (c0, nn, _) in enumerate((XSET, CSET)):
                        a.do(act.activation(rt[j % 2][:, c0:c0 + nn], ps[:, b, 0:nn], ACT.Sqrt, bias=epsc, scale=1.0 / P), s.go_rt)
                    if j % 2:
                        act.wait_ge(s.w_used, USED[("gz", hg, j // 2)])
                    else:
                        act.wait_ge(s.go_z, i // 2 + 1)
                    if j >= 2:
                        act.wait_ge(s.go_o, i - 1)
                    for b, (c0, nn, _) in enumerate((XSET, CSET)):
                        a.do(act.activation(pre[j % 2][:, c0:c0 + nn], ps[:, 2 + b + 2 * (j % 2), 0:nn], ACT.Silu), s.go_sz)

            for hg in range(GH // HG):
                project(hg)
                recurrence(hg)
                gdn_out(hg)

            def load_router(l):
                act.dma_start(rw[:, l, :].rearrange("p (k e) -> p k e", k=KD),
                              A["router_w"][l].rearrange("(k p) e -> p k e", p=P)).then_inc(s.router_in, 16)

            def route(l):
                tiles = list(range(XT0 if l else 0, NT))
                act.wait_ge(s.sm_sub, l + 1)
                x = aff[:, tiles[0]:NT, :]
                a.do(act.activation(x, x, ACT.Exp), s.sm_exp)
                for i, (t, half) in enumerate([(t, half) for t in tiles for half in range(2)]):
                    act.wait_ge(s.ht_mm, 12 * l + i + 1)
                    parts = lead(t, half)
                    for first, count, high in parts:
                        a.do(act.activation(high, ps[:, 6 + i % 2, first * P:(first + count) * P].rearrange("p (m c) -> p m c", c=P), ACT.Copy), s.ht_lead)
                ns = (SLOTS, CAPX)[l]
                xs = xsT[:, 0:KD * NE * ns].rearrange("p (k e c) -> p k e c", k=KD, c=ns)
                i = (0, 24)[l]
                for m in range(KD):
                    for b in range(3 if l == 0 else 2):
                        act.wait_ge(s.ga_mm, i + 1)
                        bank = ps[:, (i - (0, 24)[l]) % 4, :]
                        if b < 2:
                            a.do(act.activation(xs[:, m, 8 * b:8 * b + 8, 0:CAPX], bank.rearrange("p (e c) -> p e c", c=CAPX), ACT.Copy), s.ga_copied)
                        else:
                            a.do(act.activation(xs[:, m, :, CAPX:ns], bank.rearrange("p (e c) -> p e c", c=CAPC), ACT.Copy), s.ga_copied)
                        i += 1
                for i in range(8 + (4 if l == 0 else 0)):
                    act.wait_ge(s.st_mm, (0, 12)[l] + i + 1)
                    if i < 8:
                        a.do(act.activation(selxT[:, i, :], ps[:, 6 + i % 2, :], ACT.Copy), s.st_copied)
                    else:
                        a.do(act.activation(selcT[:, i - 8, :], ps[:, 6 + i % 2, 0:CTX], ACT.Copy), s.st_copied)

            def experts(l):
                ns = (SLOTS, CAPX)[l]
                with act.Fori(0, NE // EB) as it:
                    for j in range(EB):
                        for c in range(4):
                            act.wait_ge(s.w_used, it * (12 * EB) + (MOE0[l] + 12 * j + 2 * c + 1))
                            act.wait_ge(s.gu_free, it * (4 * EB) + (4 * j + c + 1 + l * 66))
                            act.activation(sg[c % 2][:, 0:2 * ns], ps[:, c % 2, 0:2 * ns], ACT.Silu).then_inc(s.sg_ready, 1)
                        act.wait_ge(s.w_used, it * (12 * EB) + (MOE0[l] + 12 * j + 12))
                        act.wait_ge(s.sc_free, it * KD + (2 + l * 34))
                        y = ps[:, 4 + 2 * (j % 2):6 + 2 * (j % 2), :].rearrange("p a b -> p (a b)")
                        if l == 0:
                            act.activation(Yc[CAPC * j:CAPC * j + CAPC, :], y[CAPX:SLOTS, :], ACT.Copy)
                        act.activation(Yx[CAPX * (j % 2):CAPX * (j % 2) + CAPX, j // 2, :], y[0:CAPX, :], ACT.Copy).then_inc(s.y_free, 1)

            act.wait_ge(s.resid, RES_GDN)
            load_router(0)
            norm(1, MSETS[0], 0, 1)
            route(0)
            experts(0)

            def ssd_scalars():
                act.wait_ge(s.st_bias, 1)
                a.do(act.activation(s_A, col("salog", 0, 2 * SH), ACT.Exp))
                a.do(act.activation(s_tmp, s_dt, ACT.Abs))
                a.settle()
                a.do(act.activation(s_tmp, s_tmp, ACT.Exp, scale=-1.0))
                a.settle()
                a.do(act.activation(s_tmp, s_tmp, ACT.Ln, bias=onec), s.st_sp)
                act.wait_ge(s.sa_cols, 1)
                a.do(act.activation(s_te, s_te, ACT.Exp), s.sa_e)
                a.do(act.activation(s_etot, s_etot, ACT.Exp), s.sa_e)
                a.do(act.activation(s_tmp, s_a, ACT.Exp, scale=-1.0), s.sa_e)
                act.wait_ge(s.sr_mm, 1)
                for d in range(2):
                    a.do(act.activation(s_rows[32 * d:32 * d + 32, :], ps[32 * d:32 * d + 32, 5, :], ACT.Copy), s.sr_rows)

            def ssd_copy(g, i):
                if i == 0:
                    act.wait_ge(s.half_done, HALF["ssd"] + g + 1)
                else:
                    act.wait_ge(s.w_used, USED[(("sx", g), ("sx", g), ("sb", g), ("sc", g))[i]])
                if i >= 2 or g:
                    act.wait_ge(s.sp_conv, 4 * g + i - 1)
                p, b = s_pre[i % 2], 4 + 2 * (i % 2)
                a.do(act.activation(p[:, CTX + 2:N + 2], ps[:, b, :], ACT.Copy), s.sp_pre)
                if i < 3:
                    a.do(act.activation(p[:, 1:CTX + 1], ps[:, b + 1, 0:CTX], ACT.Copy), s.sp_pre)

            def ssd_silu(g, i):
                b = col("sconvb", (2 * g, 2 * g + 1, 16 + g, 24 + g)[i])
                act.wait_ge(s.sp_conv, 4 * g + i + 1)
                if i < 3:
                    a.do(act.activation(s_Bc if i == 2 else s_xT[:, i, 0:CTX], s_cv[i % 2][:, 0:CTX], ACT.Silu, bias=b), s.sp_act)
                elif g:
                    act.wait_ge(s.s_w, 8 * g)
                dst = s_xT[:, i, CTX:N] if i < 2 else s_B[g % 2] if i == 2 else s_C
                a.do(act.activation(dst, s_cv[i % 2][:, CTX + 1:N + 1], ACT.Silu, bias=b), s.sp_act)

            def ssd_tokens(g):
                if g in ADA_SSD:
                    ada_row(ADA_SSD[g])
                for t in range(NT):
                    act.wait_ge(s.str_mm, NT * g + t + 1)
                    a.do(act.activation(s_xtok[g % 2][:, t, :], ps[:, 4 + t % 4, 0:2 * P], ACT.Copy))
                    a.do(act.activation(s_Btok[g % 2][:, t, :], ps[:, 4 + t % 4, 2 * P:3 * P], ACT.Copy), s.str_out)

            def ssd_decays(g, st):
                nx = 4 * g + st - 2
                for d in range(2):
                    act.wait_ge(s.s_dm, 2 * nx + d + 1)
                    if nx:
                        act.wait_ge(s.s_y, 2 * (nx - 1) + d + 1)
                    a.do(act.activation(s_Ce[d].rearrange("p a b -> p (a b)"), ps[:, 2 * d, :], ACT.Exp), s.s_e)
                    for r in range(SR):
                        h = 32 * d + SR * g + r
                        x = s_D[d][:, r, :]
                        a.do(act.activation(x, x, ACT.Exp, bias=s_a[:, CHUNK_OF[d][st], h:h + 1]), s.s_d if r == SR - 1 else None)

            def ssd_groups():
                for i in range(4):
                    ssd_copy(0, i)
                    if i:
                        ssd_silu(0, i - 1)
                ssd_silu(0, 3)
                ssd_tokens(0)
                for g in range(SG):
                    for st in range(2, 6):
                        ssd_decays(g, st)
                        if g + 1 < SG:
                            if st > 2:
                                ssd_silu(g + 1, st - 3)
                            ssd_copy(g + 1, st - 2)
                    if g + 1 < SG:
                        ssd_silu(g + 1, 3)
                        ssd_tokens(g + 1)

            def ssd_out():
                for i in range(17):
                    if i < 16:
                        if i % 2:
                            act.wait_ge(s.w_used, USED[("sz", i // 2)])
                        else:
                            act.wait_ge(s.half_done, HALF["ssd_z"] + i // 2 + 1)
                        if i >= 2:
                            act.wait_ge(s.sz_u, i - 1)
                        a.do(act.activation(z_act[i % 2], ps[:, i % 4, :], ACT.Silu), s.sz_act)
                    if i >= 1:
                        j = i - 1
                        act.wait_ge(s.sz_u, j + 1)
                        if j >= 2:
                            act.wait_ge(s.sz_sum, j - 1)
                        a.do(act.activation(z_sq[j % 2], yT[:, j, :], ACT.Square), s.sz_sq)
                        a.do(act.activation(yT[:, j, :], yT[:, j, :], ACT.Copy, scale=col("snorm", j)), s.sz_n)
                act.wait_ge(s.sz_sum, 16)
                a.do(act.activation(z_rt, ps[:, 7, :], ACT.Sqrt, bias=epsc, scale=1.0 / SI), s.sz_rt)

            act.wait_ge(s.sc_free, 34)
            norm(2, (XSET, CSET), 1, 0)
            ssd_scalars()
            ssd_groups()
            ssd_out()
            act.wait_ge(s.resid, RES_SSD)
            load_router(1)
            norm(3, MSETS[1], 1, 1)
            route(1)
            experts(1)

            def values():
                for n in range(3):
                    act.wait_ge(s.w_used, USED[("bv", n)])
                    if n < 2:
                        a.do(act.activation(vS[:, n, :, :].rearrange("p a b -> p (a b)"), ps[:, n, :], ACT.Copy), s.bv_out)
                    else:
                        a.do(act.activation(ng.rearrange("p a b -> p (a b)"), ps[:, n, 0:4 * 3 * NH], ACT.Sigmoid), s.bv_out)

            def queries_keys():
                dst = [qT[:, j, :] for j in range(4)] + [kS, kW, kC, vC]
                for i in range(8):
                    act.wait_ge(s.w_used, USED[("bq", 1) if i < 4 else ("bk", i - 4)])
                    a.do(act.activation(dst[i], ps[:, i, :], ACT.Copy), s.bq_copy)
                for i in range(6):
                    if i >= 2:
                        act.wait_ge(s.bq_sum, i - 1)
                    else:
                        a.settle()
                    a.do(act.activation(bsq[i % 2], dst[i], ACT.Square), s.bq_sq)
                    act.wait_ge(s.bq_sum, i + 1)
                    if i >= 2:
                        act.wait_ge(s.bq_n, i - 1)
                    a.do(act.activation(brt[i % 2], ps[:, i % 2, :], ACT.Sqrt, bias=epsc, scale=1.0 / HD), s.bq_rt)

            def compress():
                for which in range(2):
                    act.wait_ge(s.w_used, USED[("c1", which, 1)])
                    a.do(act.activation(hrow[which], ps[0:2 * NCMP, 4 + which, 0:CW], ACT.Gelu_apprx_tanh), s.bc_act)
                for which in range(2):
                    act.wait_ge(s.bc_sum, which + 1)
                    a.do(act.activation(hidc[:, which, :, :].rearrange("p a b -> p (a b)"), ps[:, 6 + which, 0:4 * NCMP], ACT.Copy), s.bc_act)
                act.wait_ge(s.w_used, USED[("c2",)])
                a.do(act.activation(kcm, ps[:, 0, 0:NCMP], ACT.Copy), s.bc_act)
                a.do(act.activation(vcm[0:NCMP, :], ps[0:NCMP, 1, 0:P], ACT.Copy), s.bc_act)
                a.settle()
                a.do(act.activation(bsq[0][:, 0:NCMP], kcm, ACT.Square), s.bc_act)
                act.wait_ge(s.bc_sum, 3)
                act.wait_ge(s.bq_n, 6)
                a.do(act.activation(brt[0][:, 0:NCMP], ps[:, 2, 0:NCMP], ACT.Sqrt, bias=epsc, scale=1.0 / HD), s.bc_act)

            def attention():
                act.wait_ge(s.bc_vec, 4)
                a.do(act.activation(cP, cP, ACT.Exp), s.bc_act)
                for n in range(JOBS + 5):
                    if n < JOBS:
                        nk = (n // (2 * NH) + 1) * P
                        act.wait_ge(s.at_m, n + 1)
                        if n >= 4:
                            act.wait_ge(s.at_t, n - 3)
                        a.do(act.activation(Pb[n % 4][:, 0:nk], ps[:, n % 3, 0:nk], ACT.Exp, bias=anm[:, n:n + 1], accum_out=asum[:, n:n + 1]), s.at_e)
                    if n == 3:
                        act.wait_ge(s.ao_mm, 3)
                        a.do(act.activation(cPT, ps[:, 7, :], ACT.Copy), s.bc_act)
                    if 3 <= n < JOBS + 3:
                        m = n - 3
                        nk = (m // (2 * NH) + 1) * P
                        act.wait_ge(s.at_t, m + 1)
                        if m >= 2:
                            act.wait_ge(s.at_v, m - 1)
                        a.do(act.activation(PTb[m % 2][:, 0:nk], ps[:, 3 + m % 2, 0:nk], ACT.Copy), s.at_c)
                    if n >= 20 and (n - 20) % (2 * NH) == 0:
                        qt = (n - 20) // (2 * NH)
                        act.wait_ge(s.at_v, 2 * NH * (qt + 1))
                        a.do(act.activation(oA[:, :, qt * P:(qt + 1) * P], ps[:, 5 + qt % 2, :].rearrange("p (c q) -> p c q", c=4), ACT.Copy), s.ao_copy)

            def s5_prepare():
                act.dma_start(braw, A["s5b"].rearrange("x p a b -> p x a b")).then_inc(s.router_in, 16)
                act.dma_start(craw, A["s5c"].rearrange("x p a b -> p x a b")).then_inc(s.router_in, 16)
                a.do(act.activation(dt5, col("logdt", 0, NST), ACT.Exp), s.s5_act)
                act.wait_ge(s.s5_ang, 1)
                a.do(act.activation(r5, t5, ACT.Exp), s.s5_act)
                act.wait_ge(s.s5_ang, 2)
                a.do(act.activation(sk, fk, ACT.Sin, scale=TURN), s.s5_act)
                a.do(act.activation(ck, fr, ACT.Sin, scale=TURN), s.s5_act)

            def s5_input():
                for t in range(4):
                    act.wait_ge(s.w_used, USED[("bu", t // 2)])
                    a.do(act.activation(uT[:, t, :], ps[:, t, :], ACT.Copy), s.s5_u)

            def branches():
                for i in range(4):
                    if i % 2:
                        act.wait_ge(s.w_used, USED[("cb", i // 2)])
                    else:
                        act.wait_ge(s.half_done, HALF["conv"] + i // 2 + 1)
                    if i:
                        act.wait_ge(s.cv_out, i)
                    a.do(act.activation(ccs, ps[:, (3 * i) % 5, :], ACT.Copy), s.cv_cc)
                for m in range(KD):
                    for x in range(2):
                        act.wait_ge(s.w_used, USED[("mg", 1 + x, m)])
                        if m:
                            act.wait_ge(s.mg_mix, m)
                        a.do(act.activation(mact[x], ps[:, (12 + 4 * m + x) % 5, :], ACT.Sigmoid), s.mg_act)

            def mix():
                for t in range(4):
                    act.wait_ge(s.s5_yd, t + 1)
                    a.do(act.activation(yg[:, t, :], yg[:, t, :], ACT.Gelu_apprx_tanh), s.s5_gelu)
                for m in range(KD):
                    b = 3 * (m % 2)
                    for x, item in enumerate([("mg", 0, m), ("glu", m)]):
                        act.wait_ge(s.w_used, USED[item])
                        act.wait_ge(s.mg_mix, KD + m)
                        a.do(act.activation(mact[x], ps[:, b + 2 * x, :], ACT.Sigmoid), s.mg_act)

            def ffn():
                for i in range(FF2 // P):
                    if i % 2:
                        act.wait_ge(s.w_used, USED[("fu", i // 2)])
                    else:
                        act.wait_ge(s.half_done, HALF["ffn"] + i // 2 + 1)
                    if i >= 2:
                        act.wait_ge(s.ff_hid, H2 + KD - 1 + i)
                    a.do(act.activation(fact[i % 2], ps[:, 2 * (i % 2), :], ACT.Silu), s.ff_act)

            act.wait_ge(s.sc_free, 68)
            norm(4, (XSET,))
            act.wait_ge(s.nstt, 64)
            norm(5, (XSET,))
            act.wait_ge(s.nstt, 72)
            s5_prepare()
            values()
            queries_keys()
            compress()
            attention()
            s5_input()
            branches()
            mix()
            act.wait_ge(s.resid, RES_SSD + KD)
            norm(6, (XSET,))
            ffn()

        @block.vector
        def _(dve):
            v = Lane(dve, s.vec_steps)

            def ada_out(b):
                _, l, n = ADA[b][0]
                dve.wait_ge(s.ada_cols, b + 1)
                v.do(dve.tensor_tensor(ada[:, l, 2 * n:2 * n + 4, :], ps[:, 7, 0:8].rearrange("p (m v) -> p m v", m=4),
                                       col("ada_b", 48 * l + 2 * n, 4).unsqueeze(2).to_broadcast([P, 4, 2]), ALU.add), s.ada_copied)

            def ada_gains(l, w):
                v.settle()
                for vec in range(2):
                    v.do(dve.scalar_tensor_tensor(out=gs1[:, l, w, :].rearrange("p (k v) -> p k v", v=2)[:, :, vec],
                                                  in0=ada[:, l, 24 * w + 8:24 * w + 16, vec], scalar=1.0,
                                                  in1=col(("norm1", "norm2")[w], 8 * l, 8), op0=ALU.add, op1=ALU.mult))
                v.settle()

            def norm(call, sets, gain, dst):
                dve.wait_ge(s.nrt, nrt0[call] + len(sets))
                for j, (c0, nn, _) in enumerate(sets):
                    v.do(dve.reciprocal(nrsb[:, c0:c0 + nn], nrtb[:, c0:c0 + nn]))
                v.settle()
                for k in range(KD):
                    for j, (c0, nn, vec) in enumerate(sets):
                        v.do(dve.scalar_tensor_tensor(out=dst[:, k, c0:c0 + nn], in0=RT[:, k, c0:c0 + nn],
                                                      scalar=gain(k, vec), in1=nrsb[:, c0:c0 + nn],
                                                      op0=ALU.mult, op1=ALU.mult), s.nstt)

            dve.wait_ge(s.const_in, 32)
            for b in range(ADA_FIRST):
                ada_out(b)
            ada_gains(0, 0)
            norm(0, (XSET, CSET), lambda k, vec: gs1[:, 0, 0, 2 * k + vec:2 * k + vec + 1], hT)

            dve.wait_ge(s.w_used, USED[("gtail",)])
            v.do(dve.tensor_copy(betag[:, :, 0:16], ps[:, 6, 0:32 * NT].rearrange("p (t c) -> p t c", c=32)[:, :, 0:16]))
            v.do(dve.tensor_tensor(betag[:, :, 16:32], ps[:, 6, 0:32 * NT].rearrange("p (t c) -> p t c", c=32)[:, :, 16:32],
                                   col("gdtb", 0, 16).unsqueeze(1).to_broadcast([P, NT, 16]), ALU.add), s.gt_bias)
            dve.wait_ge(s.gt_act, 1)
            v.settle()
            v.do(dve.scalar_tensor_tensor(out=gsp, in0=betag[:, :, 16:32], scalar=0.0, in1=gtmp, op0=ALU.max, op1=ALU.add))
            v.settle()
            v.do(dve.scalar_tensor_tensor(out=gsp, in0=gsp, scalar=-1.0, in1=ea.unsqueeze(1).to_broadcast([P, NT, 16]),
                                          op0=ALU.mult, op1=ALU.mult), s.gt_g)
            dve.wait_ge(s.gc_mm, 1)
            v.do(dve.tensor_copy(gcum, ps[:, 5, 0:16 * NT].rearrange("p (t c) -> p t c", c=16)), s.gc_cols)
            v.settle()
            v.do(dve.tensor_scalar(ngc, gcum, -1.0, None, ALU.mult))
            dve.wait_ge(s.gt_act, 2)
            v.do(dve.tensor_tensor(beg, beg, beta, ALU.mult))
            dve.wait_ge(s.mask_done, MASKS)
            dve.wait_ge(s.level_masks, 2 * LEVELS)
            for d in range(2):
                for l in range(LEVELS):
                    v.do(dve.tensor_reduce(rmask[:, d, l:l + 1], bmask[:, 1 - d, l, :], AX.X, ALU.max, negate=True))

            def project(hg):
                for p in pre:
                    for c in (0, CTX + 1, N + 2):
                        if hg == 1 and c == 0 and p is pre[0]:
                            dve.wait_ge(s.go_o, HG)
                        v.do(dve.memset(p[:, c:c + 1], 0.0))
                v.settle()
                for i in range(14):
                    if i < 12:
                        ch = (i // 4) * 8 + hg * HG + i % 4
                        dve.wait_ge(s.gp_pre, 2 * (12 * hg + i + 1))
                        if i >= 3:
                            dve.wait_ge(s.gp_act, 2 * (12 * hg + i - 2))
                        p, c = pre[i % 2], cv[i % 3]
                        w = [col("gconv", 3 * ch + t) for t in range(3)]
                        v.do(dve.tensor_scalar(c, p[:, 1:N + 2], w[1], None, ALU.mult))
                        v.settle()
                        v.do(dve.scalar_tensor_tensor(out=c, in0=p[:, 0:N + 1], scalar=w[0], in1=c, op0=ALU.mult, op1=ALU.add))
                        v.settle()
                        v.do(dve.scalar_tensor_tensor(out=c, in0=p[:, 2:N + 3], scalar=w[2], in1=c, op0=ALU.mult, op1=ALU.add), s.gp_conv)
                    if i in ADA_GDN[hg] and ADA_GDN[hg][i] > ADA_GDN[hg][1]:
                        ada_out(ADA_GDN[hg][i] - 1)
                    if 2 <= i < 10:
                        t = i - 2
                        dve.wait_ge(s.gp_rt, 2 * (8 * hg + t + 1))
                        r = rt[t % 2]
                        dst = qkv[t // 4][:, t % 4, :]
                        v.do(dve.reciprocal(r, r))
                        v.settle()
                        scale = float(P) ** -0.5 if t < 4 else 1.0
                        v.do(dve.scalar_tensor_tensor(out=dst, in0=dst, scalar=scale, in1=r, op0=ALU.mult, op1=ALU.mult), s.gp_norm)
                ada_out(max(ADA_GDN[hg].values()))

            def bc(colap, n=P):
                return colap.unsqueeze(2).to_broadcast([P, HG, n])

            def recurrence(hg):
                q, k_, vv = qkv
                dve.wait_ge(s.gp_act, 24 * hg + 24)
                v.do(dve.memset(oT, 0.0))
                for d in range(2):
                    v.do(dve.memset(S[d], 0.0))
                for z in sets:
                    v.do(dve.memset(z.Y, 0.0))
                for pr in range(3):
                    n = hg * 3 + pr
                    tile = [CHUNK_OF[c % 2][2 * pr + c // 2] for c in range(4)]
                    cs = [slice(t * P, t * P + P) for t in tile]
                    last = lambda c: (P - 1, 0)[c % 2]
                    g3 = lambda c, b: ps[:, 2 * c + b, :].rearrange("p (j i) -> p j i", i=P)
                    for c in range(4):
                        dve.wait_ge(s.r_in, 4 * n + c + 1)
                        v.do(dve.tensor_tensor(sets[c].T, g3(c, 0), negm[:, c % 2, :].unsqueeze(1).to_broadcast([P, HG, P]), ALU.add), s.r_dm)
                    for c in range(4):
                        z = sets[c]
                        dve.wait_ge(s.r_d, 4 * n + c + 1)
                        v.do(dve.tensor_tensor(z.XT, g3(c, 1), z.T, ALU.mult), s.r_kk)
                        v.do(dve.tensor_copy(kcol[:, c, :], z.T[:, :, last(c)]))
                    for c in range(4):
                        z = sets[c]
                        dve.wait_ge(s.r_kq, 4 * n + c + 1)
                        v.do(dve.tensor_tensor(z.A, g3(c, 0), z.T, ALU.mult))
                        v.do(dve.tensor_copy(z.U, ident.unsqueeze(1).to_broadcast([P, HG, P])))
                        v.settle()
                        v.do(dve.tensor_copy(z.T, ident.unsqueeze(1).to_broadcast([P, HG, P])))
                        dve.wait_ge(s.r_bt, 4 * n + c + 1)
                        v.do(dve.tensor_tensor(z.XT, g3(c, 1), z.XT, ALU.mult), s.r_xt)
                    for l in range(LEVELS):
                        b = 1 << l

                        def half(x, odd):
                            return x.rearrange("p j (n two b) -> p (j n) two b", two=2, b=b)[:, :, odd, :]

                        def bank(c, i, odd):
                            return ps[:, 2 * c + i, :].rearrange("p (n two b) -> p n two b", two=2, b=b)[:, :, odd, :]

                        def part(x, odd):
                            return x.rearrange("p j (n two b) -> p j n two b", two=2, b=b)[:, :, :, odd, :]

                        def block(d):
                            return bmask[:, d, l, :].rearrange("p (n b) -> p n b", b=b).unsqueeze(1).to_broadcast([P, HG, 64 // b, b])

                        if l == 0:
                            v.settle()
                            for c in range(4):
                                z, d = sets[c], c % 2
                                v.do(dve.tensor_tensor(part(z.Y, 1 - d), part(z.XT, 1 - d), block(1 - d), ALU.mult))
                            v.settle()
                            for c in range(4):
                                z, d = sets[c], c % 2
                                v.do(dve.tensor_tensor(half(z.U, 1 - d), half(z.U, 1 - d), half(z.Y, 1 - d), ALU.subtract))
                        for c in range(4):
                            d = c % 2
                            dve.wait_ge(s.r_y, 4 * (LEVELS * n + l) + c + 1)
                            v.do(dve.tensor_tensor(part(sets[c].Y, d), part(g3(c, 0), d), block(d), ALU.mult), s.r_ym if l > 0 else None)
                        if l == 0:
                            v.settle()
                            for c in range(4):
                                z, d = sets[c], c % 2
                                v.do(dve.tensor_tensor(half(z.T, d), half(z.T, d), half(z.Y, d), ALU.subtract), s.r_l)
                            continue
                        for c in range(4):
                            z, d = sets[c], c % 2
                            dve.wait_ge(s.r_tu, 4 * ((LEVELS - 1) * n + l - 1) + c + 1)
                            if l < LEVELS - 1:
                                v.do(dve.tensor_tensor(half(z.T, d), half(z.T, d), bank(c, 1, d), ALU.subtract))
                            v.do(dve.scalar_tensor_tensor(out=half(z.U, 1 - d), in0=bank(c, 0, 1 - d), scalar=rmask[:, d, l:l + 1],
                                                          in1=half(z.U, 1 - d), op0=ALU.mult, op1=ALU.add), s.r_l)
                    for c in range(4):
                        z = sets[c]
                        i = 8 * (c % 2) + hg * HG
                        dve.wait_ge(s.r_kv, 4 * n + c + 1)
                        v.do(dve.tensor_tensor(z.XT, g3(c, 0), bc(beg[:, tile[c], i:i + HG]), ALU.mult))
                        v.do(dve.tensor_tensor(z.Y, g3(c, 0), bc(kcol[:, c, :]), ALU.mult))
                        v.do(dve.tensor_tensor(z.T, g3(c, 1), bc(beta[:, tile[c], i:i + HG]), ALU.mult), s.r_kvs)
                    for step in range(2):
                        pair = (2 * step, 2 * step + 1)
                        for c in pair:
                            dve.wait_ge(s.r_eb, 4 * n + c + 1)
                            v.do(dve.tensor_copy(el[:, c % 2, :], qE[c % 2][:, :, last(c)]))
                            v.settle()
                            v.do(dve.tensor_tensor(qE[c % 2], q[:, :, cs[c]], qE[c % 2], ALU.mult), s.r_q)
                        for c in pair:
                            d = c % 2
                            dve.wait_ge(s.r_o, 4 * n + c + 1)
                            v.do(dve.tensor_tensor(S[d], S[d], bc(el[:, d, :]), ALU.mult))
                            v.do(dve.tensor_tensor(oT[:, :, cs[c]], oT[:, :, cs[c]], g3(c, 0), ALU.add))
                            v.settle()
                            v.do(dve.tensor_tensor(S[d], S[d], g3(c, 1), ALU.add), s.r_state)

            def gdn_out(hg):
                for j in range(HG):
                    i = hg * HG + j
                    dve.wait_ge(s.go_rt, 2 * (i + 1))
                    r = rt[j % 2]
                    v.do(dve.reciprocal(r, r))
                    v.settle()
                    v.do(dve.scalar_tensor_tensor(out=oT[:, j, :], in0=oT[:, j, :], scalar=col("gnorm"), in1=r,
                                                  op0=ALU.mult, op1=ALU.mult), s.go_n)
                    v.settle()
                    dve.wait_ge(s.go_sz, 2 * (i + 1))
                    v.do(dve.tensor_tensor(oT[:, j, :], oT[:, j, :], pre[j % 2][:, 0:N], ALU.mult), s.go_o)
                for m in range(KD):
                    i = hg * KD + m
                    if m == KD - 1:
                        dve.wait_ge(s.w_used, USED[("gout", hg, 1)])
                    else:
                        dve.wait_ge(s.go_mm, (KD - 1) * hg + m + 1)
                    for b, (c0, nn, vec) in enumerate((XSET, CSET)):
                        x = RT[:, m, c0:c0 + nn]
                        v.do(dve.scalar_tensor_tensor(out=x, in0=ps[:, b + 2 * (m % 2), 0:nn], scalar=ada[:, 0, 16 + m, vec:vec + 1],
                                                      in1=x, op0=ALU.mult, op1=ALU.add), s.resid)

            for hg in range(GH // HG):
                project(hg)
                recurrence(hg)
                gdn_out(hg)
            ada_gains(0, 1)
            ada_gains(1, 0)

            def route(l):
                tiles = list(range(XT0 if l else 0, NT))
                t0, nt = tiles[0], len(tiles)
                x = aff[:, t0:NT, :]
                bcast = smx[:, t0:NT].unsqueeze(2).to_broadcast([P, nt, NE])
                lg = ps[:, 2, NE * t0:NE * NT].rearrange("p (t e) -> p t e", e=NE)
                dve.wait_ge(s.lg_mm, l + 1)
                v.do(dve.tensor_reduce(smx[:, t0:NT], lg, AX.X, ALU.max))
                v.settle()
                v.do(dve.tensor_tensor(x, lg, bcast, ALU.subtract), s.sm_sub)
                dve.wait_ge(s.sm_exp, l + 1)
                v.do(dve.tensor_reduce(smx[:, t0:NT], x, AX.X, ALU.add))
                v.settle()
                v.do(dve.reciprocal(smx[:, t0:NT], smx[:, t0:NT]))
                v.settle()
                v.do(dve.tensor_tensor(x, x, bcast, ALU.mult), s.aff_ready)
                for i, (t, half) in enumerate([(t, half) for t in tiles for half in range(2)]):
                    dve.wait_ge(s.ht_lead, 18 * l + i + 1 + (i + 1) // 2)
                    parts = lead(t, half)
                    for first, count, high in parts:
                        at = (4 * half + first) * P
                        v.do(dve.tensor_tensor(h_lo[t][:, at:at + count * P].rearrange("p (m c) -> p m c", c=P),
                                               ps[:, 6 + i % 2, first * P:(first + count) * P].rearrange("p (m c) -> p m c", c=P), high.bitcast(F32), ALU.subtract),
                             s.ht_copied if first + count == 4 else None)
                dve.wait_ge(s.afft_mm, l + 1)
                for c0, nn, vec in MSETS[l]:
                    cap, bank = (CAPX, CAPC)[vec], 3 + vec
                    w, r = affT[0:NE, c0:c0 + nn], rank[0:NE, c0:c0 + nn]
                    v.do(dve.tensor_copy(w, ps[0:NE, bank, 0:nn]))
                    v.settle()
                    for _ in range(cap // 8):
                        v.do(dve.max(top8[0:NE, :], w))
                        v.settle()
                        v.do(dve.match_replace(w, top8[0:NE, :], w, -1.0))
                        v.settle()
                    v.do(dve.tensor_scalar(w, w, 0.0, None, ALU.is_lt))
                    v.settle()
                    v.do(dve.tensor_tensor_scan(r, ones[0:NE, 0:1].to_broadcast([NE, nn]), w, 0.0, ALU.mult, ALU.add))
                    v.settle()
                    v.do(dve.tensor_tensor(r, r, w, ALU.mult))
                    v.settle()
                    v.do(dve.tensor_scalar(r, r, -1.0, None, ALU.add), s.posm_ready)
                dve.wait_ge(s.post_mm, l + 1)
                v.do(dve.tensor_copy(post[:, t0:NT, :], ps[:, 5, NE * t0:NE * NT].rearrange("p (t e) -> p t e", e=NE)))
                dve.wait_ge(s.mask_done, MASKS + 1 + l)
                v.settle()

                def selection(t):
                    cap = CAPX if t >= XT0 else CAPC
                    m = selx[:, t - XT0, :] if t >= XT0 else selc[:, t, :]
                    return m.rearrange("p (e c) -> p e c", c=cap), cap

                for t in tiles:
                    cap = selection(t)[1]
                    m = sel_r[t][:, :].rearrange("p (e c) -> p e c", c=cap)
                    v.do(dve.tensor_tensor(m, iota[:, 0:cap].unsqueeze(1).to_broadcast([P, NE, cap]),
                                           post[:, t, :].unsqueeze(2).to_broadcast([P, NE, cap]), ALU.is_equal), s.sel_ready)
                dve.wait_ge(s.ga_mm, GA[l])
                for t in tiles:
                    m, cap = selection(t)
                    picked = sel_r[t][:, :].bitcast(F32).rearrange("p (e c) -> p e c", c=cap)
                    v.do(dve.tensor_tensor(m, picked, aff[:, t, :].unsqueeze(2).to_broadcast([P, NE, cap]), ALU.mult), s.selg_ready)

            def experts(l):
                ns = (SLOTS, CAPX)[l]
                for i, sem in enumerate((s.gu_free, s.gu_free, s.y_free, s.y_free, s.sc_free, s.sc_free)):
                    dve.memset(top8[:, i:i + 1], 0.0).then_inc(sem, 1)
                h3 = hid[:, 0:KD * ns].rearrange("p (k e) -> p (k e)", k=KD)
                with dve.Fori(0, NE // EB) as it:
                    for j in range(EB):
                        for c in range(4):
                            dve.wait_ge(s.w_used, it * (12 * EB) + (MOE0[l] + 12 * j + 2 * c + 2))
                            dve.wait_ge(s.sg_ready, it * (4 * EB) + (4 * j + c + 1 + l * 64))
                            dve.tensor_tensor(hid[:, 2 * c * ns:(2 * c + 2) * ns], sg[c % 2][:, 0:2 * ns], ps[:, 2 + c % 2, 0:2 * ns],
                                              ALU.mult).then_inc(s.gu_free, 1)
                    for m in range(KD):
                        dve.wait_ge(s.sc_mm, it * KD + (m + 1 + l * 32))
                        sets = MSETS[l]
                        for i, (c0, nn, vec) in enumerate(sets):
                            x = RT[:, m, c0:c0 + nn]
                            ins = dve.scalar_tensor_tensor(out=x, in0=ps[:, (m % 2) + 2 * vec, 0:nn], scalar=ada[:, l, 40 + m, vec:vec + 1], in1=x,
                                                           op0=ALU.mult, op1=ALU.add)
                        ins.then_inc(s.sc_free, 1)

            norm(1, MSETS[0], lambda k, vec: gs1[:, 0, 1, 2 * k + vec:2 * k + vec + 1], hT)
            route(0)
            experts(0)

            def over(x):
                return x.unsqueeze(2).to_broadcast([P, SR, SP_])

            def ssd_scalars():
                x3 = lambda b: ps[:, b, 0:64 * NT].rearrange("p (t h) -> p t h", t=NT)
                dve.wait_ge(s.w_used, USED[("stail", 1)])
                v.do(dve.tensor_tensor(s_dt, x3(2), col("sdtb", 0, 64).unsqueeze(1).to_broadcast([P, NT, 64]), ALU.add), s.st_bias)
                dve.wait_ge(s.st_sp, 1)
                v.settle()
                v.do(dve.scalar_tensor_tensor(out=s_dt, in0=s_dt, scalar=0.0, in1=s_tmp, op0=ALU.max, op1=ALU.add))
                v.settle()
                v.do(dve.scalar_tensor_tensor(out=s_a, in0=s_dt, scalar=-1.0, in1=s_A.unsqueeze(1).to_broadcast([P, NT, 64]),
                                              op0=ALU.mult, op1=ALU.mult), s.st_a)
                dve.wait_ge(s.sa_mm, 1)
                dve.wait_ge(s.sr_mm, 1)
                v.do(dve.tensor_scalar(s_a, x3(3), -1.0, None, ALU.mult))
                v.settle()
                v.do(dve.tensor_tensor(s_te, x3(4), s_a, ALU.add))
                v.do(dve.tensor_copy(s_etot, x3(4)), s.sa_cols)
                dve.wait_ge(s.sa_e, 3)
                v.do(dve.tensor_tensor(s_te, s_te, s_dt, ALU.mult))
                for p in s_pre:
                    for c in (0, CTX + 1, N + 2):
                        v.do(dve.memset(p[:, c:c + 1], 0.0))
                v.settle()

            def ssd_conv(g, i):
                ch = (2 * g, 2 * g + 1, 16 + g, 24 + g)[i]
                c0 = 0 if i < 3 else CTX + 1
                dve.wait_ge(s.sp_pre, TILES * g + AFTER[i])
                if i >= 2 or g:
                    dve.wait_ge(s.sp_act, TILES * g + ((-1, 0)[i] if i < 2 else AFTER[i - 2]))
                p, c = s_pre[i % 2], s_cv[i % 2]
                w = [col("sconv", 3 * ch + t) for t in range(3)]
                o = c[:, c0:N + 1]
                v.do(dve.tensor_scalar(o, p[:, c0 + 1:N + 2], w[1], None, ALU.mult))
                v.settle()
                v.do(dve.scalar_tensor_tensor(out=o, in0=p[:, c0:N + 1], scalar=w[0], in1=o, op0=ALU.mult, op1=ALU.add))
                v.settle()
                v.do(dve.scalar_tensor_tensor(out=o, in0=p[:, c0 + 2:N + 3], scalar=w[2], in1=o, op0=ALU.mult, op1=ALU.add), s.sp_conv)

            def ssd_own(g):
                dve.wait_ge(s.sp_act, TILES * g + 4)
                for i in range(2):
                    v.do(dve.tensor_scalar(yT[:, 2 * g + i, :], s_xT[:, i, CTX:N], col("sd", 2 * g + i), None, ALU.mult))

            def ssd_step(g, st):
                tile = [CHUNK_OF[d][st] for d in range(2)]
                hs = [slice(32 * d + SR * g, 32 * d + SR * g + SR) for d in range(2)]
                nx, ns = 4 * g + st - 2, 5 * g + st
                xt = [s_xtok[g % 2][:, t, :].rearrange("p (r c) -> p r c", r=SR) for t in tile]
                if st >= 2:
                    for d in range(2):
                        v.do(dve.tensor_tensor(s_xdt[d], xt[d], over(s_dt[:, tile[d], hs[d]]), ALU.mult))
                        dve.wait_ge(s.s_in, 2 * nx + d + 1)
                        v.do(dve.tensor_tensor(s_D[d], ps[:, 2 * d, :].rearrange("p (r i) -> p r i", i=P),
                                               negm[:, d, :].unsqueeze(1).to_broadcast([P, SR, P]), ALU.add), s.s_dm)
                    for d in range(2):
                        cx = slice((tile[d] - XT0) * P, (tile[d] - XT0 + 1) * P)
                        dve.wait_ge(s.s_e, 2 * nx + d + 1)
                        v.do(dve.tensor_tensor(s_Ce[d], s_Ce[d], s_C[:, cx].unsqueeze(1).to_broadcast([P, SR, P]), ALU.mult))
                        dve.wait_ge(s.s_d, 2 * nx + d + 1)
                        v.do(dve.tensor_tensor(s_D[d], s_D[d], ps[:, 2 * d + 1, 0:P].unsqueeze(1).to_broadcast([P, SR, P]), ALU.mult), s.s_w)
                if st < 5:
                    for d in range(2):
                        v.do(dve.tensor_tensor(s_xe[d], xt[d], over(s_te[:, tile[d], hs[d]]), ALU.mult), s.s_xend)
                if st >= 3 and g + 1 < SG:
                    ssd_conv(g + 1, st - 3)
                if st >= 2:
                    for d in range(2):
                        y = yT[:, 2 * g:2 * g + 2, (tile[d] - XT0) * P:(tile[d] - XT0 + 1) * P]
                        dve.wait_ge(s.s_y, 2 * nx + d + 1)
                        if d:
                            v.settle()
                        v.do(dve.tensor_tensor(y, y, ps[:, 2 * d, 0:2 * P].rearrange("p (a i) -> p a i", a=2), ALU.add), s.s_yacc)
                if st < 5:
                    for d in range(2):
                        h = s_h[:, d, :].rearrange("p (r c) -> p r c", r=SR)
                        dve.wait_ge(s.s_st, 2 * ns + d + 1)
                        v.do(dve.tensor_tensor(h, h, over(s_etot[:, tile[d], hs[d]]), ALU.mult))
                        v.settle()
                        v.do(dve.tensor_tensor(h, h, ps[:, 2 * d + 1, 256:512].rearrange("p (r c) -> p r c", r=SR), ALU.add), s.s_state)

            def ssd_groups():
                for i in range(4):
                    ssd_conv(0, i)
                ssd_own(0)
                for g in range(SG):
                    v.settle()
                    v.do(dve.memset(s_h, 0.0))
                    dve.wait_ge(s.str_out, NT * (g + 1))
                    v.settle()
                    ssd_step(g, 0)
                    ssd_step(g, 1)
                    if g in ADA_SSD:
                        ada_out(ADA_SSD[g])
                    for st in range(2, 6):
                        ssd_step(g, st)
                    if g + 1 < SG:
                        ssd_conv(g + 1, 3)
                        ssd_own(g + 1)

            def split(whole, high, low, sem):
                v.do(dve.tensor_copy(high, whole))
                v.settle()
                v.do(dve.tensor_tensor(low, whole, high.bitcast(F32), ALU.subtract), sem)

            def ssd_out():
                def split_y(i):
                    dve.wait_ge(s.sz_n, i + 1)
                    split(yT[:, i, :], tile_of(y_hi, i), tile_of(y_lo, i), s.ff_hid)

                def split_w(m):
                    item = ("sout", m)
                    dve.wait_ge(w_ready[place(item)], 16 * FILLED[item])
                    if m >= 1:
                        dve.wait_ge(s.w_used, USED[("sout", m - 4)] if m >= 4 else USED[("sz", SI // CW - 1)])
                    split(slot_view(place(item), shape_of(item)), *halves(item), s.w_split)

                v.settle()
                for i in range(16):
                    dve.wait_ge(s.sz_act, i + 1)
                    v.do(dve.tensor_tensor(yT[:, i, :], yT[:, i, :], z_act[i % 2], ALU.mult), s.sz_u)
                    if i >= 2:
                        split_y(i - 2)
                split_w(0)
                split_y(14)
                split_y(15)
                split_w(1)
                dve.wait_ge(s.sz_rt, 1)
                v.do(dve.reciprocal(z_rs, z_rt))
                v.settle()
                for m in range(KD):
                    if m + 2 < KD:
                        split_w(m + 2)
                    dve.wait_ge(s.w_used, USED[("sout", m)])
                    v.do(dve.tensor_tensor(z_tmp[m % 2], ps[:, m % 2, :], z_rs, ALU.mult))
                    v.settle()
                    x = RT[:, m, CTX:N]
                    v.do(dve.scalar_tensor_tensor(out=x, in0=z_tmp[m % 2], scalar=ada[:, 1, 16 + m, 0:1], in1=x,
                                                  op0=ALU.mult, op1=ALU.add), s.resid)

            norm(2, (XSET, CSET), lambda k, vec: gs1[:, 1, 0, 2 * k + vec:2 * k + vec + 1], hT)
            ssd_scalars()
            ssd_groups()
            ssd_out()
            ada_gains(1, 1)
            norm(3, MSETS[1], lambda k, vec: gs1[:, 1, 1, 2 * k + vec:2 * k + vec + 1], hT)
            route(1)
            experts(1)

            def norm2(call, gain, dst):
                dve.wait_ge(s.nrt, nrt0[call] + 1)
                v.do(dve.reciprocal(nrsb[:, CTX:N], nrtb[:, CTX:N]))
                v.settle()
                for k in range(KD):
                    v.do(dve.scalar_tensor_tensor(out=dst(k), in0=RT[:, k, CTX:N], scalar=col(gain, k), in1=nrsb[:, CTX:N],
                                                  op0=ALU.mult, op1=ALU.mult), s.nstt)

            def tt(out, a_, b_, op, sem=None):
                v.do(dve.tensor_tensor(out, a_, b_, op), sem)

            def ts(out, a_, c1, op0, c2=None, op1=None):
                if op1 is None:
                    v.do(dve.tensor_scalar(out, a_, c1, None, op0))
                else:
                    v.do(dve.tensor_scalar(out, a_, c1, c2, op0, op1))

            def s5_prepare():
                re, im = col("lamre", 0, NST), col("lamim", 0, NST)
                dve.wait_ge(s.s5_act, 1)
                tt(f5, im, dt5, ALU.mult)
                tt(t5, re, dt5, ALU.mult, s.s5_ang)
                v.settle()
                ts(f5, f5, 1.0 / (2.0 * np.pi), ALU.mult)
                v.settle()
                ts(den5, f5, ROUND, ALU.add)
                v.settle()
                ts(den5, den5, -ROUND, ALU.add)
                v.settle()
                tt(f5, f5, den5, ALU.subtract)
                v.settle()
                for k in range(9):
                    ts(fk[:, k, :], f5, float(1 << k), ALU.mult)
                v.settle()
                ts(fr, fk, ROUND, ALU.add)
                v.settle()
                ts(fr, fr, -ROUND, ALU.add)
                v.settle()
                tt(fk, fk, fr, ALU.subtract)
                v.settle()
                ts(fr, fk, 0.25, ALU.add)
                v.settle()
                ts(ck, fr, ROUND, ALU.add)
                v.settle()
                ts(ck, ck, -ROUND, ALU.add)
                v.settle()
                tt(fr, fr, ck, ALU.subtract, s.s5_ang)
                dve.wait_ge(s.s5_act, 2)
                dve.wait_ge(s.s5_act, 4)
                tt(nr5, r5, ck[:, 0, :], ALU.mult)
                tt(ni5, r5, sk[:, 0, :], ALU.mult)
                tt(den5, re, re, ALU.mult)
                tt(t5, im, im, ALU.mult)
                v.settle()
                tt(den5, den5, t5, ALU.add)
                ts(nr5, nr5, -1.0, ALU.add)
                v.settle()
                v.do(dve.reciprocal(den5, den5))
                tt(kr5, nr5, re, ALU.mult)
                tt(t5, ni5, im, ALU.mult)
                v.settle()
                tt(kr5, kr5, t5, ALU.add)
                v.settle()
                tt(kr5, kr5, den5, ALU.mult)
                tt(ki5, ni5, re, ALU.mult)
                tt(t5, nr5, im, ALU.mult)
                v.settle()
                tt(ki5, ki5, t5, ALU.subtract)
                v.settle()
                tt(ki5, ki5, den5, ALU.mult)
                v.settle()
                dve.wait_ge(s.router_in, 64)
                kr = kr5.unsqueeze(2).to_broadcast([P, NST, 16])
                ki = ki5.unsqueeze(2).to_broadcast([P, NST, 16])
                v.do(dve.tensor_reduce(parb, ident.rearrange("p (n two c) -> p two n c", two=2, c=16), AX.XY, ALU.add))
                v.settle()

                def blocks(out, x, par):
                    for y in range(2):
                        v.do(dve.tensor_scalar(out[:, :, y, :], x, par[:, y:y + 1], None, ALU.mult))

                for x in range(2):
                    blocks(Bbd[:, x, :, :].rearrange("p t (two c) -> p t two c", two=2), braw[:, x, :, :], parb)
                for x, (f1, f2) in enumerate(((kr, ki), (ki, kr))):
                    v.settle()
                    tt(c1t, craw[:, 0, :, :], f1, ALU.mult)
                    tt(c2t, craw[:, 1, :, :], f2, ALU.mult)
                    v.settle()
                    if x == 0:
                        tt(c1t, c1t, c2t, ALU.subtract)
                    else:
                        v.do(dve.scalar_tensor_tensor(out=c1t, in0=c1t, scalar=-1.0, in1=c2t, op0=ALU.mult, op1=ALU.subtract))
                    v.settle()
                    blocks(Cbd[:, x, :, :].rearrange("p t (two c) -> p t two c", two=2), c1t, parc)
                v.settle()
                v.do(dve.memset(t5, 0.0), s.s5_ang)

            def queries_keys():
                ts(qg, col("qn"), HD ** -0.5, ALU.mult)
                v.settle()
                gains = [qg] * 4 + [col("kn", 1), col("kn", 2)]
                dve.wait_ge(s.bq_copy, 8)
                for which, x in enumerate((kC, vC)):
                    y = x.rearrange("p (b i) -> p b i", i=CMPB // 2)
                    tt(y, y, col("pe", CMPB // 2 * which, CMPB // 2).unsqueeze(1).to_broadcast([P, 2 * NCMP, CMPB // 2]), ALU.add, s.bc_vec)
                dst = [qT[:, j, :] for j in range(4)] + [kS, kW]
                for i in range(6):
                    dve.wait_ge(s.bq_rt, i + 1)
                    r = brt[i % 2]
                    v.do(dve.reciprocal(r, r))
                    v.settle()
                    v.do(dve.scalar_tensor_tensor(out=dst[i], in0=dst[i], scalar=gains[i], in1=r, op0=ALU.mult, op1=ALU.mult), s.bq_n)

            def compress():
                tt(cRep.rearrange("p (h c) -> p h c", h=NH), ident[0:NCMP, 0:NCMP].unsqueeze(1).to_broadcast([NCMP, NH, NCMP]),
                   ident[0:NCMP, 0:NCMP].unsqueeze(1).to_broadcast([NCMP, NH, NCMP]), ALU.mult)
                v.do(dve.tensor_reduce(cHead, ident.rearrange("p (h c) -> p h c", h=NH), AX.X, ALU.max))
                dve.wait_ge(s.bc_act, 8)
                r = brt[0][:, 0:NCMP]
                v.do(dve.reciprocal(r, r))
                v.settle()
                v.do(dve.scalar_tensor_tensor(out=kcm, in0=kcm, scalar=col("kn", 0), in1=r, op0=ALU.mult, op1=ALU.mult), s.bc_vec)

            def attention():
                w = cP.rearrange("p (q h c) -> p q h c", q=4, h=NH)
                rows = cP.rearrange("p (u c) -> p u c", c=NCMP)
                over_ = lambda x: x.unsqueeze(2).to_broadcast([P, 4 * NH, NCMP])
                cm, csum = anm[:, JOBS:96], asum[:, JOBS:96]
                dve.wait_ge(s.ao_mm, 1)
                for q in range(4):
                    for g in range(2):
                        tt(w[:, q, 4 * g:4 * g + 4], ps[:, (7, 4)[g], 64 * q:64 * (q + 1)].rearrange("p (h c) -> p h c", h=4),
                           cmask[:, q, :].unsqueeze(1).to_broadcast([P, 4, NCMP]), ALU.add)
                v.settle()
                v.do(dve.tensor_reduce(cm, rows, AX.X, ALU.max, negate=True))
                v.settle()
                ts(cm, cm, 1e25, ALU.min)
                v.settle()
                tt(rows, rows, over_(cm), ALU.add, s.bc_vec)
                dve.wait_ge(s.ao_mm, 2)
                for g in range(2):
                    tt(cV[:, 4 * g:4 * g + 4, :], ps[:, 6, HD * g:HD * g + HD].unsqueeze(1).to_broadcast([P, 4, HD]),
                       cHead[:, 4 * g:4 * g + 4].unsqueeze(2).to_broadcast([P, 4, HD]), ALU.mult)
                dve.wait_ge(s.bc_act, 9)
                v.do(dve.tensor_reduce(csum, rows, AX.X, ALU.add))
                v.settle()
                ts(csum, csum, 1e-30, ALU.max)
                v.settle()
                v.do(dve.reciprocal(csum, csum))
                v.settle()
                gates = ng.rearrange("p q (h b) -> p q h b", b=3)
                tt(csum.rearrange("p (q h) -> p q h", q=4), csum.rearrange("p (q h) -> p q h", q=4), gates[:, :, :, 0], ALU.mult)
                v.settle()
                tt(rows, rows, over_(csum), ALU.mult, s.bc_vec)

                def weigh(n):
                    u, b = n // 2, n % 2
                    qt, h = u // NH, u % NH
                    nk = (qt + 1) * P
                    dve.wait_ge(s.at_e, n + 1)
                    c = asum[:, n:n + 1]
                    v.do(dve.reciprocal(c, c))
                    v.settle()
                    x = Pb[n % 4][:, 0:nk]
                    v.do(dve.tensor_scalar(x, x, c, ng[:, qt, 3 * h + 1 + b:3 * h + 2 + b], ALU.mult, ALU.mult), s.at_o)

                for n in range(JOBS + 1):
                    if n < JOBS:
                        qt = n // (2 * NH)
                        dve.wait_ge(s.at_s, n + 1)
                        x = ps[:, n % 3, qt * P:(qt + 1) * P]
                        tt(x, x, negm[:, 1, :], ALU.add)
                        v.settle()
                        v.do(dve.tensor_reduce(anm[:, n:n + 1], ps[:, n % 3, 0:(qt + 1) * P], AX.X, ALU.max, negate=True), s.at_m)
                    if n >= 1:
                        weigh(n - 1)

            def s5_input():
                v.settle()
                dve.wait_ge(s.at_v, JOBS)
                v.do(dve.memset(zpad[:, 0:2], 0.0))
                v.settle()

            def s5_step(st):
                z = S5
                if st < NST:
                    c, si = Ec[:, st % 4, :], Es[:, st % 4, :]
                    if st % 2 == 0:
                        dve.wait_ge(s.s5_tab, st // 2 + 1)
                    dve.wait_ge(s.s5_b, st + 1)
                    br, bi = ps[:, 5, :], ps[:, 6, :]
                    v.settle()
                    tt(z.t1, br, c, ALU.mult)
                    tt(z.t2, bi, si, ALU.mult)
                    tt(z.t3, bi, c, ALU.mult)
                    tt(z.t4, br, si, ALU.mult, s.s5_w)
                    v.settle()
                    tt(z.zr, z.t1, z.t2, ALU.add)
                    tt(z.zi, z.t3, z.t4, ALU.subtract)
                    v.settle()
                    r = r5[:, st:st + 1].to_broadcast([P, SEQ])
                    v.do(dve.tensor_tensor_scan(z.wr, r, z.zr, 0.0, ALU.mult, ALU.add))
                    v.do(dve.tensor_tensor_scan(z.wi, r, z.zi, 0.0, ALU.mult, ALU.add))
                    v.settle()
                    tt(z.t1, z.wr, c, ALU.mult)
                    tt(z.t2, z.wi, si, ALU.mult)
                    tt(z.t3, z.wr, si, ALU.mult)
                    tt(z.t4, z.wi, c, ALU.mult)
                    v.settle()
                    if st:
                        dve.wait_ge(s.s5_y, st)
                    tt(z.xr, z.t1, z.t2, ALU.subtract)
                    tt(z.xi, z.t3, z.t4, ALU.add, s.s5_x)
                if st % 4 == 0 and st:
                    t = st // 4 - 1
                    dve.wait_ge(s.s5_y, st)
                    v.do(dve.scalar_tensor_tensor(out=yg[:, t, :], in0=uT[:, t, :], scalar=col("ssmd", t), in1=ps[:, 7, :],
                                                  op0=ALU.mult, op1=ALU.add), s.s5_yd)

            def conv_unit(i):
                dve.wait_ge(s.cv_cc, i + 1)
                bank = lambda x: ps[:, (3 * i + x) % 5, :]
                w = [col("conv2", 3 * i + x) for x in range(3)]
                v.settle()
                tt(zpad[:, 2:SEQ + 2], ccs, bank(1), ALU.mult)
                v.settle()
                v.do(dve.tensor_scalar(cvt, zpad[:, 2:SEQ + 2], w[2], None, ALU.mult))
                for x in (1, 0):
                    v.settle()
                    v.do(dve.scalar_tensor_tensor(out=cvt, in0=zpad[:, x:x + SEQ], scalar=w[x], in1=cvt, op0=ALU.mult, op1=ALU.add))
                v.settle()
                tt(ycv[:, i, :], cvt, bank(2), ALU.mult, s.cv_out)

            def mix_unit(m):
                bank = lambda x: ps[:, (12 + 4 * m + x) % 5, :]
                dve.wait_ge(s.mg_act, 2 * m + 2)
                dve.wait_ge(s.w_used, USED[("nso", m)])
                v.settle()
                tt(mt1, mact[0], bank(2), ALU.mult)
                tt(mt2, mact[1], bank(3), ALU.mult)
                v.settle()
                tt(mixed[:, m, :], mt1, mt2, ALU.add, s.mg_mix)

            def branches():
                for u in range(UNITS):
                    if 2 * u <= NST:
                        s5_step(2 * u)
                    if u < 4:
                        conv_unit(u)
                    else:
                        mix_unit(u - 4)
                    if 2 * u + 1 <= NST:
                        s5_step(2 * u + 1)

            def mix():
                for m in range(KD):
                    b = 3 * (m % 2)
                    dve.wait_ge(s.mg_act, 2 * KD + 2 * m + 2)
                    v.settle()
                    tt(mt1, mact[1], ps[:, b + 1, :], ALU.mult)
                    v.settle()
                    tt(mt1, mt1, mact[0], ALU.mult)
                    v.settle()
                    tt(mixed[:, m, :], mixed[:, m, :], mt1, ALU.add, s.mg_mix)
                for m in range(KD):
                    if m % 2:
                        dve.wait_ge(s.w_used, USED[("wo", m // 2)])
                    else:
                        dve.wait_ge(s.half_done, HALF["mix"] + m // 2 + 1)
                    x = RT[:, m, CTX:N]
                    tt(x, x, ps[:, m % 2, :], ALU.add, s.resid)

            units = [[x for x in FFN if x[0] != "fd" and x[1] == n] if kind else [("fd", part, n)]
                     for part, pairs in enumerate(FF_PARTS) for kind, over_ in ((1, pairs), (0, range(KD))) for n in over_]

            def split_unit(u):
                for item in units[u]:
                    c = FFN.index(item)
                    dve.wait_ge(w_ready[place(item)], 16 * FILLED[item])
                    if c >= 4:
                        dve.wait_ge(s.w_used, USED[FFN[c - 4]])
                    split(slot_view(place(item), shape_of(item)), *halves(item), s.w_split)

            def ffn():
                v.settle()
                for k in range(KD):
                    split(h2[:, k, :], tile_of(h2_hi, k), tile_of(h2_lo, k), s.ff_hid)
                for u, unit in enumerate(units):
                    if u + 1 < len(units):
                        split_unit(u + 1)
                    if unit[0][0] == "fd":
                        _, part, m = unit[0]
                        dve.wait_ge(s.w_used, USED[unit[0]])
                        x = RT[:, m, CTX:N]
                        tt(x, x, ps[:, 4 + m % 2, :], ALU.add, s.resid)
                        continue
                    for x in range(2):
                        i = 2 * unit[0][1] + x
                        dve.wait_ge(s.ff_act, i + 1)
                        if i >= 8 and i % 8 == 0:
                            dve.wait_ge(s.w_used, USED[("fd", i // 8 - 1, KD - 1)])
                        tt(f[:, i % 8, :], fact[i % 2], ps[:, 2 * (i % 2) + 1, :], ALU.mult)
                        v.settle()
                        split(f[:, i % 8, :], tile_of(f_hi, i), tile_of(f_lo, i), s.ff_hid)

            norm2(4, "final", lambda k: RT[:, k, CTX:N])
            norm2(5, "mixn", lambda k: h2[:, k, :])
            dve.wait_ge(s.mask_done, MASKS + 10)
            s5_prepare()
            queries_keys()
            compress()
            attention()
            s5_input()
            branches()
            mix()
            split_unit(0)
            norm2(6, "ffnn", lambda k: h2[:, k, :])
            ffn()


def pack_cols(i):
    def chan(a, lead=()):
        a = np.asarray(a)
        n = a.shape[-1] // P
        a = a.reshape(a.shape[:-1] + (n, P))
        return np.moveaxis(a, -1, 0)

    def row(a):
        a = np.asarray(a).reshape(1, -1)
        return np.broadcast_to(a, (P, a.shape[1]))

    c2 = np.stack([np.asarray(i["c"])[0], np.asarray(i["c_ctx"])])
    cols = dict(
        cvec=np.moveaxis(chan(c2), 1, 2),
        ada_b=chan(i["ada_b"]), norm1=chan(i["norm1_g"]), norm2=chan(i["norm2_g"]),
        final=chan(i["final_norm_g"]), mixn=chan(i["mix_norm_g_2"][0]), ffnn=chan(i["ffn_norm_g_2"][0]),
        gconv=np.moveaxis(chan(i["gdn_conv_w"][0]), 1, 2), galog=row(i["gdn_a_log"]), gdtb=row(i["gdn_dt_bias"]),
        gnorm=chan(i["gdn_norm_g"][0]),
        sconv=np.moveaxis(chan(i["ssd_conv_w"][0]), 1, 2), sconvb=chan(i["ssd_conv_b"][0]),
        salog=row(i["ssd_a_log"]), sdtb=row(i["ssd_dt_bias"]),
        sd=chan(np.repeat(np.asarray(i["ssd_d"][0]), SP_)), snorm=chan(i["ssd_norm_g"][0]),
    )
    g = lambda a: np.asarray(a)[0].reshape(16, P).T
    cols.update(
        lamre=g(i["ssm_lam_re_2"]), lamim=g(i["ssm_lam_im_2"]),
        logdt=np.repeat(np.asarray(i["ssm_log_dt_2"])[0], 64).reshape(16, P).T,
        ssmd=chan(i["ssm_d_2"][0]), conv2=np.moveaxis(chan(i["conv_w_2"][0]), 1, 2),
        qn=np.concatenate([np.asarray(i["q_norm_g_2"])[0]] * 2)[:, None],
        kn=np.concatenate([np.asarray(i["k_norm_g_2"])[0]] * 2, axis=1).T,
        pe=np.asarray(i["cmp_pe_2"])[0].reshape(2, CMPB // 2, P).transpose(2, 0, 1),
    )
    out = np.empty((P, NCOLS), np.float32)
    for k, (a, w) in AT.items():
        out[:, a:a + w] = np.asarray(cols[k]).reshape(P, w)
    return out


WEIGHTS = ["ada_w", "router_w", "moe_w_gate", "moe_w_up", "moe_w_down", "gdn_w_in", "gdn_w_out", "ssd_w_in",
           "ssd_w_out", "w_in_2", "ssm_w_glu_2", "conv_w_out_2", "cmp_w1_2", "cmp_w2_2", "nsa_w_o_2", "w_out_2",
           "ffn_w_gate_up_2", "ffn_w_down_2"]


def lay_out(inputs):
    tokens = np.concatenate([np.asarray(inputs["ctx"])[0], np.asarray(inputs["x"])[0]])
    pair = lambda a: np.asarray(a)[0]
    s5b = np.stack([pair(inputs[n]).transpose(0, 2, 1).reshape(4, P, 64).transpose(1, 0, 2) for n in ("ssm_b_re_2", "ssm_b_im_2")])
    s5c = np.stack([pair(inputs[n]).transpose(0, 2, 1).reshape(NST, P, 16).transpose(1, 0, 2) for n in ("ssm_c_re_2", "ssm_c_im_2")])
    arrays = {"s5b": s5b, "s5c": s5c, "tokens": np.ascontiguousarray(tokens.T.reshape(KD, P, N).transpose(1, 0, 2)), "cols": pack_cols(inputs)}
    for n in WEIGHTS:
        arrays[n] = np.ascontiguousarray(inputs[n])
    return arrays


def kernel(**inputs):
    import concourse.bacc as bacc
    from concourse.bass_utils import run_bass_kernel_spmd

    arrays = {n: np.ascontiguousarray(a) for n, a in lay_out(inputs).items()}
    nc = bacc.Bacc("TRN2", target_bir_lowering=False, num_devices=1)
    aps = {n: nc.dram_tensor(n, a.shape, F32, kind="ExternalInput").ap() for n, a in arrays.items()}
    aps["out"] = nc.dram_tensor("out", (KD, P, SEQ), F32, kind="ExternalOutput").ap()
    build(nc, aps)
    got = run_bass_kernel_spmd(nc, [arrays], core_ids=[0]).results[0]["out"]
    return np.ascontiguousarray(np.asarray(got).reshape(D, SEQ).T)[None]
```
